# Optimizing a Trainium2 kernel written in Bass

```python
import math
import jax, jax.numpy as jnp
from jax import lax
import numpy as np

D_MODEL = 1024
BATCH = 1
SEQ = 256
DEPTH = 2

N_A_LAYERS = DEPTH // 2
N_B_LAYERS = DEPTH - N_A_LAYERS
HG_HEADS = 8
HG_DK = D_MODEL // HG_HEADS
HG_DV = D_MODEL // HG_HEADS
HG_KEY = HG_HEADS * HG_DK
HG_VAL = HG_HEADS * HG_DV
HG_CHUNK = 64
ATT_HEADS = 8
ATT_HD = D_MODEL // ATT_HEADS
ATT_SCALE = ATT_HD ** -0.5
MOBA_BLOCK = 256
MOBA_TOPK = 3
Q_CHUNK = 16
NUM_BUCKETS = 32
MAX_DISTANCE = 1024
N_GROUPS = 4
EXPERTS_PER_GROUP = 8
N_EXPERTS = N_GROUPS * EXPERTS_PER_GROUP
EXPERT_TOPK = 2
EXPERT_FF = D_MODEL // 2
ROW_BLOCK = 128
EPS = 1e-6

kernel_name = 'hgrn2_moba_yoco_hmoe'

def rms_norm(x, w):
    xf = x.astype(jnp.float32)
    y = xf * lax.rsqrt(jnp.mean(xf * xf, axis=-1, keepdims=True) + EPS)
    return (y * w.astype(jnp.float32)).astype(x.dtype)

def _to_chunks(t, n_heads):
    b, l, _ = t.shape
    return t.reshape(b, l // HG_CHUNK, HG_CHUNK, n_heads, -1).transpose(1, 0, 3, 2, 4)

def _gla_chunk_step(state, inp):
    q, k, v, log_f = inp
    b = jnp.cumsum(log_f, axis=2)
    causal = jnp.tril(jnp.ones((HG_CHUNK, HG_CHUNK), dtype=bool))[:, :, None]
    diff = b[:, :, :, None, :] - b[:, :, None, :, :]
    decay = jnp.where(causal, jnp.exp(jnp.where(causal, diff, 0.0)), 0.0)
    scores = jnp.einsum('bhtsd,bhsd->bhts', q[:, :, :, None, :] * decay, k)
    o = (jnp.einsum('bhts,bhsv->bhtv', scores, v)
         + jnp.einsum('bhtd,bhdv->bhtv', q * jnp.exp(b), state))
    b_last = b[:, :, -1, :]
    k_dec = k * jnp.exp(b_last[:, :, None, :] - b)
    state = jnp.exp(b_last)[..., None] * state + jnp.einsum('bhsd,bhsv->bhdv', k_dec, v)
    return state, o

def hgrn2_mixer(h, w_in, lower_bound, o_norm, w_out):
    bsz, seqlen, _ = h.shape
    proj = h @ w_in
    q, f_logit, i, g = jnp.split(proj, [HG_KEY, 2 * HG_KEY, 2 * HG_KEY + HG_VAL], axis=-1)
    lb = lower_bound.astype(jnp.float32)
    f = lb + (1.0 - lb) * jax.nn.sigmoid(f_logit.astype(jnp.float32))
    log_f = jnp.log(f)
    k = 1.0 - f
    qs = _to_chunks(q.astype(jnp.float32) * HG_DK ** -0.5, HG_HEADS)
    ks = _to_chunks(k, HG_HEADS)
    vs = _to_chunks(i.astype(jnp.float32), HG_HEADS)
    gs = _to_chunks(log_f, HG_HEADS)
    state0 = jnp.zeros((bsz, HG_HEADS, HG_DK, HG_DV), jnp.float32)
    _, o = lax.scan(_gla_chunk_step, state0, (qs, ks, vs, gs))
    o = o.transpose(1, 0, 3, 2, 4).reshape(bsz, seqlen, HG_HEADS, HG_DV)
    gate = jax.nn.silu(g.astype(jnp.float32).reshape(bsz, seqlen, HG_HEADS, HG_DV))
    o = rms_norm(o, o_norm) * gate
    return o.reshape(bsz, seqlen, HG_VAL).astype(h.dtype) @ w_out

def shared_kv(mem, kv_norm, w_kv, k_norm):
    bsz, seqlen, _ = mem.shape
    n_blocks = -(-seqlen // MOBA_BLOCK)
    pad = n_blocks * MOBA_BLOCK - seqlen
    kv = rms_norm(mem, kv_norm) @ w_kv
    k, v = jnp.split(kv, 2, axis=-1)
    k = rms_norm(k.reshape(bsz, seqlen, ATT_HEADS, ATT_HD), k_norm)
    v = v.reshape(bsz, seqlen, ATT_HEADS, ATT_HD)

    def to_blocks(t):
        t = jnp.pad(t, ((0, 0), (0, pad), (0, 0), (0, 0)))
        return t.reshape(bsz, n_blocks, MOBA_BLOCK, ATT_HEADS, ATT_HD).transpose(0, 3, 1, 2, 4)

    k_blocks = to_blocks(k)
    v_blocks = to_blocks(v)
    k_mean = jnp.mean(k_blocks.astype(jnp.float32), axis=3).astype(k.dtype)
    return k_blocks, v_blocks, k_mean

def t5_bucket(dist):
    n = jnp.maximum(dist, 0)
    max_exact = NUM_BUCKETS // 2
    log_ratio = (jnp.log(jnp.maximum(n, max_exact).astype(jnp.float32) / max_exact)
                 / math.log(MAX_DISTANCE / max_exact))
    large = max_exact + (log_ratio * (NUM_BUCKETS - max_exact)).astype(jnp.int32)
    large = jnp.minimum(large, NUM_BUCKETS - 1)
    return jnp.where(n < max_exact, n, large)

def moba_mixer(h, w_q, q_norm, w_o, k_blocks, v_blocks, k_mean, rel_bias):
    bsz, seqlen, _ = h.shape
    n_blocks = k_blocks.shape[2]
    topk = min(MOBA_TOPK, n_blocks)
    q = rms_norm((h @ w_q).reshape(bsz, seqlen, ATT_HEADS, ATT_HD), q_norm)
    q = q.transpose(0, 2, 1, 3)
    bias_tab = rel_bias.astype(jnp.float32)
    b_ix = jnp.arange(bsz)[:, None, None, None]
    h_ix = jnp.arange(ATT_HEADS)[None, :, None, None]
    key_off = jnp.arange(MOBA_BLOCK)

    def attend(c):
        start = c * Q_CHUNK
        blk = start // MOBA_BLOCK
        q_c = lax.dynamic_slice_in_dim(q, start, Q_CHUNK, axis=2)
        q_pos = start + jnp.arange(Q_CHUNK)
        gate = jnp.einsum('bhqd,bhnd->bhqn', q_c, k_mean, preferred_element_type=jnp.float32)
        gate = jnp.where(jnp.arange(n_blocks) < blk, gate, -jnp.inf)
        _, sel = lax.top_k(gate, topk)
        valid = jnp.arange(topk) < blk
        k_sel = k_blocks[b_ix, h_ix, sel]
        v_sel = v_blocks[b_ix, h_ix, sel]
        s_sel = jnp.einsum('bhqd,bhqnkd->bhqnk', q_c, k_sel,
                           preferred_element_type=jnp.float32) * ATT_SCALE
        dist_sel = q_pos[None, None, :, None, None] - (sel[..., None] * MOBA_BLOCK + key_off)
        s_sel = s_sel + bias_tab[t5_bucket(dist_sel), h_ix[..., None]]
        s_sel = jnp.where(valid[:, None], s_sel, -jnp.inf)
        k_own = lax.dynamic_index_in_dim(k_blocks, blk, axis=2, keepdims=False)
        v_own = lax.dynamic_index_in_dim(v_blocks, blk, axis=2, keepdims=False)
        s_own = jnp.einsum('bhqd,bhkd->bhqk', q_c, k_own,
                           preferred_element_type=jnp.float32) * ATT_SCALE
        dist_own = q_pos[:, None] - (blk * MOBA_BLOCK + key_off)[None, :]
        s_own = s_own + bias_tab[t5_bucket(dist_own)].transpose(2, 0, 1)
        s_own = jnp.where(dist_own >= 0, s_own, -jnp.inf)
        logits = jnp.concatenate([s_sel.reshape(bsz, ATT_HEADS, Q_CHUNK, topk * MOBA_BLOCK), s_own], axis=-1)
        p = jax.nn.softmax(logits, axis=-1).astype(v_blocks.dtype)
        p_sel = p[..., :topk * MOBA_BLOCK].reshape(bsz, ATT_HEADS, Q_CHUNK, topk, MOBA_BLOCK)
        p_own = p[..., topk * MOBA_BLOCK:]
        return (jnp.einsum('bhqnk,bhqnkd->bhqd', p_sel, v_sel)
                + jnp.einsum('bhqk,bhkd->bhqd', p_own, v_own))

    o = lax.map(attend, jnp.arange(seqlen // Q_CHUNK))
    o = o.transpose(1, 0, 3, 2, 4).reshape(bsz, seqlen, ATT_HEADS * ATT_HD)
    return o @ w_o

def hier_moe(h, w_group, b_group, w_expert, b_expert, w_in, w_out):
    bsz, seqlen, d = h.shape
    ht = h.reshape(-1, d)
    n_tok = ht.shape[0]
    g_logits = (ht @ w_group).astype(jnp.float32) + b_group.astype(jnp.float32)
    g_prob = jax.nn.softmax(g_logits, axis=-1)
    g_idx = jnp.argmax(g_logits, axis=-1)
    g_w = jnp.take_along_axis(g_prob, g_idx[:, None], axis=1)
    e_logits = ((ht @ w_expert).astype(jnp.float32) + b_expert.astype(jnp.float32)).reshape(
        n_tok, N_GROUPS, EXPERTS_PER_GROUP)
    e_logits = jnp.take_along_axis(e_logits, g_idx[:, None, None], axis=1)[:, 0]
    top_p, top_i = lax.top_k(jax.nn.softmax(e_logits, axis=-1), EXPERT_TOPK)
    weights = g_w * (top_p / jnp.sum(top_p, axis=-1, keepdims=True))
    expert_id = (g_idx[:, None] * EXPERTS_PER_GROUP + top_i).astype(jnp.int32)
    flat_id = expert_id.reshape(-1)
    flat_w = weights.reshape(-1)
    n_assign = flat_id.shape[0]
    order = jnp.argsort(flat_id)
    sorted_id = flat_id[order]
    token_of = order // EXPERT_TOPK
    counts = jnp.bincount(flat_id, length=N_EXPERTS).astype(jnp.int32)
    padded = (counts + ROW_BLOCK - 1) // ROW_BLOCK * ROW_BLOCK
    seg_start = jnp.cumsum(counts) - counts
    pad_end = jnp.cumsum(padded)
    pad_start = pad_end - padded
    dest = pad_start[sorted_id] + jnp.arange(n_assign, dtype=jnp.int32) - seg_start[sorted_id]
    n_rb = -(-n_assign // ROW_BLOCK) + N_EXPERTS
    cap = n_rb * ROW_BLOCK
    row_token = jnp.zeros((cap,), jnp.int32).at[dest].set(token_of.astype(jnp.int32))
    x_buf = ht[row_token].reshape(n_rb, ROW_BLOCK, d)
    block_expert = jnp.minimum(
        jnp.searchsorted(pad_end, jnp.arange(n_rb, dtype=jnp.int32) * ROW_BLOCK, side='right'),
        N_EXPERTS - 1)

    def expert_block(args):
        xb, e = args
        hu = xb @ w_in[e]
        return (jax.nn.silu(hu[:, :EXPERT_FF]) * hu[:, EXPERT_FF:]) @ w_out[e]

    y_buf = lax.map(expert_block, (x_buf, block_expert)).reshape(cap, d)
    y = y_buf[dest] * flat_w[order][:, None].astype(y_buf.dtype)
    out = jnp.zeros_like(ht).at[token_of].add(y)
    return out.reshape(bsz, seqlen, d)

def setup_inputs(seed: int = 0) -> dict:
    key = jax.random.key(seed)
    ks = jax.random.split(key, 24)

    def nrm(k, shape, scale):
        return jax.random.normal(k, shape, jnp.float32) * scale

    res = (2.0 * DEPTH) ** -0.5
    return {
        'x': nrm(ks[0], (BATCH, SEQ, D_MODEL), 1.0),
        'mix_norm': 1.0 + nrm(ks[1], (DEPTH, D_MODEL), 0.05),
        'ffn_norm': 1.0 + nrm(ks[2], (DEPTH, D_MODEL), 0.05),
        'hg_w_in': nrm(ks[3], (N_A_LAYERS, D_MODEL, 2 * HG_KEY + 2 * HG_VAL), D_MODEL ** -0.5),
        'hg_lb': nrm(ks[4], (N_A_LAYERS + 1, HG_KEY), 0.5),
        'hg_o_norm': 1.0 + nrm(ks[5], (N_A_LAYERS, HG_DV), 0.05),
        'hg_w_out': nrm(ks[6], (N_A_LAYERS, HG_VAL, D_MODEL), HG_VAL ** -0.5 * res),
        'kv_norm': 1.0 + nrm(ks[7], (D_MODEL,), 0.05),
        'w_kv': nrm(ks[8], (D_MODEL, 2 * ATT_HEADS * ATT_HD), D_MODEL ** -0.5),
        'k_norm': 1.0 + nrm(ks[9], (ATT_HD,), 0.05),
        'att_w_q': nrm(ks[10], (N_B_LAYERS, D_MODEL, ATT_HEADS * ATT_HD), D_MODEL ** -0.5),
        'q_norm': 1.0 + nrm(ks[11], (N_B_LAYERS, ATT_HD), 0.05),
        'att_w_o': nrm(ks[12], (N_B_LAYERS, ATT_HEADS * ATT_HD, D_MODEL), (ATT_HEADS * ATT_HD) ** -0.5 * res),
        'rel_bias': nrm(ks[13], (NUM_BUCKETS, ATT_HEADS), 0.5),
        'moe_w_group': nrm(ks[14], (DEPTH, D_MODEL, N_GROUPS), D_MODEL ** -0.5),
        'moe_b_group': nrm(ks[15], (DEPTH, N_GROUPS), 0.01),
        'moe_w_expert': nrm(ks[16], (DEPTH, D_MODEL, N_EXPERTS), D_MODEL ** -0.5),
        'moe_b_expert': nrm(ks[17], (DEPTH, N_EXPERTS), 0.01),
        'moe_w_in': nrm(ks[18], (DEPTH, N_EXPERTS, D_MODEL, 2 * EXPERT_FF), D_MODEL ** -0.5),
        'moe_w_out': nrm(ks[19], (DEPTH, N_EXPERTS, EXPERT_FF, D_MODEL), EXPERT_FF ** -0.5 * res),
    }

def reference(x, mix_norm, ffn_norm, hg_w_in, hg_lb, hg_o_norm, hg_w_out, kv_norm, w_kv, k_norm,
              att_w_q, q_norm, att_w_o, rel_bias, moe_w_group, moe_b_group, moe_w_expert,
              moe_b_expert, moe_w_in, moe_w_out):
    lower_bounds = jnp.cumsum(jax.nn.softmax(hg_lb.astype(jnp.float32), axis=0), axis=0)
    k_blocks = v_blocks = k_mean = None
    for layer in range(DEPTH):
        hmix = rms_norm(x, mix_norm[layer])
        if layer < N_A_LAYERS:
            x = x + hgrn2_mixer(hmix, hg_w_in[layer], lower_bounds[layer], hg_o_norm[layer], hg_w_out[layer])
        else:
            j = layer - N_A_LAYERS
            x = x + moba_mixer(hmix, att_w_q[j], q_norm[j], att_w_o[j], k_blocks, v_blocks, k_mean, rel_bias)
        x = x + hier_moe(rms_norm(x, ffn_norm[layer]), moe_w_group[layer], moe_b_group[layer],
                         moe_w_expert[layer], moe_b_expert[layer], moe_w_in[layer], moe_w_out[layer])
        if layer == N_A_LAYERS - 1:
            k_blocks, v_blocks, k_mean = shared_kv(x, kv_norm, w_kv, k_norm)
    return x


_drawn_inputs = setup_inputs


def setup_inputs(seed=0):
    import zlib

    import numpy as np

    out = dict(_drawn_inputs(seed))
    spreads = {}
    factors = {'kv_norm': 4.582,
     'k_norm': 8.0,
     'q_norm': 5.829,
     'moe_b_group': 6.703,
     'moe_b_expert': 5.332}
    for name, (base, spread) in spreads.items():
        noise = np.random.default_rng([zlib.crc32(name.encode()), seed]).standard_normal(out[name].shape)
        drawn = base * np.exp(spread * noise) if base else spread * noise
        out[name] = __import__('jax').numpy.asarray(drawn.astype(out[name].dtype))
    for name, factor in factors.items():
        out[name] = (out[name] * factor).astype(out[name].dtype)
    return out
```

```python
import concourse.bass as bass
from concourse import mybir
from contextlib import ExitStack

FP32 = mybir.dt.float32
I32 = mybir.dt.int32
U8 = mybir.dt.uint8
ALU = mybir.AluOpType
ACT = mybir.ActivationFunctionType
AX = mybir.AxisListType

P = 128
T = 256
TT = T // P
D = 1024
KD = D // P
H = 8
LEVELS = 7
NG, EG = 4, 8
E = NG * EG
FF = 512
KF = FF // P
EPS = 1e-6
QSCALE = float(P) ** -0.5

BLK = 64
CAP = 64
PAIRS = E // 2
RING = 8
UN = 4
ITERS = PAIRS // UN
TURNS = 6 * UN // RING
MIX0, MOE0 = 0, 10
MIX1 = MOE0 + 6 * PAIRS
MOE1 = MIX1 + 8
MOE = [MOE0, MOE1]
NR = 3 * P

POW_MIX0, POW_O, POW_FFN0, POW_MIX1, POW_K, POW_Q, POW_FFN1 = range(1, 8)


def build(nc, x, mix_norm, ffn_norm, hg_w_in, hg_lb, hg_o_norm, hg_w_out, kv_norm, w_kv, k_norm,
          att_w_q, q_norm, att_w_o, rel_bias, moe_w_group, moe_b_group, moe_w_expert, moe_b_expert,
          moe_w_in, moe_w_out, c_ident, c_before, c_masks, c_slot, c_prio, c_bucket, c_future, out):
    with ExitStack() as ctx:
        def sb(name, shape, dt=FP32):
            return ctx.enter_context(nc.sbuf_tensor(name, shape, dt))

        def sem(name):
            return ctx.enter_context(nc.semaphore(name))

        ctx.enter_context(nc.allow_non_contiguous_dma(reason="small vectors spread over partitions"))
        ps = ctx.enter_context(nc.psum_tensor("ps", [P, 8, 512], FP32))
        bias_dram = nc.dram_tensor("bias_scratch", (H, P * (NR + 1)), FP32, kind="Internal").ap()

        ring = sb("ring", [P, RING, 4096])
        xs = sb("xs", [P, TT, D])
        ident = sb("ident", [P, P])
        before = sb("before", [P, P])
        ones = sb("ones", [P, P])
        masks = sb("masks", [P, LEVELS + 1, P], U8)
        slot = sb("slot", [P, BLK])
        prio = sb("prio", [P, EG])
        wcol = sb("wcol", [P, 3, KD])
        lbl = sb("lbl", [P, 2, H])
        lbw = sb("lbw", [P, 6, H])
        onorm = sb("onorm", [P, P])
        kqcol = sb("kqcol", [P, 3])
        wr = sb("wr", [P, 2, KD, NG + E])
        br = sb("br", [P, 2, NG + E])
        ms = sb("ms", [P, 16])
        rstd = sb("rstd", [P, 16])
        mhalf = sb("mhalf", [P, 16])
        nmax = sb("nmax", [P, H, 2])
        esum = sb("esum", [P, H, 2])
        einv = sb("einv", [P, H, 2])
        nblk = sb("nblk", [P, 2], I32)
        nblf = sb("nblf", [P, 4])
        mark = sb("mark", [P, 8])

        work = sb("work", [P, 8, 2048])

        def region(i, k=1):
            return work[:, i:i + k, :].rearrange("p r n -> p (r n)")

        hT = region(0).rearrange("p (k t) -> p k t", t=T)
        f_all = region(1)
        ks_all = region(2)
        qp_all = region(3)
        sdiag = region(4).rearrange("p (b t) -> p b t", t=P)
        scross = region(5)[:, 0:1024].rearrange("p (h t) -> p h t", t=P)
        t_odd = region(5)[:, 1024:2048]
        v_all = region(6).rearrange("p (a n) -> p a n", n=D)
        gate = region(7).rearrange("p (a n) -> p a n", n=D)
        xn = region(5).rearrange("p (a n) -> p a n", n=D)
        osq = region(0).rearrange("p (a n) -> p a n", n=D)
        og = region(2).rearrange("p (a n) -> p a n", n=D)
        oT0 = region(3).rearrange("p (k t) -> p k t", t=T)
        hkvT = hT
        hqT = region(1).rearrange("p (k t) -> p k t", t=T)
        kn = region(2).rearrange("p (a n) -> p a n", n=D)
        qn = region(3).rearrange("p (a n) -> p a n", n=D)
        kT = region(4).rearrange("p (h t) -> p h t", t=T)
        qT = region(5).rearrange("p (h t) -> p h t", t=T)
        bias = region(7).rearrange("p (h s) -> p h s", s=T)
        prob = region(0, 2)[:, 0:H * NR].rearrange("p (h s) -> p h s", s=NR)
        probT = region(2, 2)[:, 0:H * NR].rearrange("p (h s) -> p h s", s=NR)
        oT1 = region(4).rearrange("p (h t) -> p h t", t=T)
        hn = region(0).rearrange("p (a n) -> p a n", n=D)
        hrT = region(1).rearrange("p (k t) -> p k t", t=T)
        yT = region(1).rearrange("p (b k s) -> p b k s", b=2, s=P)
        xgT = region(2).rearrange("p (b k s) -> p b k s", b=2, s=P)
        y = region(3)[:, 0:1024]
        hid = region(3)[:, 1024:1536].rearrange("p (b m s) -> p b m s", b=2, s=BLK)
        en = region(3)[:, 1536:1792]
        th = region(3)[:, 1792:2048]
        en_b = th
        pick = region(4)[:, 0:256].rearrange("p (a e s) -> p a e s", a=TT, s=BLK)
        pickw = region(4)[:, 256:512].rearrange("p (a e s) -> p a e s", a=TT, s=BLK)
        spread = region(4)[:, 512:768]
        wrow = region(4)[:, 1024:2048]
        rt = region(5)
        lg = rt[:, 0:72].rearrange("p (a n) -> p a n", n=NG + E)
        gmx, gsm, m1, m2, dd, e2, ss, w1, w2 = (rt[:, 72 + 2 * i:74 + 2 * i] for i in range(9))
        goh, gpr, gex = (rt[:, 100 + 8 * i:108 + 8 * i].rearrange("p (a g) -> p a g", g=NG) for i in range(3))
        es, oh1, oh2, pr8, wt8, a8, es2 = (rt[:, 128 + 16 * i:144 + 16 * i].rearrange("p (a g) -> p a g", g=EG)
                                           for i in range(7))
        tmp32 = rt[:, 256:320].rearrange("p (a g e) -> p a g e", a=TT, g=NG)
        asg = rt[:, 320:384].rearrange("p (a e) -> p a e", a=TT)
        wgt = rt[:, 384:448].rearrange("p (q a e) -> p q a e", a=TT, e=2)
        pos = rt[:, 448:512].rearrange("p (q a e) -> p q a e", a=TT, e=2)
        tpos = rt[:, 512:576].rearrange("p (a e) -> p a e", a=TT)
        cmx = rt[:, 576:577]
        junk = region(6)[:, 0:1024]
        rbw = region(6)[0:32, 1024:1032]
        bucket = region(6)[0:32, 1040:1040 + NR]
        future = region(6)[0:H, 1430:1430 + NR]
        brow = region(7)[0:H, 0:NR]
        masks_in = region(7)[:, 1024:2048].rearrange("p (l t) -> p l t", t=P)

        loaded = [sem(f"slot_loaded{i}") for i in range(RING)]
        x_in, c_in, w_in = sem("x_in"), sem("const_in"), sem("small_in")
        rowload, biasload, biasout = sem("ffn_row_in"), sem("bias_in"), sem("bias_out")
        setup = sem("memsets_done")
        dv = sem("dve_step")
        ms_ready, rstd_ready = sem("ms_ready"), sem("rstd_ready")
        xn_ready, nt_done = sem("normed_ready"), sem("normed_transposed")
        hT_dve, hT_act = sem("hT_by_dve"), sem("hT_by_act")
        lb_in, lb_exp = sem("lb_logits"), sem("lb_exp")
        f_done, f_exp, k_ready, q_done, q_ready = (sem(n) for n in ("f_done", "f_exp", "k_ready", "q_done", "q_ready"))
        lev_done, upd_ready, pred_done = sem("level_done"), sem("level_operands"), sem("level_scores")
        vg_done, v_ready, g_exp, gate_ready = (sem(n) for n in ("vg_done", "v_ready", "g_exp", "gate_ready"))
        cross_ready = sem("cross_ready")
        o_done, osq_done, og_ready = sem("o_done"), sem("osq_done"), sem("og_ready")
        ot_done, oT_ready, pr_done, x_ready = (sem(n) for n in ("ot_done", "oT_ready", "proj_done", "x_ready"))
        rb_done, rb_ready = sem("bias_row_done"), sem("bias_row_ready")
        rt_done, gl_ready, gl_exp, el_ready, el_exp = (sem(n) for n in ("router_done", "group_logits", "group_exp",
                                                                        "top2_gap", "top2_exp"))
        asg_ready, pos_done, nblk_ready = sem("assigned"), sem("positions_done"), sem("blocks_ready")
        pick_ready, pickw_ready, gat_done, xg_ready = (sem(n) for n in ("pick_ready", "pickw_ready", "gather_done",
                                                                        "gathered_ready"))
        hu_done, exp_done, silu_step, hid_ready = (sem(n) for n in ("up_done", "silu_exp", "silu_step", "hidden_ready"))
        y_done, yT_ready, st_done, s_ready = (sem(n) for n in ("down_done", "yT_ready", "spread_transposed",
                                                               "spread_ready"))
        t_done, y_ready, c_done = sem("y_transposed"), sem("y_ready"), sem("combine_done")
        kq_done, sq_done, kqn_ready, tkq_done, kqT_ready = (sem(n) for n in ("kq_done", "kq_squares", "kq_normed",
                                                                             "kq_transposed", "kqT_ready"))
        av_done, av_ready = sem("att_v_done"), sem("att_v_ready")
        sc_done, mx_ready, ex_done, ei_ready, pn_ready = (sem(n) for n in ("scores_done", "max_ready", "probs_exp",
                                                                           "inv_sum", "probs_ready"))
        pt_done, pT_ready, pv_done = sem("probs_transposed"), sem("probT_ready"), sem("pv_done")
        out_done = sem("out_done")
        ov = [{n: sem(f"over{l}_{n}") for n in ("w", "shift", "picked", "pick", "gat", "xg", "hu", "exp", "den", "rec",
                                                "sil", "hid", "y", "yt", "tr", "ye", "c", "x", "end")}
              for l in range(2)]

        def chunk(c):
            return ring[:, c % RING, :]

        def up_view(c):
            return chunk(c).rearrange("p (k n) -> p k n", n=512)

        def down_view(c):
            return chunk(c).rearrange("p (k n) -> p k n", n=D)

        def over_pairs(eng, body):
            body(0)
            with eng.Fori(1, ITERS - 1) as it:
                body(it)
            body(ITERS - 1)

        def is_int(v, n):
            return type(v) is int and v == n

        block = ctx.enter_context(nc.Block())

        @block.sync
        def _(sp):
            sp.dma_start(xs[:], x[0].rearrange("(a p) n -> p a n", p=P)).then_inc(x_in, 16)

            def expert_read(layer, r, it=0):
                e = layer * E + r // 3
                if r % 3 < 2:
                    return hu_done, it * (4 * UN) + (2 * e + 1 + r % 3)
                return y_done, it * (2 * UN) + (e + 1)

            def read(c):
                if c >= MOE1:
                    return expert_read(1, c - MOE1)
                if c >= MIX1:
                    return ((kq_done, 2), (kq_done, 4), (kq_done, 6), (kq_done, 8), (av_done, 2), (av_done, 4),
                            (pr_done, 6), (pr_done, 8))[c - MIX1]
                if c >= MOE0:
                    return expert_read(0, c - MOE0)
                return ((f_done, 2), (f_done, 4), (q_done, 2), (q_done, 4), (vg_done, 2), (vg_done, 4), (vg_done, 6),
                        (vg_done, 8), (pr_done, 2), (pr_done, 4))[c]

            def load(c, dst, src):
                if c >= RING:
                    sp.wait_ge(*read(c - RING))
                sp.dma_start(dst, src).then_inc(loaded[c % RING], 16)

            def load_expert(layer, r, dst, src, it):
                c = MOE[layer] + r
                if type(it) is int and it == 0 and r < RING:
                    sp.wait_ge(*read(c - RING))
                else:
                    sp.wait_ge(*expert_read(layer, r - RING, it))
                sp.dma_start(dst, src).then_inc(loaded[c % RING], 16)

            def cols(w, j):
                return w[:, j * 512:(j + 1) * 512].rearrange("(k p) n -> p k n", p=P)

            for c, j in enumerate((2, 3, 0, 1, 4, 5, 6, 7)):
                load(MIX0 + c, up_view(c), cols(hg_w_in[0], j))
            for j in range(2):
                load(MIX0 + 8 + j, up_view(MIX0 + 8 + j), cols(hg_w_out[0], j))

            def experts(layer):
                def body(it):
                    for u in range(UN):
                        for j in range(6):
                            e = it * (2 * UN) + (2 * u + j // 3)
                            r = 6 * u + j
                            c = MOE[layer] + r
                            if j % 3 < 2:
                                load_expert(layer, r, up_view(c), cols(moe_w_in[layer, e], j % 3), it)
                            else:
                                load_expert(layer, r, down_view(c),
                                            moe_w_out[layer, e].rearrange("(k p) n -> p k n", p=P), it)
                over_pairs(sp, body)
                over(layer)

            def over(layer):
                s = ov[layer]
                sp.wait_ge(nblk_ready, layer + 1)
                n = sp.value_load(nblk[0:1, layer:layer + 1], min_val=1, max_val=4)
                with sp.If(n > 1):
                    sp.wait_ge(y_done, (layer + 1) * E)
                    with sp.Fori(1, n) as b:
                        with sp.Fori(0, PAIRS) as q:
                            sp.wait_ge(s["x"], b * PAIRS + q - (PAIRS - 1))
                            for j in range(6):
                                e = q * 2 + j // 3
                                if j % 3 < 2:
                                    src, dst = cols(moe_w_in[layer, e], j % 3), up_view(j)
                                else:
                                    src, dst = moe_w_out[layer, e].rearrange("(k p) n -> p k n", p=P), down_view(j)
                                sp.dma_start(dst, src).then_inc(s["w"], 16)
                    sp.wait_ge(s["end"], 1)

            experts(0)
            c = MIX1
            for w, j in ((w_kv, 0), (w_kv, 1), (att_w_q[0], 0), (att_w_q[0], 1), (w_kv, 2), (w_kv, 3),
                         (att_w_o[0], 0), (att_w_o[0], 1)):
                load(c, up_view(c), cols(w, j))
                c += 1
            experts(1)
            for a in range(TT):
                sp.wait_ge(x_ready, a + 1)
                sp.dma_start(out[0, a * P:(a + 1) * P, :], xs[:, a, :]).then_inc(out_done, 16)
            sp.wait_ge(out_done, 16 * TT)
            sp.wait_ge(biasout, 16)

        @block.gpsimd
        def _(pool):
            pool.memset(ones[:], 1.0).then_inc(setup, 1)
            pool.memset(mhalf[:], -0.5).then_inc(setup, 1)
            pool.wait_ge(setup, 2)

            def root(i, n):
                pool.wait_ge(ms_ready, i)
                pool.tensor_tensor(rstd[:, 0:n], ms[:, 0:n], mhalf[:, 0:n], ALU.pow).then_inc(rstd_ready, 1)

            pool.memset(region(4), 0.0).then_inc(setup, 1)
            root(POW_MIX0, TT)
            pool.wait_ge(rb_ready, 1)
            pool.dma_start(bias_dram.rearrange("h (p n) -> h p n", p=P)[:, :, 0:NR],
                           brow.unsqueeze(1).to_broadcast([H, P, NR])).then_inc(biasout, 16)
            root(POW_O, TT * H)
            pool.wait_ge(o_done, 2)
            pool.dma_start(wrow, ffn_norm[0:1, :].to_broadcast([P, D])).then_inc(rowload, 16)
            root(POW_FFN0, TT)
            pool.wait_ge(biasout, 16)
            pool.wait_ge(og_ready, 2)
            pool.dma_start(bias, bass.AP(bias_dram.tensor, P - 1, [[NR, P], [P * (NR + 1), H], [1, T]])).then_inc(biasload, 16)
            root(POW_MIX1, TT)
            root(POW_K, TT * H)
            root(POW_Q, TT * H)
            for h in range(H):
                pool.wait_ge(ei_ready, h + 1)
                pool.tensor_scalar(prob[:, h, 0:P], prob[:, h, 0:P], einv[:, h, 0:1], None, ALU.mult)
                pool.tensor_scalar(prob[:, h, P:NR], prob[:, h, P:NR], einv[:, h, 1:2], None,
                                   ALU.mult).then_inc(pn_ready, 1)
            pool.wait_ge(pr_done, 8)
            pool.dma_start(wrow, ffn_norm[1:2, :].to_broadcast([P, D])).then_inc(rowload, 16)
            root(POW_FFN1, TT)

        @block.scalar
        def _(act):
            act.dma_start(ident[:], c_ident).then_inc(c_in, 16)
            act.dma_start(wcol[:, 0, :], mix_norm[0].rearrange("(k p) -> p k", p=P)).then_inc(w_in, 16)
            act.dma_start(lbl[:], hg_lb.rearrange("a (k p) -> p a k", p=P)).then_inc(w_in, 16)
            act.dma_start(masks_in, c_masks).then_inc(w_in, 16)
            act.dma_start(onorm[:], hg_o_norm[0:1, :].to_broadcast([P, P])).then_inc(w_in, 16)
            act.dma_start(wcol[:, 1, :], kv_norm.rearrange("(k p) -> p k", p=P)).then_inc(w_in, 16)
            act.dma_start(wcol[:, 2, :], mix_norm[1].rearrange("(k p) -> p k", p=P)).then_inc(w_in, 16)
            act.dma_start(kqcol[:, 0:1], k_norm.rearrange("(p a) -> p a", a=1)).then_inc(w_in, 16)
            act.dma_start(kqcol[:, 1:2], q_norm[0].rearrange("(p a) -> p a", a=1)).then_inc(w_in, 16)
            act.dma_start(before[:], c_before).then_inc(w_in, 16)
            act.dma_start(slot[:], c_slot).then_inc(w_in, 16)
            act.dma_start(prio[:], c_prio).then_inc(w_in, 16)
            for l in range(2):
                act.dma_start(wr[:, l, :, 0:NG], moe_w_group[l].rearrange("(k p) n -> p k n", p=P)).then_inc(w_in, 16)
                act.dma_start(wr[:, l, :, NG:], moe_w_expert[l].rearrange("(k p) n -> p k n", p=P)).then_inc(w_in, 16)
                act.dma_start(br[:, l, 0:NG], moe_b_group[l:l + 1, :].to_broadcast([P, NG])).then_inc(w_in, 16)
                act.dma_start(br[:, l, NG:], moe_b_expert[l:l + 1, :].to_broadcast([P, E])).then_inc(w_in, 16)
            act.dma_start(rbw, rel_bias).then_inc(w_in, 16)
            act.dma_start(bucket, c_bucket).then_inc(w_in, 16)
            act.dma_start(future, c_future).then_inc(w_in, 16)

            def transposed(stage, dsts):
                for b in (2, 3):
                    act.wait_ge(nt_done, 4 * stage + b + 1)
                    for dst, w in dsts:
                        src = ps[:, 4 + b, :].rearrange("p (k t) -> p k t", t=T)
                        if w is None:
                            act.copy(dst[:, 2 * b:2 * b + 2, :], src).then_inc(hT_act, 1)
                        else:
                            for j in range(2):
                                i = act.activation(dst[:, 2 * b + j, :], src[:, j, :], ACT.Copy,
                                                   scale=wcol[:, w, 2 * b + j:2 * b + j + 1])
                            i.then_inc(hT_act, 1)

            act.wait_ge(lb_in, 1)
            act.activation(lbw[:, 2:4, :], lbw[:, 0:2, :], ACT.Exp).then_inc(lb_exp, 1)
            act.wait_ge(w_in, SMALL)
            transposed(0, [(hT, 0)])
            for hp in range(4):
                act.wait_ge(f_done, hp + 1)
                act.activation(f_all[:, hp * 512:(hp + 1) * 512], ps[:, hp, :], ACT.Exp, scale=-1.0).then_inc(f_exp, 1)
            for hp in range(4):
                act.wait_ge(q_done, hp + 1)
                act.activation(qp_all[:, hp * 512:(hp + 1) * 512], ps[:, 4 + hp, :], ACT.Copy,
                               scale=QSCALE).then_inc(q_ready, 1)
            for i in range(4):
                act.wait_ge(vg_done, i + 1)
                act.copy(v_all[:, i % 2, (i // 2) * 512:(i // 2 + 1) * 512], ps[:, 4 + i, :]).then_inc(v_ready, 1)
            act.wait_ge(biasout, 16)
            for i in range(4):
                act.wait_ge(vg_done, 5 + i)
                act.activation(gate[:, i % 2, (i // 2) * 512:(i // 2 + 1) * 512], ps[:, 4 + i, :], ACT.Exp,
                               scale=-1.0).then_inc(g_exp, 1)
            act.wait_ge(lev_done, 9)
            act.wait_ge(upd_ready, 8)
            act.copy(scross, ps[:, 0:2, :].rearrange("p b (h t) -> p (b h) t", t=P)).then_inc(cross_ready, 1)
            for a in range(TT):
                act.wait_ge(o_done, a + 1)
                act.activation(osq[:, a, :], ps[:, 4 + 2 * a:6 + 2 * a, :].rearrange("p b n -> p (b n)"),
                               ACT.Square).then_inc(osq_done, 1)
            for b in (2, 3):
                act.wait_ge(ot_done, b + 1)
                act.copy(oT0[:, 2 * b:2 * b + 2, :], ps[:, b, :].rearrange("p (k t) -> p k t", t=T))\
                   .then_inc(oT_ready, 1)

            def over(layer):
                s = ov[layer]
                act.wait_ge(nblk_ready, layer + 1)
                n = act.value_load(nblk[0:1, layer:layer + 1], min_val=1, max_val=4)
                with act.If(n > 1):
                    with act.Fori(1, n) as b:
                        with act.Fori(0, PAIRS) as q:
                            v = b * PAIRS + q - (PAIRS - 1)
                            act.wait_ge(s["gat"], v)
                            act.copy(xgT[:, 0, 0:4, :], ps[:, 4, :].rearrange("p (k s) -> p k s", s=P))
                            act.copy(xgT[:, 0, 4:8, :], ps[:, 5, :].rearrange("p (k s) -> p k s", s=P))
                            act.copy(spread, ps[:, 0, 0:T]).then_inc(s["xg"], 1)
                            act.wait_ge(s["hu"], v)
                            act.activation(en, ps[:, 6, 0:256], ACT.Exp, scale=-1.0)
                            act.activation(en_b, ps[:, 1, 0:256], ACT.Exp,
                                           scale=-1.0).then_inc(s["exp"], 1)
                            act.wait_ge(s["y"], v)
                            act.copy(yT[:, 0, :, 0:BLK], ps[:, 7, :].rearrange("p (k s) -> p k s", s=BLK))
                            act.copy(yT[:, 0, :, BLK:P], ps[:, 2, :].rearrange("p (k s) -> p k s", s=BLK))\
                               .then_inc(s["yt"], 1)
                            act.wait_ge(s["tr"], v)
                            act.copy(y, ps[:, 0:2, :].rearrange("p b n -> p (b n)")).then_inc(s["ye"], 1)
                    act.wait_ge(s["end"], 1)

            def moe(layer):
                transposed(1 + 2 * layer, [(hrT, None)])
                act.wait_ge(gl_ready, layer + 1)
                act.activation(gex, gpr, ACT.Exp).then_inc(gl_exp, 1)
                act.wait_ge(el_ready, layer + 1)
                act.activation(e2, dd, ACT.Exp).then_inc(el_exp, 1)
                P0 = layer * PAIRS

                def gathered(it, u, half):
                    q = P0 + u
                    act.wait_ge(gat_done, it * (2 * UN) + (2 * q + half + 1))
                    if not (type(it) is int and it * UN + q < 2):
                        act.wait_ge(hu_done, it * (4 * UN) + 4 * (q - 1))
                    act.copy(xgT[:, u % 2, 4 * half:4 * half + 4, :],
                             ps[:, 4, :].rearrange("p (k s) -> p k s", s=P)).then_inc(xg_ready, 1)

                def body(it):
                    for u in range(UN):
                        q = P0 + u
                        last = is_int(it, ITERS - 1) and u == UN - 1
                        for x2 in range(2):
                            e = 2 * q + x2
                            act.wait_ge(hu_done, it * (4 * UN) + (2 * e + 2))
                            if not (type(it) is int and it * 2 * UN + e < 1):
                                act.wait_ge(hid_ready, it * (2 * UN) + e)
                            act.activation(en, ps[:, 6, 0:256], ACT.Exp, scale=-1.0).then_inc(exp_done, 1)
                            if not last:
                                gathered(it, u + 1, x2)
                            act.wait_ge(y_done, it * (2 * UN) + (e + 1))
                            if not (type(it) is int and it * UN + q < 2):
                                act.wait_ge(t_done, it * (2 * UN) + (2 * q - 2))
                            act.copy(yT[:, u % 2, :, x2 * BLK:(x2 + 1) * BLK],
                                     ps[:, 7, :].rearrange("p (k s) -> p k s", s=BLK)).then_inc(yT_ready, 1)

                gathered(0, 0, 0)
                gathered(0, 0, 1)
                over_pairs(act, body)
                over(layer)

            moe(0)

            transposed(2, [(hkvT, 1), (hqT, 2)])
            for i in range(8):
                dst = (kn, qn)[i // 4]
                half, a = (i % 4) // 2, i % 2
                act.wait_ge(kq_done, i + 1)
                act.activation(dst[:, a, half * 512:(half + 1) * 512], ps[:, (i // 4) * 4 + 2 * a + half, :],
                               ACT.Square).then_inc(sq_done, 1)

            def heads_T(i0, dst, w):
                for b in range(4):
                    act.wait_ge(tkq_done, i0 + b + 1)
                    act.activation(dst[:, 2 * b:2 * b + 2, :], ps[:, i0 + b, :].rearrange("p (k t) -> p k t", t=T),
                                   ACT.Copy, scale=kqcol[:, w:w + 1]).then_inc(kqT_ready, 1)

            def att_v(i):
                act.wait_ge(av_done, i + 1)
                act.copy(v_all[:, i % 2, (i // 2) * 512:(i // 2 + 1) * 512], ps[:, i, :]).then_inc(av_ready, 1)

            heads_T(0, kT, 0)
            att_v(0)
            att_v(1)
            heads_T(4, qT, 2)
            att_v(2)
            att_v(3)
            for h in range(H + 2):
                if h < H:
                    act.wait_ge(mx_ready, h + 1)
                    act.activation(prob[:, h, 0:P], prob[:, h, 0:P], ACT.Exp, bias=nmax[:, h, 0:1],
                                   accum_out=esum[:, h, 0:1])
                    act.activation(prob[:, h, P:NR], prob[:, h, P:NR], ACT.Exp, bias=nmax[:, h, 1:2],
                                   accum_out=esum[:, h, 1:2]).then_inc(ex_done, 1)
                if h >= 2:
                    act.wait_ge(pt_done, h - 1)
                    act.copy(probT[:, h - 2, :], ps[:, (h + 2) % 8, 0:NR]).then_inc(pT_ready, 1)
            for b in range(4):
                act.wait_ge(pv_done, b + 1)
                act.copy(oT1[:, 2 * b:2 * b + 2, :], ps[:, 4 + b, :].rearrange("p (k t) -> p k t", t=T))\
                   .then_inc(oT_ready, 1)
            moe(1)

        @block.vector
        def _(dve):
            steps = [0]

            def link(ins):
                steps[0] += 1
                ins.then_inc(dv, 1)
                dve.wait_ge(dv, steps[0])

            def rms(i, n, width):
                dve.tensor_scalar(ms[:, 0:n], ms[:, 0:n], 1.0 / width, EPS, ALU.mult, ALU.add).then_inc(ms_ready, 1)
                dve.wait_ge(rstd_ready, i)

            def sum_squares():
                for a in range(TT):
                    ins = dve.tensor_tensor_reduce(out=junk, in0=xs[:, a, :], in1=xs[:, a, :], scale=1.0, scalar=0.0,
                                                   op0=ALU.mult, op1=ALU.add, accum_out=ms[:, a:a + 1])
                    link(ins)

            def transposed(stage, dsts):
                for b in (0, 1):
                    dve.wait_ge(nt_done, 4 * stage + b + 1)
                    src = ps[:, 4 + b, :].rearrange("p (k t) -> p k t", t=T)
                    for dst, w in dsts:
                        if w is None:
                            dve.tensor_copy(dst[:, 2 * b:2 * b + 2, :], src).then_inc(hT_dve, 1)
                        else:
                            dve.tensor_tensor(dst[:, 2 * b:2 * b + 2, :], src,
                                              wcol[:, w, 2 * b:2 * b + 2].unsqueeze(2).to_broadcast([P, 2, T]),
                                              ALU.mult).then_inc(hT_dve, 1)

            def norm_plain(i):
                sum_squares()
                rms(i, TT, D)
                for a in range(TT):
                    dve.tensor_scalar(xn[:, a, :], xs[:, a, :], rstd[:, a:a + 1], None, ALU.mult).then_inc(xn_ready, 1)

            def add_projection(base, bank0):
                for i in range(4):
                    dve.wait_ge(pr_done, base + i + 1)
                    dst = xs[:, i % 2, (i // 2) * 512:(i // 2 + 1) * 512]
                    link(dve.tensor_tensor(dst, dst, ps[:, bank0 + i, :], ALU.add))

            dve.wait_ge(x_in, 16)
            norm_plain(POW_MIX0)
            dve.wait_ge(w_in, SMALL)
            link(dve.tensor_tensor(lbw[:, 4, :], lbl[:, 0, :], lbl[:, 1, :], ALU.max))
            dve.tensor_tensor(lbw[:, 0:2, :], lbl[:], lbw[:, 4:5, :].to_broadcast([P, 2, H]),
                              ALU.subtract).then_inc(lb_in, 1)
            dve.wait_ge(lb_exp, 1)
            link(dve.tensor_tensor(lbw[:, 4, :], lbw[:, 2, :], lbw[:, 3, :], ALU.add))
            link(dve.reciprocal(lbw[:, 4, :], lbw[:, 4, :]))
            link(dve.tensor_tensor(lbw[:, 0, :], lbw[:, 2, :], lbw[:, 4, :], ALU.mult))
            link(dve.tensor_scalar(lbw[:, 1, :], lbw[:, 0, :], -1.0, 1.0, ALU.mult, ALU.add))
            link(dve.tensor_copy(masks[:], masks_in))
            link(dve.tensor_scalar(kqcol[:, 2:3], kqcol[:, 1:2], QSCALE, None, ALU.mult))
            transposed(0, [(hT, 0)])
            for hp in range(4):
                sl = slice(hp * 512, (hp + 1) * 512)
                dve.wait_ge(f_exp, hp + 1)
                link(dve.tensor_scalar(f_all[:, sl], f_all[:, sl], 1.0, None, ALU.add))
                link(dve.reciprocal(f_all[:, sl], f_all[:, sl]))
                for h in (2 * hp, 2 * hp + 1):
                    hs = slice(h * T, (h + 1) * T)
                    i = dve.tensor_scalar(f_all[:, hs], f_all[:, hs], lbw[:, 1, h:h + 1], lbw[:, 0, h:h + 1],
                                          ALU.mult, ALU.add)
                link(i)
                dve.tensor_scalar(ks_all[:, sl], f_all[:, sl], -1.0, 1.0, ALU.mult, ALU.add).then_inc(k_ready, 1)

            dve.wait_ge(rb_done, 1)
            dve.tensor_tensor(brow, ps[0:H, 7, 0:NR], future, ALU.add).then_inc(rb_ready, 1)

            def level(l):
                dve.wait_ge(lev_done, l + 1)
                m = 1 << l >> 1
                if l == 0:
                    dve.tensor_tensor(qp_all, qp_all, f_all, ALU.mult).then_inc(upd_ready, 1)
                else:
                    t_now, t_next = (f_all, t_odd) if l % 2 else (t_odd, f_all)
                    tv = t_now[:, 0:2048 // m].rearrange("p (b two) -> p b two", two=2)
                    qv = qp_all.rearrange("p (b two m) -> p b two m", two=2, m=m)
                    kv = ks_all.rearrange("p (b two m) -> p b two m", two=2, m=m)
                    nb = 2048 // (2 * m)
                    dve.tensor_tensor(qv[:, :, 1, :], qv[:, :, 1, :],
                                      tv[:, :, 0].unsqueeze(2).to_broadcast([P, nb, m]), ALU.mult)
                    dve.tensor_tensor(kv[:, :, 0, :], kv[:, :, 0, :],
                                      tv[:, :, 1].unsqueeze(2).to_broadcast([P, nb, m]), ALU.mult)\
                       .then_inc(upd_ready, 1)
                    if l < LEVELS:
                        link(dve.tensor_tensor(t_next[:, 0:nb], tv[:, :, 0], tv[:, :, 1], ALU.mult))
                dve.copy_predicated(sdiag, masks[:, l:l + 1, :].to_broadcast([P, 2 * H, P]),
                                    ps[:, 0:4, :].rearrange("p b (h t) -> p (b h) t", t=P)).then_inc(pred_done, 1)
                dve.wait_ge(upd_ready, l + 1)
                dve.wait_ge(pred_done, l + 1)

            def silu_gate(i):
                gv = gate[:, i % 2, (i // 2) * 512:(i // 2 + 1) * 512]
                dve.wait_ge(g_exp, i + 1)
                link(dve.tensor_scalar(gv, gv, 1.0, None, ALU.add))
                link(dve.reciprocal(gv, gv))
                link(dve.tensor_tensor(gv, ps[:, 4 + i, :], gv, ALU.mult))
                g3 = gv.rearrange("p (h n) -> p h n", n=P)
                dve.tensor_tensor(g3, g3, onorm[:, :].unsqueeze(1).to_broadcast([P, 4, P]), ALU.mult)\
                   .then_inc(gate_ready, 1)

            dve.wait_ge(setup, 3)
            dve.wait_ge(q_ready, 4)
            dve.wait_ge(k_ready, 4)
            for l in range(LEVELS + 1):
                level(l)
                if l >= 4:
                    silu_gate(l - 4)
            for a in range(TT):
                dve.wait_ge(osq_done, a + 1)
                link(dve.tensor_reduce(ms[:, a * H:(a + 1) * H], osq[:, a, :].rearrange("p (h n) -> p h n", n=P),
                                       AX.X, ALU.add))
            rms(POW_O, TT * H, P)
            dve.wait_ge(gate_ready, 4)
            for a in range(TT):
                o3 = og[:, a, :].rearrange("p (h n) -> p h n", n=P)
                link(dve.tensor_tensor(o3, ps[:, 4 + 2 * a:6 + 2 * a, :].rearrange("p b (h n) -> p (b h) n", n=P),
                                       rstd[:, a * H:(a + 1) * H].unsqueeze(2).to_broadcast([P, H, P]), ALU.mult))
                dve.tensor_tensor(og[:, a, :], og[:, a, :], gate[:, a, :], ALU.mult).then_inc(og_ready, 1)
            for b in (0, 1):
                dve.wait_ge(ot_done, b + 1)
                dve.tensor_copy(oT0[:, 2 * b:2 * b + 2, :], ps[:, b, :].rearrange("p (k t) -> p k t", t=T))\
                   .then_inc(oT_ready, 1)
            add_projection(0, 4)

            def router(layer):
                dve.wait_ge(rt_done, layer + 1)
                link(dve.tensor_tensor(lg, ps[:, 3, 0:TT * (NG + E)].rearrange("p (a n) -> p a n", n=NG + E),
                                       br[:, layer:layer + 1, :].to_broadcast([P, TT, NG + E]), ALU.add))

                def b(v, n):
                    return v.unsqueeze(2).to_broadcast([P, TT, n])

                def one_hot(dst, tmp, v, mx, n):
                    link(dve.tensor_reduce(mx, v, AX.X, ALU.max))
                    link(dve.tensor_tensor(tmp, v, b(mx, n), ALU.is_equal))
                    link(dve.tensor_tensor(tmp, tmp, prio[:, 0:n].unsqueeze(1).to_broadcast([P, TT, n]), ALU.mult))
                    link(dve.tensor_reduce(ss, tmp, AX.X, ALU.max))
                    link(dve.tensor_tensor(dst, tmp, b(ss, n), ALU.is_equal))

                one_hot(goh, gpr, lg[:, :, 0:NG], gmx, NG)
                dve.tensor_tensor(gpr, lg[:, :, 0:NG], b(gmx, NG), ALU.subtract).then_inc(gl_ready, 1)
                link(dve.tensor_tensor(tmp32, lg[:, :, NG:].rearrange("p a (g e) -> p a g e", g=NG),
                                       goh.unsqueeze(3).to_broadcast([P, TT, NG, EG]), ALU.mult))
                link(dve.tensor_reduce(es, tmp32.rearrange("p a g e -> p a e g"), AX.X, ALU.add))
                one_hot(oh1, pr8, es, m1, EG)
                link(dve.scalar_tensor_tensor(es2, oh1, -3e38, es, ALU.mult, ALU.add))
                one_hot(oh2, pr8, es2, m2, EG)
                dve.tensor_tensor(dd, m2, m1, ALU.subtract).then_inc(el_ready, 1)
                link(dve.tensor_tensor(a8, oh1, oh2, ALU.add))
                dve.tensor_tensor(asg.rearrange("p a (g e) -> p a g e", g=NG), goh.unsqueeze(3)
                                  .to_broadcast([P, TT, NG, EG]), a8.unsqueeze(2).to_broadcast([P, TT, NG, EG]),
                                  ALU.mult).then_inc(asg_ready, 1)
                dve.wait_ge(gl_exp, layer + 1)
                link(dve.tensor_reduce(gsm, gex, AX.X, ALU.add))
                dve.wait_ge(el_exp, layer + 1)
                link(dve.tensor_scalar(w1, e2, 1.0, None, ALU.add))
                link(dve.tensor_tensor(w1, w1, gsm, ALU.mult))
                link(dve.reciprocal(w1, w1))
                link(dve.tensor_tensor(w2, w1, e2, ALU.mult))
                link(dve.tensor_tensor(oh1, oh1, b(w1, EG), ALU.mult))
                link(dve.tensor_tensor(oh2, oh2, b(w2, EG), ALU.mult))
                link(dve.tensor_tensor(wt8, oh1, oh2, ALU.add))
                link(dve.tensor_tensor(tmp32, goh.unsqueeze(3).to_broadcast([P, TT, NG, EG]),
                                       wt8.unsqueeze(2).to_broadcast([P, TT, NG, EG]), ALU.mult))
                t3 = tmp32.rearrange("p a g e -> p a (g e)")
                for a in range(TT):
                    i = dve.tensor_copy(wgt[:, :, a, :], t3[:, a, :].rearrange("p (q e) -> p q e", e=2))
                dve.wait_ge(pos_done, layer + 1)
                link(dve.scalar_tensor_tensor(tpos, ps[:, 2, 0:TT * E].rearrange("p (a e) -> p a e", e=E), 1.0, asg,
                                              ALU.add, ALU.mult))
                for a in range(TT):
                    i = dve.tensor_scalar(pos[:, :, a, :], tpos[:, a, :].rearrange("p (q e) -> p q e", e=2), -1.0,
                                          None, ALU.add)
                link(i)
                link(dve.tensor_reduce(cmx, ps[:, 2, TT * E:TT * E + E], AX.X, ALU.max))
                for j in range(1, 4):
                    i = dve.tensor_scalar(nblf[:, j:j + 1], cmx, float(j * CAP), None, ALU.is_gt)
                link(i)
                link(dve.tensor_reduce(nblf[:, 0:1], nblf[:, 1:4], AX.X, ALU.add))
                dve.tensor_scalar(nblk[:, layer:layer + 1], nblf[:, 0:1], 1.0, None, ALU.add).then_inc(nblk_ready, 1)

            def over(layer):
                s = ov[layer]
                dve.wait_ge(nblk_ready, layer + 1)
                n = dve.value_load(nblk[0:1, layer:layer + 1], min_val=1, max_val=4)
                with dve.If(n > 1):
                    dve.memset(mark[:, 2:3], 0.0).then_inc(s["x"], 1)
                    with dve.Fori(1, n) as b:
                        dve.tensor_scalar(pos, pos, -float(CAP), None, ALU.add).then_inc(s["shift"], 1)
                        dve.wait_ge(s["shift"], b)
                        dve.memset(mark[:, 4:5], 0.0)
                        with dve.Fori(0, PAIRS) as q:
                            v = b * PAIRS + q - (PAIRS - 1)
                            dve.wait_ge(s["x"], v)
                            build_pick(q, s["picked"])
                            dve.wait_ge(s["picked"], v)
                            dve.tensor_tensor(pickw, pick, wgt[:, q].unsqueeze(3).to_broadcast([P, TT, 2, BLK]),
                                              ALU.mult).then_inc(s["pick"], 1)
                            dve.wait_ge(s["exp"], v)
                            both = ((en, 6), (en_b, 1))
                            for e_, bank in both:
                                i = dve.tensor_scalar(e_, e_, 1.0, None, ALU.add)
                            i.then_inc(s["den"], 1)
                            dve.wait_ge(s["den"], v)
                            for e_, bank in both:
                                i = dve.reciprocal(e_, e_)
                            i.then_inc(s["rec"], 1)
                            dve.wait_ge(s["rec"], v)
                            for e_, bank in both:
                                i = dve.tensor_tensor(e_, e_, ps[:, bank, 0:256], ALU.mult)
                            i.then_inc(s["sil"], 1)
                            dve.wait_ge(s["sil"], v)
                            for x2, (e_, bank) in enumerate(both):
                                i = dve.tensor_tensor(hid[:, x2].rearrange("p m s -> p (m s)"), e_,
                                                      ps[:, bank, 256:512], ALU.mult)
                            i.then_inc(s["hid"], 1)
                            dve.wait_ge(s["c"], v)
                            for a in range(TT):
                                i = dve.tensor_tensor(xs[:, a, :], xs[:, a, :],
                                                      ps[:, 2 * a:2 * a + 2, :].rearrange("p b n -> p (b n)"),
                                                      ALU.add)
                            i.then_inc(s["x"], 1)
                    dve.memset(mark[:, 3:4], 0.0).then_inc(s["end"], 1)
                    dve.wait_ge(s["end"], 1)

            def build_pick(q, signal):
                ins = dve.tensor_tensor(pick, pos[:, q].unsqueeze(3).to_broadcast([P, TT, 2, BLK]),
                                        slot[:, :].unsqueeze(1).unsqueeze(1).to_broadcast([P, TT, 2, BLK]),
                                        ALU.is_equal)
                ins.then_inc(signal, 1)

            def moe(layer):
                st = 1 + 2 * layer
                sum_squares()
                rms((POW_FFN0, POW_FFN1)[layer], TT, D)
                dve.wait_ge(rowload, 16 * (layer + 1))
                for a in range(TT):
                    dve.scalar_tensor_tensor(hn[:, a, :], xs[:, a, :], rstd[:, a:a + 1], wrow, ALU.mult,
                                             ALU.mult).then_inc(xn_ready, 1)
                transposed(st, [(hrT, None)])
                router(layer)
                P0 = layer * PAIRS

                def silu(it, e):
                    dve.wait_ge(exp_done, it * (2 * UN) + (e + 1))
                    dve.tensor_scalar(en, en, 1.0, None, ALU.add).then_inc(silu_step, 1)
                    dve.wait_ge(silu_step, it * (6 * UN) + (3 * e + 1))
                    dve.reciprocal(en, en).then_inc(silu_step, 1)
                    dve.wait_ge(silu_step, it * (6 * UN) + (3 * e + 2))
                    dve.tensor_tensor(th, en, ps[:, 6, 0:256], ALU.mult).then_inc(silu_step, 1)
                    dve.wait_ge(silu_step, it * (6 * UN) + (3 * e + 3))
                    if not (type(it) is int and it * 2 * UN + e < 2):
                        dve.wait_ge(y_done, it * (2 * UN) + (e - 1))
                    dve.tensor_tensor(hid[:, e % 2].rearrange("p m s -> p (m s)"), th, ps[:, 6, 256:512],
                                      ALU.mult).then_inc(hid_ready, 1)

                def spread_out(it, u):
                    q = P0 + u
                    dve.wait_ge(st_done, it * UN + (q + 1))
                    if not (type(it) is int and it * UN + q < 1):
                        dve.wait_ge(c_done, it * (2 * UN) + 2 * q)
                    dve.tensor_copy(spread, ps[:, 5, 0:T]).then_inc(s_ready, 1)

                def y_out(it, u, half):
                    q = P0 + u
                    dve.wait_ge(t_done, it * (2 * UN) + (2 * q + 1 + half))
                    dve.tensor_copy(y[:, half * 512:(half + 1) * 512], ps[:, 5, :]).then_inc(y_ready, 1)

                def pick_for(it, u):
                    q = P0 + u
                    if not (type(it) is int and it * UN + q < 1):
                        dve.wait_ge(gat_done, it * (2 * UN) + 2 * q)
                        dve.wait_ge(pickw_ready, it * UN + q)
                    build_pick(it * UN + u, pick_ready)

                def weigh(it, u):
                    q = P0 + u
                    dve.wait_ge(pick_ready, it * UN + (q + 1))
                    if not (type(it) is int and it * UN + q < 1):
                        dve.wait_ge(st_done, it * UN + q)
                    dve.tensor_tensor(pickw, pick, wgt[:, it * UN + u].unsqueeze(3).to_broadcast([P, TT, 2, BLK]),
                                      ALU.mult).then_inc(pickw_ready, 1)

                pick_for(0, 0)

                def body(it):
                    for u in range(UN):
                        first = is_int(it, 0) and u == 0
                        last = is_int(it, ITERS - 1) and u == UN - 1
                        if not first:
                            spread_out(it, u - 1)
                        weigh(it, u)
                        if not last:
                            pick_for(it, u + 1)
                        silu(it, 2 * (P0 + u))
                        if not first:
                            y_out(it, u - 1, 0)
                        silu(it, 2 * (P0 + u) + 1)
                        if not first:
                            y_out(it, u - 1, 1)

                over_pairs(dve, body)
                spread_out(ITERS - 1, UN - 1)
                y_out(ITERS - 1, UN - 1, 0)
                y_out(ITERS - 1, UN - 1, 1)
                dve.wait_ge(c_done, 2 * (P0 + PAIRS))
                for a in range(TT):
                    link(dve.tensor_tensor(xs[:, a, :], xs[:, a, :],
                                           ps[:, 2 * a:2 * a + 2, :].rearrange("p b n -> p (b n)"), ALU.add))
                over(layer)

            moe(0)

            norm_plain(POW_MIX1)
            transposed(2, [(hkvT, 1), (hqT, 2)])

            def head_norm(i0, dst, i):
                for j in range(4):
                    half, a = j // 2, j % 2
                    dve.wait_ge(sq_done, i0 + j + 1)
                    link(dve.tensor_reduce(ms[:, a * H + half * 4:a * H + half * 4 + 4],
                                           dst[:, a, half * 512:(half + 1) * 512]
                                           .rearrange("p (h n) -> p h n", n=P), AX.X, ALU.add))
                rms(i, TT * H, P)
                for a in range(TT):
                    dve.tensor_tensor(dst[:, a, :].rearrange("p (h n) -> p h n", n=P),
                                      ps[:, i0 + 2 * a:i0 + 2 * a + 2, :].rearrange("p b (h n) -> p (b h) n", n=P),
                                      rstd[:, a * H:(a + 1) * H].unsqueeze(2).to_broadcast([P, H, P]),
                                      ALU.mult).then_inc(kqn_ready, 1)

            head_norm(0, kn, POW_K)
            head_norm(4, qn, POW_Q)
            dve.wait_ge(biasload, 16)
            for h in range(H + 1):
                if h < H:
                    bank = (4 + h) % 8
                    dve.wait_ge(sc_done, h + 1)
                    dve.tensor_tensor(prob[:, h, 0:P], ps[:, bank, 0:P], bias[:, h, P:T], ALU.add)
                    link(dve.tensor_tensor(prob[:, h, P:NR], ps[:, bank, P:NR], bias[:, h, :], ALU.add))
                    dve.tensor_reduce(nmax[:, h, 0:1], prob[:, h, 0:P], AX.X, ALU.max, negate=True)
                    dve.tensor_reduce(nmax[:, h, 1:2], prob[:, h, P:NR], AX.X, ALU.max, negate=True)\
                       .then_inc(mx_ready, 1)
                if h >= 1:
                    dve.wait_ge(ex_done, h)
                    dve.reciprocal(einv[:, h - 1, :], esum[:, h - 1, :]).then_inc(ei_ready, 1)
            add_projection(4, 0)
            moe(1)
            for a in range(TT):
                dve.memset(mark[:, a:a + 1], 0.0).then_inc(x_ready, 1)

        @block.tensor
        def _(pe):
            def mm(o, l, r, start=True, stop=True):
                return pe.matmul(o, l, r, start=start, stop=stop)

            def tr(o, i):
                return pe.transpose(o, i, ident[:])

            def arrived(c, it=0):
                pe.wait_ge(loaded[c % RING], it * (16 * TURNS) + 16 * (c // RING + 1))

            def transposes(stage, src):
                for a in range(TT):
                    pe.wait_ge(xn_ready, TT * stage + a + 1)
                    for k in range(KD):
                        i = tr(ps[:, 4 + k // 2, (k % 2) * T + a * P:(k % 2) * T + (a + 1) * P],
                               src[:, a, k * P:(k + 1) * P])
                        if a == TT - 1 and k % 2:
                            i.then_inc(nt_done, 1)

            def project(c, lhs, bank, a, signal):
                arrived(c)
                for k in range(KD):
                    i = mm(ps[:, bank, :], lhs[:, k, a * P:(a + 1) * P], up_view(c)[:, k, :], k == 0, k == KD - 1)
                i.then_inc(signal, 1)

            pe.wait_ge(c_in, 16)
            transposes(0, xn)
            pe.wait_ge(hT_dve, 2)
            pe.wait_ge(hT_act, 2)
            for j, (signal, bank0) in enumerate(((f_done, 0), (q_done, 4))):
                for hp in range(4):
                    c = MIX0 + 2 * j + hp // 2
                    arrived(c)
                    if j == 1 and hp == 3:
                        pe.wait_ge(rb_ready, 1)
                    for h in (2 * hp, 2 * hp + 1):
                        for k in range(KD):
                            i = mm(ps[:, bank0 + hp, (h % 2) * T:(h % 2 + 1) * T],
                                   up_view(c)[:, k, (h % 4) * P:(h % 4 + 1) * P], hT[:, k, :], k == 0, k == KD - 1)
                    i.then_inc(signal, 1)
                if j == 0:
                    pe.wait_ge(w_in, SMALL)
                    mm(ps[0:H, 7, 0:NR], rbw, bucket).then_inc(rb_done, 1)

            q3 = qp_all.rearrange("p (h t) -> p h t", t=T)
            k3 = ks_all.rearrange("p (h t) -> p h t", t=T)
            pe.wait_ge(k_ready, 4)
            pe.wait_ge(q_ready, 4)
            for l in range(LEVELS + 1):
                if l:
                    pe.wait_ge(upd_ready, l)
                    pe.wait_ge(pred_done, l)
                for h in range(H):
                    for a in range(TT):
                        b = 2 * h + a
                        i = mm(ps[:, b // 4, (b % 4) * P:(b % 4 + 1) * P], k3[:, h, a * P:(a + 1) * P],
                               q3[:, h, a * P:(a + 1) * P])
                i.then_inc(lev_done, 1)
                if l >= 4:
                    pe.wait_ge(v_ready, l - 3)
                project(MIX0 + 4 + l // 2, hT, 4 + l % 4, l % 2, vg_done)
            pe.wait_ge(upd_ready, LEVELS + 1)
            pe.wait_ge(pred_done, LEVELS + 1)
            for h in range(H):
                i = mm(ps[:, h // 4, (h % 4) * P:(h % 4 + 1) * P], k3[:, h, 0:P], q3[:, h, P:T])
            i.then_inc(lev_done, 1)
            pe.wait_ge(gate_ready, 4)
            pe.wait_ge(v_ready, 4)
            for a in range(TT):
                if a:
                    pe.wait_ge(cross_ready, 1)
                for h in range(H):
                    o = ps[:, 4 + 2 * a + h // 4, (h % 4) * P:(h % 4 + 1) * P]
                    if a:
                        mm(o, scross[:, h, :], v_all[:, 0, h * P:(h + 1) * P], True, False)
                    i = mm(o, sdiag[:, 2 * h + a, :], v_all[:, a, h * P:(h + 1) * P], a == 0, True)
                i.then_inc(o_done, 1)
            for a in range(TT):
                pe.wait_ge(og_ready, a + 1)
                for k in range(KD):
                    i = tr(ps[:, k // 2, (k % 2) * T + a * P:(k % 2) * T + (a + 1) * P], og[:, a, k * P:(k + 1) * P])
                    if a == TT - 1 and k % 2:
                        i.then_inc(ot_done, 1)
            pe.wait_ge(oT_ready, 4)
            for i in range(4):
                project(MIX0 + 8 + i // 2, oT0, 4 + i, i % 2, pr_done)

            def gather(q, bank, half, signal):
                for k in range(4):
                    for a in range(TT):
                        i = mm(ps[:, bank, k * P:(k + 1) * P], hn[:, a, (4 * half + k) * P:(4 * half + k + 1) * P],
                               pick[:, a].rearrange("p e s -> p (e s)"), a == 0, a == TT - 1)
                if signal is not None:
                    i.then_inc(signal, 1)
                return i

            def up(c, bank, half, buf, x2, signal):
                for m in range(KF):
                    for k in range(KD):
                        i = mm(ps[:, bank, half * 256 + m * BLK:half * 256 + (m + 1) * BLK],
                               up_view(c)[:, k, m * P:(m + 1) * P], xgT[:, buf, k, x2 * BLK:(x2 + 1) * BLK],
                               k == 0, k == KD - 1)
                if signal is not None:
                    i.then_inc(signal, 1)

            def down(c, bank, buf, signal):
                for m in range(KD):
                    for k in range(KF):
                        i = mm(ps[:, bank, m * BLK:(m + 1) * BLK], down_view(c)[:, k, m * P:(m + 1) * P],
                               hid[:, buf, k, :], k == 0, k == KF - 1)
                if signal is not None:
                    i.then_inc(signal, 1)

            def spread_T(bank, signal):
                for a in range(TT):
                    i = tr(ps[:, bank, a * P:(a + 1) * P], pickw[:, a].rearrange("p e s -> p (e s)"))
                if signal is not None:
                    i.then_inc(signal, 1)

            def over(layer):
                s = ov[layer]
                pe.wait_ge(nblk_ready, layer + 1)
                n = pe.value_load(nblk[0:1, layer:layer + 1], min_val=1, max_val=4)
                with pe.If(n > 1):
                    with pe.Fori(1, n) as b:
                        with pe.Fori(0, PAIRS) as q:
                            v = b * PAIRS + q - (PAIRS - 1)
                            pe.wait_ge(s["pick"], v)
                            gather(q, 4, 0, None)
                            gather(q, 5, 1, None)
                            spread_T(0, s["gat"])
                            pe.wait_ge(s["xg"], v)
                            pe.wait_ge(s["w"], v * (16 * 6))
                            up(0, 6, 0, 0, 0, None)
                            up(1, 6, 1, 0, 0, None)
                            up(3, 1, 0, 0, 1, None)
                            up(4, 1, 1, 0, 1, s["hu"])
                            pe.wait_ge(s["hid"], v)
                            down(2, 7, 0, None)
                            down(5, 2, 1, s["y"])
                            pe.wait_ge(s["yt"], v)
                            for k in range(KD):
                                i = tr(ps[:, k // 4, (k % 4) * P:(k % 4 + 1) * P], yT[:, 0, k, :])
                            i.then_inc(s["tr"], 1)
                            pe.wait_ge(s["ye"], v)
                            for a in range(TT):
                                for half in range(2):
                                    i = mm(ps[:, 2 * a + half, :], spread[:, a * P:(a + 1) * P],
                                           y[:, half * 512:(half + 1) * 512])
                            i.then_inc(s["c"], 1)
                    pe.wait_ge(s["end"], 1)

            def moe(layer):
                transposes(1 + 2 * layer, hn)
                pe.wait_ge(hT_dve, (4, 10)[layer])
                pe.wait_ge(hT_act, (4, 10)[layer])
                for a in range(TT):
                    for k in range(KD):
                        i = mm(ps[:, 3, a * (NG + E):(a + 1) * (NG + E)], hrT[:, k, a * P:(a + 1) * P],
                               wr[:, layer, k, :], k == 0, k == KD - 1)
                i.then_inc(rt_done, 1)
                pe.wait_ge(asg_ready, layer + 1)
                mm(ps[:, 2, 0:E], before[:], asg[:, 0, :])
                mm(ps[:, 2, E:2 * E], ones[:], asg[:, 0, :], True, False)
                mm(ps[:, 2, E:2 * E], before[:], asg[:, 1, :], False, True)
                mm(ps[:, 2, 2 * E:3 * E], ones[:], asg[:, 0, :], True, False)
                mm(ps[:, 2, 2 * E:3 * E], ones[:], asg[:, 1, :], False, True).then_inc(pos_done, 1)
                P0 = layer * PAIRS

                def gather_next(it, u, half):
                    q = P0 + u
                    if half == 0:
                        pe.wait_ge(pick_ready, it * UN + (q + 1))
                    if not (type(it) is int and it * UN + q < 1 and half == 0):
                        pe.wait_ge(xg_ready, it * (2 * UN) + (2 * q + half))
                    gather(None, 4, half, gat_done)

                def spread_of(it, u):
                    q = P0 + u
                    pe.wait_ge(pickw_ready, it * UN + (q + 1))
                    if not (type(it) is int and it * UN + q < 1):
                        pe.wait_ge(y_ready, it * (2 * UN) + 2 * q)
                    spread_T(5, st_done)

                def y_rows(it, u, half):
                    q = P0 + u
                    if half == 0:
                        pe.wait_ge(yT_ready, it * (2 * UN) + (2 * q + 2))
                        pe.wait_ge(s_ready, it * UN + (q + 1))
                    else:
                        pe.wait_ge(y_ready, it * (2 * UN) + (2 * q + 1))
                    for j in range(4):
                        i = tr(ps[:, 5, j * P:(j + 1) * P], yT[:, u % 2, 4 * half + j, :])
                    i.then_inc(t_done, 1)

                def combine(it, u, half, start, stop):
                    q = P0 + u
                    if half == 0:
                        pe.wait_ge(s_ready, it * UN + (q + 1))
                    pe.wait_ge(y_ready, it * (2 * UN) + (2 * q + 1 + half))
                    for a in range(TT):
                        i = mm(ps[:, 2 * a + half, :], spread[:, a * P:(a + 1) * P],
                               y[:, half * 512:(half + 1) * 512], start, stop)
                    i.then_inc(c_done, 1)

                gather_next(0, 0, 0)
                gather_next(0, 0, 1)

                def body(it):
                    for u in range(UN):
                        first = is_int(it, 0) and u == 0
                        last = is_int(it, ITERS - 1) and u == UN - 1
                        start = is_int(it, 0) and u == 1
                        q = P0 + u
                        c0 = MOE[layer] + 6 * u
                        if not first:
                            spread_of(it, u - 1)
                        for x2 in range(2):
                            e = 2 * q + x2
                            if x2 == 0:
                                pe.wait_ge(xg_ready, it * (2 * UN) + (2 * q + 2))
                            for half in range(2):
                                arrived(c0 + 3 * x2 + half, it)
                                if half == 0 and not (type(it) is int and it * 2 * UN + e < 1):
                                    pe.wait_ge(hid_ready, it * (2 * UN) + e)
                                up(c0 + 3 * x2 + half, 6, half, u % 2, x2, hu_done)
                            if not last:
                                gather_next(it, u + 1, x2)
                            if not first:
                                y_rows(it, u - 1, x2)
                                if x2:
                                    combine(it, u - 1, 0, start, False)
                            arrived(c0 + 3 * x2 + 2, it)
                            pe.wait_ge(hid_ready, it * (2 * UN) + (e + 1))
                            if not (type(it) is int and it * 2 * UN + e < 1):
                                pe.wait_ge(yT_ready, it * (2 * UN) + e)
                            down(c0 + 3 * x2 + 2, 7, x2, y_done)
                        if not first:
                            combine(it, u - 1, 1, start, False)

                over_pairs(pe, body)
                spread_of(ITERS - 1, UN - 1)
                y_rows(ITERS - 1, UN - 1, 0)
                y_rows(ITERS - 1, UN - 1, 1)
                combine(ITERS - 1, UN - 1, 0, False, True)
                combine(ITERS - 1, UN - 1, 1, False, True)
                over(layer)

            moe(0)

            transposes(2, xn)
            pe.wait_ge(hT_dve, 8)
            pe.wait_ge(hT_act, 8)
            for i in range(4):
                project(MIX1 + i // 2, hkvT, 2 * (i % 2) + i // 2, i % 2, kq_done)
            for i in range(4):
                project(MIX1 + 2 + i // 2, hqT, 4 + 2 * (i % 2) + i // 2, i % 2, kq_done)

            def heads_transposes(src, bank0, n0):
                for a in range(TT):
                    pe.wait_ge(kqn_ready, n0 + a + 1)
                    if a == 0:
                        pe.wait_ge(kqn_ready, n0 + 2)
                    for h in range(H):
                        i = tr(ps[:, bank0 + h // 2, (h % 2) * T + a * P:(h % 2) * T + (a + 1) * P],
                               src[:, a, h * P:(h + 1) * P])
                        if a and h % 2:
                            i.then_inc(tkq_done, 1)

            def att_v(i):
                pe.wait_ge(kqT_ready, i + 1)
                project(MIX1 + 4 + i // 2, hkvT, i, i % 2, av_done)

            heads_transposes(kn, 0, 0)
            att_v(0)
            att_v(1)
            heads_transposes(qn, 4, 2)
            att_v(2)
            att_v(3)
            pe.wait_ge(kqT_ready, 8)
            for h in range(H):
                if h == 4:
                    pe.wait_ge(av_ready, 4)
                bank = (4 + h) % 8
                mm(ps[:, bank, 0:P], qT[:, h, 0:P], kT[:, h, 0:P])
                mm(ps[:, bank, P:NR], qT[:, h, P:T], kT[:, h, :]).then_inc(sc_done, 1)
            for h in range(H):
                pe.wait_ge(pn_ready, h + 1)
                for j in range(3):
                    i = tr(ps[:, (4 + h) % 8, j * P:(j + 1) * P], prob[:, h, j * P:(j + 1) * P])
                i.then_inc(pt_done, 1)
            for b in range(4):
                pe.wait_ge(pT_ready, 2 * b + 2)
                for h in (2 * b, 2 * b + 1):
                    o = (h % 2) * T
                    mm(ps[:, 4 + b, o:o + T], v_all[:, 0, h * P:(h + 1) * P], probT[:, h, 0:T], True, False)
                    i = mm(ps[:, 4 + b, o + P:o + T], v_all[:, 1, h * P:(h + 1) * P], probT[:, h, T:NR], False, True)
                i.then_inc(pv_done, 1)
            pe.wait_ge(oT_ready, 8)
            pe.wait_ge(pT_ready, 8)
            for i in range(4):
                project(MIX1 + 6 + i // 2, oT1, i, i % 2, pr_done)
            moe(1)


SMALL = 16 * 22

_INS = ['x', 'mix_norm', 'ffn_norm', 'hg_w_in', 'hg_lb', 'hg_o_norm', 'hg_w_out', 'kv_norm', 'w_kv', 'k_norm',
        'att_w_q', 'q_norm', 'att_w_o', 'rel_bias', 'moe_w_group', 'moe_b_group', 'moe_w_expert', 'moe_b_expert',
        'moe_w_in', 'moe_w_out']


def constants():
    import math
    import numpy as np
    i = np.arange(P)
    masks = np.zeros((P, LEVELS + 1, P), np.float32)
    masks[i, 0, i] = 1
    for l in range(1, LEVELS + 1):
        m = 1 << (l - 1)
        masks[:, l, :] = ((i[:, None] // (2 * m) == i[None, :] // (2 * m)) & (i[:, None] // m % 2 == 0)
                          & (i[None, :] // m % 2 == 1))
    places = np.arange(BLK, dtype=np.float32)
    places[CAP:] = -1000.0
    dist = T - 1 - np.arange(NR)
    n = np.maximum(dist, 0)
    ratio = np.log(np.maximum(n, 16).astype(np.float32) / np.float32(16)) / np.float32(math.log(1024 / 16))
    buckets = np.where(n < 16, n, np.minimum(16 + (ratio * np.float32(16)).astype(np.int32), 31))
    return {
        "ident": np.eye(P, dtype=np.float32),
        "before": (i[:, None] < i[None, :]).astype(np.float32),
        "masks": masks,
        "slot": np.ascontiguousarray(np.broadcast_to(places, (P, BLK))),
        "prio": np.ascontiguousarray(np.broadcast_to(np.arange(EG, 0, -1, dtype=np.float32), (P, EG))),
        "bucket": (buckets[None, :] == np.arange(32)[:, None]).astype(np.float32),
        "future": np.ascontiguousarray(np.broadcast_to(np.where(dist < 0, -1e30, 0.0).astype(np.float32), (H, NR))),
    }


def kernel(**inputs):
    import numpy as _np
    import concourse.bacc as _bacc
    from concourse.bass_utils import run_bass_kernel_spmd as _run

    nc = _bacc.Bacc("TRN2", target_bir_lowering=False, num_devices=1)
    arrays, args = {}, []

    def give(name, a):
        arrays[name] = a
        args.append(nc.dram_tensor(name, a.shape, mybir.dt.from_np(a.dtype), kind="ExternalInput").ap())

    for name in _INS:
        give(f"in_{name}", _np.ascontiguousarray(inputs[name]))
    for name, a in constants().items():
        give(f"const_{name}", a)
    args.append(nc.dram_tensor("out_0", (1, T, D), FP32, kind="ExternalOutput").ap())
    build(nc, *args)
    r = _run(nc, [arrays], core_ids=[0])
    return r.results[0]["out_0"]
```

```python
import concourse.bass as bass
from concourse import mybir
from contextlib import ExitStack

FP32 = mybir.dt.float32
I32 = mybir.dt.int32
U8 = mybir.dt.uint8
ALU = mybir.AluOpType
ACT = mybir.ActivationFunctionType
AX = mybir.AxisListType

P = 128
T = 256
TT = T // P
D = 1024
KD = D // P
H = 8
LEVELS = 7
NG, EG = 4, 8
E = NG * EG
FF = 512
KF = FF // P
EPS = 1e-6
QSCALE = float(P) ** -0.5

BLK = 64
CAP = 64
PAIRS = E // 2
RING = 8
UN = 4
ITERS = PAIRS // UN
TURNS = 6 * UN // RING
MIX0, MOE0 = 0, 10
MIX1 = MOE0 + 6 * PAIRS
MOE1 = MIX1 + 8
MOE = [MOE0, MOE1]
NR = 3 * P

POW_MIX0, POW_O, POW_FFN0, POW_MIX1, POW_K, POW_Q, POW_FFN1 = range(1, 8)


def build(nc, x, mix_norm, ffn_norm, hg_w_in, hg_lb, hg_o_norm, hg_w_out, kv_norm, w_kv, k_norm,
          att_w_q, q_norm, att_w_o, rel_bias, moe_w_group, moe_b_group, moe_w_expert, moe_b_expert,
          moe_w_in, moe_w_out, c_ident, c_before, c_masks, c_slot, c_prio, c_bucket, c_future, out):
    with ExitStack() as ctx:
        def sb(name, shape, dt=FP32):
            return ctx.enter_context(nc.sbuf_tensor(name, shape, dt))

        def sem(name):
            return ctx.enter_context(nc.semaphore(name))

        ctx.enter_context(nc.allow_non_contiguous_dma(reason="small vectors spread over partitions"))
        ps = ctx.enter_context(nc.psum_tensor("ps", [P, 8, 512], FP32))
        bias_dram = nc.dram_tensor("bias_scratch", (H, P * (NR + 1)), FP32, kind="Internal").ap()

        ring = sb("ring", [P, RING, 4096])
        xs = sb("xs", [P, TT, D])
        ident = sb("ident", [P, P])
        before = sb("before", [P, P])
        ones = sb("ones", [P, P])
        masks = sb("masks", [P, LEVELS + 1, P], U8)
        slot = sb("slot", [P, BLK])
        prio = sb("prio", [P, EG])
        wcol = sb("wcol", [P, 3, KD])
        lbl = sb("lbl", [P, 2, H])
        lbw = sb("lbw", [P, 6, H])
        onorm = sb("onorm", [P, P])
        kqcol = sb("kqcol", [P, 3])
        wr = sb("wr", [P, 2, KD, NG + E])
        br = sb("br", [P, 2, NG + E])
        ms = sb("ms", [P, 16])
        rstd = sb("rstd", [P, 16])
        mhalf = sb("mhalf", [P, 16])
        nmax = sb("nmax", [P, H, 2])
        esum = sb("esum", [P, H, 2])
        einv = sb("einv", [P, H, 2])
        nblk = sb("nblk", [P, 2], I32)
        nblf = sb("nblf", [P, 4])
        mark = sb("mark", [P, 8])

        work = sb("work", [P, 8, 2048])

        def region(i, k=1):
            return work[:, i:i + k, :].rearrange("p r n -> p (r n)")

        hT = region(0).rearrange("p (k t) -> p k t", t=T)
        f_all = region(1)
        ks_all = region(2)
        qp_all = region(3)
        sdiag = region(4).rearrange("p (b t) -> p b t", t=P)
        scross = region(5)[:, 0:1024].rearrange("p (h t) -> p h t", t=P)
        t_odd = region(5)[:, 1024:2048]
        v_all = region(6).rearrange("p (a n) -> p a n", n=D)
        gate = region(7).rearrange("p (a n) -> p a n", n=D)
        xn = region(5).rearrange("p (a n) -> p a n", n=D)
        osq = region(0).rearrange("p (a n) -> p a n", n=D)
        og = region(2).rearrange("p (a n) -> p a n", n=D)
        oT0 = region(3).rearrange("p (k t) -> p k t", t=T)
        hkvT = hT
        hqT = region(1).rearrange("p (k t) -> p k t", t=T)
        kn = region(2).rearrange("p (a n) -> p a n", n=D)
        qn = region(3).rearrange("p (a n) -> p a n", n=D)
        kT = region(4).rearrange("p (h t) -> p h t", t=T)
        qT = region(5).rearrange("p (h t) -> p h t", t=T)
        bias = region(7).rearrange("p (h s) -> p h s", s=T)
        prob = region(0, 2)[:, 0:H * NR].rearrange("p (h s) -> p h s", s=NR)
        probT = region(2, 2)[:, 0:H * NR].rearrange("p (h s) -> p h s", s=NR)
        oT1 = region(4).rearrange("p (h t) -> p h t", t=T)
        hn = region(0).rearrange("p (a n) -> p a n", n=D)
        hrT = region(1).rearrange("p (k t) -> p k t", t=T)
        xgT = region(2).rearrange("p (b k s) -> p b k s", b=2, s=P)
        y = region(3)[:, 0:1024]
        en = region(3)[:, 1024:1536]
        hid = region(3)[:, 1536:2048]
        hidT = region(6)[:, 1024:1536].rearrange("p (k s) -> p k s", s=P)
        pick = region(4)[:, 0:256].rearrange("p (a e s) -> p a e s", a=TT, s=BLK)
        pickw = region(4)[:, 256:512].rearrange("p (a e s) -> p a e s", a=TT, s=BLK)
        spread = region(4)[:, 512:768]
        wrow = region(4)[:, 1024:2048]
        rt = region(5)
        lg = rt[:, 0:72].rearrange("p (a n) -> p a n", n=NG + E)
        gmx, gsm, m1, m2, dd, e2, ss, w1, w2 = (rt[:, 72 + 2 * i:74 + 2 * i] for i in range(9))
        goh, gpr, gex = (rt[:, 100 + 8 * i:108 + 8 * i].rearrange("p (a g) -> p a g", g=NG) for i in range(3))
        es, oh1, oh2, pr8, wt8, a8, es2 = (rt[:, 128 + 16 * i:144 + 16 * i].rearrange("p (a g) -> p a g", g=EG)
                                           for i in range(7))
        tmp32 = rt[:, 256:320].rearrange("p (a g e) -> p a g e", a=TT, g=NG)
        asg = rt[:, 320:384].rearrange("p (a e) -> p a e", a=TT)
        wgt = rt[:, 384:448].rearrange("p (q a e) -> p q a e", a=TT, e=2)
        pos = rt[:, 448:512].rearrange("p (q a e) -> p q a e", a=TT, e=2)
        tpos = rt[:, 512:576].rearrange("p (a e) -> p a e", a=TT)
        cmx = rt[:, 576:577]
        junk = region(6)[:, 0:1024]
        rbw = region(6)[0:32, 1024:1032]
        bucket = region(6)[0:32, 1040:1040 + NR]
        future = region(6)[0:H, 1430:1430 + NR]
        brow = region(7)[0:H, 0:NR]
        masks_in = region(7)[:, 1024:2048].rearrange("p (l t) -> p l t", t=P)

        loaded = [sem(f"slot_loaded{i}") for i in range(RING)]
        x_in, c_in, w_in = sem("x_in"), sem("const_in"), sem("small_in")
        rowload, biasload, biasout = sem("ffn_row_in"), sem("bias_in"), sem("bias_out")
        setup = sem("memsets_done")
        dv = sem("dve_step")
        ms_ready, rstd_ready = sem("ms_ready"), sem("rstd_ready")
        xn_ready, nt_done = sem("normed_ready"), sem("normed_transposed")
        hT_dve, hT_act = sem("hT_by_dve"), sem("hT_by_act")
        lb_in, lb_exp = sem("lb_logits"), sem("lb_exp")
        f_done, f_exp, k_ready, q_done, q_ready = (sem(n) for n in ("f_done", "f_exp", "k_ready", "q_done", "q_ready"))
        lev_done, upd_ready, pred_done = sem("level_done"), sem("level_operands"), sem("level_scores")
        vg_done, v_ready, g_exp, gate_ready = (sem(n) for n in ("vg_done", "v_ready", "g_exp", "gate_ready"))
        cross_ready = sem("cross_ready")
        o_done, osq_done, og_ready = sem("o_done"), sem("osq_done"), sem("og_ready")
        ot_done, oT_ready, pr_done, x_ready = (sem(n) for n in ("ot_done", "oT_ready", "proj_done", "x_ready"))
        rb_done, rb_ready = sem("bias_row_done"), sem("bias_row_ready")
        rt_done, gl_ready, gl_exp, el_ready, el_exp = (sem(n) for n in ("router_done", "group_logits", "group_exp",
                                                                        "top2_gap", "top2_exp"))
        asg_ready, pos_done, nblk_ready = sem("assigned"), sem("positions_done"), sem("blocks_ready")
        pick_ready, pickw_ready, gat_done, xg_ready = (sem(n) for n in ("pick_ready", "pickw_ready", "gather_done",
                                                                        "gathered_ready"))
        up_done, exp_done, den_ready, sig_ready, silu_ready, hid_ready = (
            sem(n) for n in ("up_done", "silu_exp", "silu_denominator", "silu_sigmoid", "silu_ready", "hidden_ready"))
        ht_done, hidT_ready = sem("hidden_transposed"), sem("hiddenT_ready")
        st_done, s_ready = sem("spread_transposed"), sem("spread_ready")
        down_done, y_ready, c_done = sem("down_done"), sem("y_ready"), sem("combine_done")
        kq_done, sq_done, kqn_ready, tkq_done, kqT_ready = (sem(n) for n in ("kq_done", "kq_squares", "kq_normed",
                                                                             "kq_transposed", "kqT_ready"))
        av_done, av_ready = sem("att_v_done"), sem("att_v_ready")
        sc_done, mx_ready, ex_done, ei_ready, pn_ready = (sem(n) for n in ("scores_done", "max_ready", "probs_exp",
                                                                           "inv_sum", "probs_ready"))
        pt_done, pT_ready, pv_done = sem("probs_transposed"), sem("probT_ready"), sem("pv_done")
        out_done = sem("out_done")
        ov = [{n: sem(f"over{l}_{n}") for n in ("w", "shift", "picked", "pick", "gat", "xg", "up", "exp", "den", "rec",
                                                "sil", "hid", "ht", "hidT", "y", "ye", "c", "x", "end")}
              for l in range(2)]

        def chunk(c):
            return ring[:, c % RING, :]

        def up_view(c):
            return chunk(c).rearrange("p (k n) -> p k n", n=512)

        def down_view(c):
            return chunk(c).rearrange("p (k n) -> p k n", n=D)

        def over_pairs(eng, body):
            body(0)
            with eng.Fori(1, ITERS - 1) as it:
                body(it)
            body(ITERS - 1)

        def is_int(v, n):
            return type(v) is int and v == n

        block = ctx.enter_context(nc.Block())

        @block.sync
        def _(sp):
            sp.dma_start(xs[:], x[0].rearrange("(a p) n -> p a n", p=P)).then_inc(x_in, 16)

            def expert_read(layer, r, it=0):
                q = layer * PAIRS + r // 6
                if r % 6 < 4:
                    return up_done, it * (2 * UN) + (2 * q + 1 + r % 6 // 2)
                return down_done, it * (2 * UN) + (2 * q + 2)

            def read(c):
                if c >= MOE1:
                    return expert_read(1, c - MOE1)
                if c >= MIX1:
                    return ((kq_done, 2), (kq_done, 4), (kq_done, 6), (kq_done, 8), (av_done, 2), (av_done, 4),
                            (pr_done, 6), (pr_done, 8))[c - MIX1]
                if c >= MOE0:
                    return expert_read(0, c - MOE0)
                return ((f_done, 2), (f_done, 4), (q_done, 2), (q_done, 4), (vg_done, 2), (vg_done, 4), (vg_done, 6),
                        (vg_done, 8), (pr_done, 2), (pr_done, 4))[c]

            def load(c, dst, src):
                if c >= RING:
                    sp.wait_ge(*read(c - RING))
                sp.dma_start(dst, src).then_inc(loaded[c % RING], 16)

            def load_expert(layer, r, dst, src, it):
                c = MOE[layer] + r
                if type(it) is int and it == 0 and r < RING:
                    sp.wait_ge(*read(c - RING))
                else:
                    sp.wait_ge(*expert_read(layer, r - RING, it))
                sp.dma_start(dst, src).then_inc(loaded[c % RING], 16)

            def cols(w, j):
                return w[:, j * 512:(j + 1) * 512].rearrange("(k p) n -> p k n", p=P)

            for c, j in enumerate((2, 3, 0, 1, 4, 5, 6, 7)):
                load(MIX0 + c, up_view(c), cols(hg_w_in[0], j))
            for j in range(2):
                load(MIX0 + 8 + j, up_view(MIX0 + 8 + j), cols(hg_w_out[0], j))

            def expert_chunk(layer, j, e, copy, c):
                if j < 4:
                    copy(up_view(c), cols(moe_w_in[layer, e], j // 2))
                else:
                    copy(down_view(c), moe_w_out[layer, e].rearrange("(k p) n -> p k n", p=P))

            def experts(layer):
                def body(it):
                    for u in range(UN):
                        for j in range(6):
                            r = 6 * u + j
                            expert_chunk(layer, j, it * (2 * UN) + (2 * u + j % 2),
                                         lambda dst, src: load_expert(layer, r, dst, src, it), MOE[layer] + r)
                over_pairs(sp, body)
                over(layer)

            def over(layer):
                s = ov[layer]
                sp.wait_ge(nblk_ready, layer + 1)
                n = sp.value_load(nblk[0:1, layer:layer + 1], min_val=1, max_val=4)
                with sp.If(n > 1):
                    sp.wait_ge(down_done, 2 * (layer + 1) * PAIRS)
                    with sp.Fori(1, n) as b:
                        with sp.Fori(0, PAIRS) as q:
                            sp.wait_ge(s["x"], b * PAIRS + q - (PAIRS - 1))
                            for j in range(6):
                                expert_chunk(layer, j, q * 2 + j % 2,
                                             lambda dst, src: sp.dma_start(dst, src).then_inc(s["w"], 16), j)
                    sp.wait_ge(s["end"], 1)

            experts(0)
            c = MIX1
            for w, j in ((w_kv, 0), (w_kv, 1), (att_w_q[0], 0), (att_w_q[0], 1), (w_kv, 2), (w_kv, 3),
                         (att_w_o[0], 0), (att_w_o[0], 1)):
                load(c, up_view(c), cols(w, j))
                c += 1
            experts(1)
            for a in range(TT):
                sp.wait_ge(x_ready, a + 1)
                sp.dma_start(out[0, a * P:(a + 1) * P, :], xs[:, a, :]).then_inc(out_done, 16)
            sp.wait_ge(out_done, 16 * TT)
            sp.wait_ge(biasout, 16)

        @block.gpsimd
        def _(pool):
            pool.memset(ones[:], 1.0).then_inc(setup, 1)
            pool.memset(mhalf[:], -0.5).then_inc(setup, 1)
            pool.wait_ge(setup, 2)

            def root(i, n):
                pool.wait_ge(ms_ready, i)
                pool.tensor_tensor(rstd[:, 0:n], ms[:, 0:n], mhalf[:, 0:n], ALU.pow).then_inc(rstd_ready, 1)

            pool.memset(region(4), 0.0).then_inc(setup, 1)
            root(POW_MIX0, TT)
            pool.wait_ge(rb_ready, 1)
            pool.dma_start(bias_dram.rearrange("h (p n) -> h p n", p=P)[:, :, 0:NR],
                           brow.unsqueeze(1).to_broadcast([H, P, NR])).then_inc(biasout, 16)
            root(POW_O, TT * H)
            pool.wait_ge(o_done, 2)
            pool.dma_start(wrow, ffn_norm[0:1, :].to_broadcast([P, D])).then_inc(rowload, 16)
            root(POW_FFN0, TT)
            pool.wait_ge(biasout, 16)
            pool.wait_ge(og_ready, 2)
            pool.dma_start(bias, bass.AP(bias_dram.tensor, P - 1, [[NR, P], [P * (NR + 1), H], [1, T]])).then_inc(biasload, 16)
            root(POW_MIX1, TT)
            root(POW_K, TT * H)
            root(POW_Q, TT * H)
            for h in range(H):
                pool.wait_ge(ei_ready, h + 1)
                pool.tensor_scalar(prob[:, h, 0:P], prob[:, h, 0:P], einv[:, h, 0:1], None, ALU.mult)
                pool.tensor_scalar(prob[:, h, P:NR], prob[:, h, P:NR], einv[:, h, 1:2], None,
                                   ALU.mult).then_inc(pn_ready, 1)
            pool.wait_ge(pr_done, 8)
            pool.dma_start(wrow, ffn_norm[1:2, :].to_broadcast([P, D])).then_inc(rowload, 16)
            root(POW_FFN1, TT)

        @block.scalar
        def _(act):
            act.dma_start(ident[:], c_ident).then_inc(c_in, 16)
            act.dma_start(wcol[:, 0, :], mix_norm[0].rearrange("(k p) -> p k", p=P)).then_inc(w_in, 16)
            act.dma_start(lbl[:], hg_lb.rearrange("a (k p) -> p a k", p=P)).then_inc(w_in, 16)
            act.dma_start(masks_in, c_masks).then_inc(w_in, 16)
            act.dma_start(onorm[:], hg_o_norm[0:1, :].to_broadcast([P, P])).then_inc(w_in, 16)
            act.dma_start(wcol[:, 1, :], kv_norm.rearrange("(k p) -> p k", p=P)).then_inc(w_in, 16)
            act.dma_start(wcol[:, 2, :], mix_norm[1].rearrange("(k p) -> p k", p=P)).then_inc(w_in, 16)
            act.dma_start(kqcol[:, 0:1], k_norm.rearrange("(p a) -> p a", a=1)).then_inc(w_in, 16)
            act.dma_start(kqcol[:, 1:2], q_norm[0].rearrange("(p a) -> p a", a=1)).then_inc(w_in, 16)
            act.dma_start(before[:], c_before).then_inc(w_in, 16)
            act.dma_start(slot[:], c_slot).then_inc(w_in, 16)
            act.dma_start(prio[:], c_prio).then_inc(w_in, 16)
            for l in range(2):
                act.dma_start(wr[:, l, :, 0:NG], moe_w_group[l].rearrange("(k p) n -> p k n", p=P)).then_inc(w_in, 16)
                act.dma_start(wr[:, l, :, NG:], moe_w_expert[l].rearrange("(k p) n -> p k n", p=P)).then_inc(w_in, 16)
                act.dma_start(br[:, l, 0:NG], moe_b_group[l:l + 1, :].to_broadcast([P, NG])).then_inc(w_in, 16)
                act.dma_start(br[:, l, NG:], moe_b_expert[l:l + 1, :].to_broadcast([P, E])).then_inc(w_in, 16)
            act.dma_start(rbw, rel_bias).then_inc(w_in, 16)
            act.dma_start(bucket, c_bucket).then_inc(w_in, 16)
            act.dma_start(future, c_future).then_inc(w_in, 16)

            def transposed(stage, dsts):
                for b in (2, 3):
                    act.wait_ge(nt_done, 4 * stage + b + 1)
                    for dst, w in dsts:
                        src = ps[:, 4 + b, :].rearrange("p (k t) -> p k t", t=T)
                        if w is None:
                            act.copy(dst[:, 2 * b:2 * b + 2, :], src).then_inc(hT_act, 1)
                        else:
                            for j in range(2):
                                i = act.activation(dst[:, 2 * b + j, :], src[:, j, :], ACT.Copy,
                                                   scale=wcol[:, w, 2 * b + j:2 * b + j + 1])
                            i.then_inc(hT_act, 1)

            act.wait_ge(lb_in, 1)
            act.activation(lbw[:, 2:4, :], lbw[:, 0:2, :], ACT.Exp).then_inc(lb_exp, 1)
            act.wait_ge(w_in, SMALL)
            transposed(0, [(hT, 0)])
            for hp in range(4):
                act.wait_ge(f_done, hp + 1)
                act.activation(f_all[:, hp * 512:(hp + 1) * 512], ps[:, hp, :], ACT.Exp, scale=-1.0).then_inc(f_exp, 1)
            for hp in range(4):
                act.wait_ge(q_done, hp + 1)
                act.activation(qp_all[:, hp * 512:(hp + 1) * 512], ps[:, 4 + hp, :], ACT.Copy,
                               scale=QSCALE).then_inc(q_ready, 1)
            for i in range(4):
                act.wait_ge(vg_done, i + 1)
                act.copy(v_all[:, i % 2, (i // 2) * 512:(i // 2 + 1) * 512], ps[:, 4 + i, :]).then_inc(v_ready, 1)
            act.wait_ge(biasout, 16)
            for i in range(4):
                act.wait_ge(vg_done, 5 + i)
                act.activation(gate[:, i % 2, (i // 2) * 512:(i // 2 + 1) * 512], ps[:, 4 + i, :], ACT.Exp,
                               scale=-1.0).then_inc(g_exp, 1)
            act.wait_ge(lev_done, 9)
            act.wait_ge(upd_ready, 8)
            act.copy(scross, ps[:, 0:2, :].rearrange("p b (h t) -> p (b h) t", t=P)).then_inc(cross_ready, 1)
            for a in range(TT):
                act.wait_ge(o_done, a + 1)
                act.activation(osq[:, a, :], ps[:, 4 + 2 * a:6 + 2 * a, :].rearrange("p b n -> p (b n)"),
                               ACT.Square).then_inc(osq_done, 1)
            for b in (2, 3):
                act.wait_ge(ot_done, b + 1)
                act.copy(oT0[:, 2 * b:2 * b + 2, :], ps[:, b, :].rearrange("p (k t) -> p k t", t=T))\
                   .then_inc(oT_ready, 1)

            def over(layer):
                s = ov[layer]
                act.wait_ge(nblk_ready, layer + 1)
                n = act.value_load(nblk[0:1, layer:layer + 1], min_val=1, max_val=4)
                with act.If(n > 1):
                    with act.Fori(1, n) as b:
                        with act.Fori(0, PAIRS) as q:
                            v = b * PAIRS + q - (PAIRS - 1)
                            act.wait_ge(s["gat"], v)
                            act.copy(xgT[:, 0, 0:4, :], ps[:, 4, :].rearrange("p (k s) -> p k s", s=P))
                            act.copy(xgT[:, 0, 4:8, :], ps[:, 5, :].rearrange("p (k s) -> p k s", s=P))
                            act.copy(spread, ps[:, 0, 0:T]).then_inc(s["xg"], 1)
                            act.wait_ge(s["up"], v)
                            act.activation(en, ps[:, 6, :], ACT.Exp, scale=-1.0).then_inc(s["exp"], 1)
                            act.wait_ge(s["y"], v)
                            act.copy(y, ps[:, 6:8, :].rearrange("p b n -> p (b n)")).then_inc(s["ye"], 1)
                    act.wait_ge(s["end"], 1)

            def moe(layer):
                transposed(1 + 2 * layer, [(hrT, None)])
                act.wait_ge(gl_ready, layer + 1)
                act.activation(gex, gpr, ACT.Exp).then_inc(gl_exp, 1)
                act.wait_ge(el_ready, layer + 1)
                act.activation(e2, dd, ACT.Exp).then_inc(el_exp, 1)
                P0 = layer * PAIRS

                def gathered(it, u, half):
                    q = P0 + u
                    act.wait_ge(gat_done, it * (2 * UN) + (2 * q + half + 1))
                    if not (type(it) is int and it * UN + q < 2):
                        act.wait_ge(up_done, it * (2 * UN) + 2 * (q - 1))
                    act.copy(xgT[:, u % 2, 4 * half:4 * half + 4, :],
                             ps[:, 4, :].rearrange("p (k s) -> p k s", s=P)).then_inc(xg_ready, 1)

                def body(it):
                    for u in range(UN):
                        q = P0 + u
                        last = is_int(it, ITERS - 1) and u == UN - 1
                        act.wait_ge(up_done, it * (2 * UN) + (2 * q + 1))
                        if not (type(it) is int and it * UN + q < 1):
                            act.wait_ge(hid_ready, it * UN + q)
                        act.activation(en, ps[:, 6, :], ACT.Exp, scale=-1.0).then_inc(exp_done, 1)
                        if not last:
                            gathered(it, u + 1, 0)
                            gathered(it, u + 1, 1)
                        for half in range(2):
                            act.wait_ge(down_done, it * (2 * UN) + (2 * q + 1 + half))
                            if not (type(it) is int and it * UN + q < 1):
                                act.wait_ge(c_done, it * UN + q)
                            act.copy(y[:, half * 512:(half + 1) * 512], ps[:, 6 + half, :]).then_inc(y_ready, 1)

                gathered(0, 0, 0)
                gathered(0, 0, 1)
                over_pairs(act, body)
                over(layer)

            moe(0)

            transposed(2, [(hkvT, 1), (hqT, 2)])
            for i in range(8):
                dst = (kn, qn)[i // 4]
                half, a = (i % 4) // 2, i % 2
                act.wait_ge(kq_done, i + 1)
                act.activation(dst[:, a, half * 512:(half + 1) * 512], ps[:, (i // 4) * 4 + 2 * a + half, :],
                               ACT.Square).then_inc(sq_done, 1)

            def heads_T(i0, dst, w):
                for b in range(4):
                    act.wait_ge(tkq_done, i0 + b + 1)
                    act.activation(dst[:, 2 * b:2 * b + 2, :], ps[:, i0 + b, :].rearrange("p (k t) -> p k t", t=T),
                                   ACT.Copy, scale=kqcol[:, w:w + 1]).then_inc(kqT_ready, 1)

            def att_v(i):
                act.wait_ge(av_done, i + 1)
                act.copy(v_all[:, i % 2, (i // 2) * 512:(i // 2 + 1) * 512], ps[:, i, :]).then_inc(av_ready, 1)

            heads_T(0, kT, 0)
            att_v(0)
            att_v(1)
            heads_T(4, qT, 2)
            att_v(2)
            att_v(3)
            for h in range(H + 2):
                if h < H:
                    act.wait_ge(mx_ready, h + 1)
                    act.activation(prob[:, h, 0:P], prob[:, h, 0:P], ACT.Exp, bias=nmax[:, h, 0:1],
                                   accum_out=esum[:, h, 0:1])
                    act.activation(prob[:, h, P:NR], prob[:, h, P:NR], ACT.Exp, bias=nmax[:, h, 1:2],
                                   accum_out=esum[:, h, 1:2]).then_inc(ex_done, 1)
                if h >= 2:
                    act.wait_ge(pt_done, h - 1)
                    act.copy(probT[:, h - 2, :], ps[:, (h + 2) % 8, 0:NR]).then_inc(pT_ready, 1)
            for b in range(4):
                act.wait_ge(pv_done, b + 1)
                act.copy(oT1[:, 2 * b:2 * b + 2, :], ps[:, 4 + b, :].rearrange("p (k t) -> p k t", t=T))\
                   .then_inc(oT_ready, 1)
            moe(1)

        @block.vector
        def _(dve):
            steps = [0]

            def link(ins):
                steps[0] += 1
                ins.then_inc(dv, 1)
                dve.wait_ge(dv, steps[0])

            def rms(i, n, width):
                dve.tensor_scalar(ms[:, 0:n], ms[:, 0:n], 1.0 / width, EPS, ALU.mult, ALU.add).then_inc(ms_ready, 1)
                dve.wait_ge(rstd_ready, i)

            def sum_squares():
                for a in range(TT):
                    ins = dve.tensor_tensor_reduce(out=junk, in0=xs[:, a, :], in1=xs[:, a, :], scale=1.0, scalar=0.0,
                                                   op0=ALU.mult, op1=ALU.add, accum_out=ms[:, a:a + 1])
                    link(ins)

            def transposed(stage, dsts):
                for b in (0, 1):
                    dve.wait_ge(nt_done, 4 * stage + b + 1)
                    src = ps[:, 4 + b, :].rearrange("p (k t) -> p k t", t=T)
                    for dst, w in dsts:
                        if w is None:
                            dve.tensor_copy(dst[:, 2 * b:2 * b + 2, :], src).then_inc(hT_dve, 1)
                        else:
                            dve.tensor_tensor(dst[:, 2 * b:2 * b + 2, :], src,
                                              wcol[:, w, 2 * b:2 * b + 2].unsqueeze(2).to_broadcast([P, 2, T]),
                                              ALU.mult).then_inc(hT_dve, 1)

            def norm_plain(i):
                sum_squares()
                rms(i, TT, D)
                for a in range(TT):
                    dve.tensor_scalar(xn[:, a, :], xs[:, a, :], rstd[:, a:a + 1], None, ALU.mult).then_inc(xn_ready, 1)

            def add_projection(base, bank0):
                for i in range(4):
                    dve.wait_ge(pr_done, base + i + 1)
                    dst = xs[:, i % 2, (i // 2) * 512:(i // 2 + 1) * 512]
                    link(dve.tensor_tensor(dst, dst, ps[:, bank0 + i, :], ALU.add))

            dve.wait_ge(x_in, 16)
            norm_plain(POW_MIX0)
            dve.wait_ge(w_in, SMALL)
            link(dve.tensor_tensor(lbw[:, 4, :], lbl[:, 0, :], lbl[:, 1, :], ALU.max))
            dve.tensor_tensor(lbw[:, 0:2, :], lbl[:], lbw[:, 4:5, :].to_broadcast([P, 2, H]),
                              ALU.subtract).then_inc(lb_in, 1)
            dve.wait_ge(lb_exp, 1)
            link(dve.tensor_tensor(lbw[:, 4, :], lbw[:, 2, :], lbw[:, 3, :], ALU.add))
            link(dve.reciprocal(lbw[:, 4, :], lbw[:, 4, :]))
            link(dve.tensor_tensor(lbw[:, 0, :], lbw[:, 2, :], lbw[:, 4, :], ALU.mult))
            link(dve.tensor_scalar(lbw[:, 1, :], lbw[:, 0, :], -1.0, 1.0, ALU.mult, ALU.add))
            link(dve.tensor_copy(masks[:], masks_in))
            link(dve.tensor_scalar(kqcol[:, 2:3], kqcol[:, 1:2], QSCALE, None, ALU.mult))
            transposed(0, [(hT, 0)])
            for hp in range(4):
                sl = slice(hp * 512, (hp + 1) * 512)
                dve.wait_ge(f_exp, hp + 1)
                link(dve.tensor_scalar(f_all[:, sl], f_all[:, sl], 1.0, None, ALU.add))
                link(dve.reciprocal(f_all[:, sl], f_all[:, sl]))
                for h in (2 * hp, 2 * hp + 1):
                    hs = slice(h * T, (h + 1) * T)
                    i = dve.tensor_scalar(f_all[:, hs], f_all[:, hs], lbw[:, 1, h:h + 1], lbw[:, 0, h:h + 1],
                                          ALU.mult, ALU.add)
                link(i)
                dve.tensor_scalar(ks_all[:, sl], f_all[:, sl], -1.0, 1.0, ALU.mult, ALU.add).then_inc(k_ready, 1)

            dve.wait_ge(rb_done, 1)
            dve.tensor_tensor(brow, ps[0:H, 7, 0:NR], future, ALU.add).then_inc(rb_ready, 1)

            def level(l):
                dve.wait_ge(lev_done, l + 1)
                m = 1 << l >> 1
                if l == 0:
                    dve.tensor_tensor(qp_all, qp_all, f_all, ALU.mult).then_inc(upd_ready, 1)
                else:
                    t_now, t_next = (f_all, t_odd) if l % 2 else (t_odd, f_all)
                    tv = t_now[:, 0:2048 // m].rearrange("p (b two) -> p b two", two=2)
                    qv = qp_all.rearrange("p (b two m) -> p b two m", two=2, m=m)
                    kv = ks_all.rearrange("p (b two m) -> p b two m", two=2, m=m)
                    nb = 2048 // (2 * m)
                    dve.tensor_tensor(qv[:, :, 1, :], qv[:, :, 1, :],
                                      tv[:, :, 0].unsqueeze(2).to_broadcast([P, nb, m]), ALU.mult)
                    dve.tensor_tensor(kv[:, :, 0, :], kv[:, :, 0, :],
                                      tv[:, :, 1].unsqueeze(2).to_broadcast([P, nb, m]), ALU.mult)\
                       .then_inc(upd_ready, 1)
                    if l < LEVELS:
                        link(dve.tensor_tensor(t_next[:, 0:nb], tv[:, :, 0], tv[:, :, 1], ALU.mult))
                dve.copy_predicated(sdiag, masks[:, l:l + 1, :].to_broadcast([P, 2 * H, P]),
                                    ps[:, 0:4, :].rearrange("p b (h t) -> p (b h) t", t=P)).then_inc(pred_done, 1)
                dve.wait_ge(upd_ready, l + 1)
                dve.wait_ge(pred_done, l + 1)

            def silu_gate(i):
                gv = gate[:, i % 2, (i // 2) * 512:(i // 2 + 1) * 512]
                dve.wait_ge(g_exp, i + 1)
                link(dve.tensor_scalar(gv, gv, 1.0, None, ALU.add))
                link(dve.reciprocal(gv, gv))
                link(dve.tensor_tensor(gv, ps[:, 4 + i, :], gv, ALU.mult))
                g3 = gv.rearrange("p (h n) -> p h n", n=P)
                dve.tensor_tensor(g3, g3, onorm[:, :].unsqueeze(1).to_broadcast([P, 4, P]), ALU.mult)\
                   .then_inc(gate_ready, 1)

            dve.wait_ge(setup, 3)
            dve.wait_ge(q_ready, 4)
            dve.wait_ge(k_ready, 4)
            for l in range(LEVELS + 1):
                level(l)
                if l >= 4:
                    silu_gate(l - 4)
            for a in range(TT):
                dve.wait_ge(osq_done, a + 1)
                link(dve.tensor_reduce(ms[:, a * H:(a + 1) * H], osq[:, a, :].rearrange("p (h n) -> p h n", n=P),
                                       AX.X, ALU.add))
            rms(POW_O, TT * H, P)
            dve.wait_ge(gate_ready, 4)
            for a in range(TT):
                o3 = og[:, a, :].rearrange("p (h n) -> p h n", n=P)
                link(dve.tensor_tensor(o3, ps[:, 4 + 2 * a:6 + 2 * a, :].rearrange("p b (h n) -> p (b h) n", n=P),
                                       rstd[:, a * H:(a + 1) * H].unsqueeze(2).to_broadcast([P, H, P]), ALU.mult))
                dve.tensor_tensor(og[:, a, :], og[:, a, :], gate[:, a, :], ALU.mult).then_inc(og_ready, 1)
            for b in (0, 1):
                dve.wait_ge(ot_done, b + 1)
                dve.tensor_copy(oT0[:, 2 * b:2 * b + 2, :], ps[:, b, :].rearrange("p (k t) -> p k t", t=T))\
                   .then_inc(oT_ready, 1)
            add_projection(0, 4)

            def router(layer):
                dve.wait_ge(rt_done, layer + 1)
                link(dve.tensor_tensor(lg, ps[:, 3, 0:TT * (NG + E)].rearrange("p (a n) -> p a n", n=NG + E),
                                       br[:, layer:layer + 1, :].to_broadcast([P, TT, NG + E]), ALU.add))

                def b(v, n):
                    return v.unsqueeze(2).to_broadcast([P, TT, n])

                def one_hot(dst, tmp, v, mx, n):
                    link(dve.tensor_reduce(mx, v, AX.X, ALU.max))
                    link(dve.tensor_tensor(tmp, v, b(mx, n), ALU.is_equal))
                    link(dve.tensor_tensor(tmp, tmp, prio[:, 0:n].unsqueeze(1).to_broadcast([P, TT, n]), ALU.mult))
                    link(dve.tensor_reduce(ss, tmp, AX.X, ALU.max))
                    link(dve.tensor_tensor(dst, tmp, b(ss, n), ALU.is_equal))

                one_hot(goh, gpr, lg[:, :, 0:NG], gmx, NG)
                dve.tensor_tensor(gpr, lg[:, :, 0:NG], b(gmx, NG), ALU.subtract).then_inc(gl_ready, 1)
                link(dve.tensor_tensor(tmp32, lg[:, :, NG:].rearrange("p a (g e) -> p a g e", g=NG),
                                       goh.unsqueeze(3).to_broadcast([P, TT, NG, EG]), ALU.mult))
                link(dve.tensor_reduce(es, tmp32.rearrange("p a g e -> p a e g"), AX.X, ALU.add))
                one_hot(oh1, pr8, es, m1, EG)
                link(dve.scalar_tensor_tensor(es2, oh1, -3e38, es, ALU.mult, ALU.add))
                one_hot(oh2, pr8, es2, m2, EG)
                dve.tensor_tensor(dd, m2, m1, ALU.subtract).then_inc(el_ready, 1)
                link(dve.tensor_tensor(a8, oh1, oh2, ALU.add))
                dve.tensor_tensor(asg.rearrange("p a (g e) -> p a g e", g=NG), goh.unsqueeze(3)
                                  .to_broadcast([P, TT, NG, EG]), a8.unsqueeze(2).to_broadcast([P, TT, NG, EG]),
                                  ALU.mult).then_inc(asg_ready, 1)
                dve.wait_ge(gl_exp, layer + 1)
                link(dve.tensor_reduce(gsm, gex, AX.X, ALU.add))
                dve.wait_ge(el_exp, layer + 1)
                link(dve.tensor_scalar(w1, e2, 1.0, None, ALU.add))
                link(dve.tensor_tensor(w1, w1, gsm, ALU.mult))
                link(dve.reciprocal(w1, w1))
                link(dve.tensor_tensor(w2, w1, e2, ALU.mult))
                link(dve.tensor_tensor(oh1, oh1, b(w1, EG), ALU.mult))
                link(dve.tensor_tensor(oh2, oh2, b(w2, EG), ALU.mult))
                link(dve.tensor_tensor(wt8, oh1, oh2, ALU.add))
                link(dve.tensor_tensor(tmp32, goh.unsqueeze(3).to_broadcast([P, TT, NG, EG]),
                                       wt8.unsqueeze(2).to_broadcast([P, TT, NG, EG]), ALU.mult))
                t3 = tmp32.rearrange("p a g e -> p a (g e)")
                for a in range(TT):
                    i = dve.tensor_copy(wgt[:, :, a, :], t3[:, a, :].rearrange("p (q e) -> p q e", e=2))
                dve.wait_ge(pos_done, layer + 1)
                link(dve.scalar_tensor_tensor(tpos, ps[:, 2, 0:TT * E].rearrange("p (a e) -> p a e", e=E), 1.0, asg,
                                              ALU.add, ALU.mult))
                for a in range(TT):
                    i = dve.tensor_scalar(pos[:, :, a, :], tpos[:, a, :].rearrange("p (q e) -> p q e", e=2), -1.0,
                                          None, ALU.add)
                link(i)
                link(dve.tensor_reduce(cmx, ps[:, 2, TT * E:TT * E + E], AX.X, ALU.max))
                for j in range(1, 4):
                    i = dve.tensor_scalar(nblf[:, j:j + 1], cmx, float(j * CAP), None, ALU.is_gt)
                link(i)
                link(dve.tensor_reduce(nblf[:, 0:1], nblf[:, 1:4], AX.X, ALU.add))
                dve.tensor_scalar(nblk[:, layer:layer + 1], nblf[:, 0:1], 1.0, None, ALU.add).then_inc(nblk_ready, 1)

            def over(layer):
                s = ov[layer]
                dve.wait_ge(nblk_ready, layer + 1)
                n = dve.value_load(nblk[0:1, layer:layer + 1], min_val=1, max_val=4)
                with dve.If(n > 1):
                    dve.memset(mark[:, 2:3], 0.0).then_inc(s["x"], 1)
                    with dve.Fori(1, n) as b:
                        dve.tensor_scalar(pos, pos, -float(CAP), None, ALU.add).then_inc(s["shift"], 1)
                        dve.wait_ge(s["shift"], b)
                        dve.memset(mark[:, 4:5], 0.0)
                        with dve.Fori(0, PAIRS) as q:
                            v = b * PAIRS + q - (PAIRS - 1)
                            dve.wait_ge(s["x"], v)
                            build_pick(q, s["picked"])
                            dve.wait_ge(s["picked"], v)
                            dve.tensor_tensor(pickw, pick, wgt[:, q].unsqueeze(3).to_broadcast([P, TT, 2, BLK]),
                                              ALU.mult).then_inc(s["pick"], 1)
                            dve.wait_ge(s["exp"], v)
                            dve.tensor_scalar(en, en, 1.0, None, ALU.add).then_inc(s["den"], 1)
                            dve.wait_ge(s["den"], v)
                            dve.reciprocal(en, en).then_inc(s["rec"], 1)
                            dve.wait_ge(s["rec"], v)
                            dve.tensor_tensor(en, en, ps[:, 6, :], ALU.mult).then_inc(s["sil"], 1)
                            dve.wait_ge(s["sil"], v)
                            dve.tensor_tensor(hid, en, ps[:, 7, :], ALU.mult).then_inc(s["hid"], 1)
                            dve.wait_ge(s["ht"], v)
                            dve.tensor_copy(hidT, ps[:, 1, :].rearrange("p (k s) -> p k s", s=P))\
                               .then_inc(s["hidT"], 1)
                            dve.wait_ge(s["c"], v)
                            for a in range(TT):
                                i = dve.tensor_tensor(xs[:, a, :], xs[:, a, :],
                                                      ps[:, 2 * a:2 * a + 2, :].rearrange("p b n -> p (b n)"),
                                                      ALU.add)
                            i.then_inc(s["x"], 1)
                    dve.memset(mark[:, 3:4], 0.0).then_inc(s["end"], 1)
                    dve.wait_ge(s["end"], 1)

            def build_pick(q, signal):
                ins = dve.tensor_tensor(pick, pos[:, q].unsqueeze(3).to_broadcast([P, TT, 2, BLK]),
                                        slot[:, :].unsqueeze(1).unsqueeze(1).to_broadcast([P, TT, 2, BLK]),
                                        ALU.is_equal)
                ins.then_inc(signal, 1)

            def moe(layer):
                st = 1 + 2 * layer
                sum_squares()
                rms((POW_FFN0, POW_FFN1)[layer], TT, D)
                dve.wait_ge(rowload, 16 * (layer + 1))
                for a in range(TT):
                    dve.scalar_tensor_tensor(hn[:, a, :], xs[:, a, :], rstd[:, a:a + 1], wrow, ALU.mult,
                                             ALU.mult).then_inc(xn_ready, 1)
                transposed(st, [(hrT, None)])
                router(layer)
                P0 = layer * PAIRS

                def silu(it, u):
                    q = P0 + u
                    dve.wait_ge(exp_done, it * UN + (q + 1))
                    dve.tensor_scalar(en, en, 1.0, None, ALU.add).then_inc(den_ready, 1)
                    dve.wait_ge(den_ready, it * UN + (q + 1))
                    dve.reciprocal(en, en).then_inc(sig_ready, 1)
                    dve.wait_ge(sig_ready, it * UN + (q + 1))
                    dve.tensor_tensor(en, en, ps[:, 6, :], ALU.mult).then_inc(silu_ready, 1)
                    dve.wait_ge(silu_ready, it * UN + (q + 1))
                    dve.wait_ge(up_done, it * (2 * UN) + (2 * q + 2))
                    if not (type(it) is int and it * UN + q < 1):
                        dve.wait_ge(ht_done, it * UN + q)
                    dve.tensor_tensor(hid, en, ps[:, 7, :], ALU.mult).then_inc(hid_ready, 1)
                    dve.wait_ge(ht_done, it * UN + (q + 1))
                    if not (type(it) is int and it * UN + q < 1):
                        dve.wait_ge(down_done, it * (2 * UN) + 2 * q)
                    dve.tensor_copy(hidT, ps[:, 5, :].rearrange("p (k s) -> p k s", s=P)).then_inc(hidT_ready, 1)

                def spread_out(it, u):
                    q = P0 + u
                    dve.wait_ge(st_done, it * UN + (q + 1))
                    if not (type(it) is int and it * UN + q < 1):
                        dve.wait_ge(c_done, it * UN + q)
                    dve.tensor_copy(spread, ps[:, 5, 0:T]).then_inc(s_ready, 1)

                def pick_for(it, u):
                    q = P0 + u
                    if not (type(it) is int and it * UN + q < 1):
                        dve.wait_ge(gat_done, it * (2 * UN) + 2 * q)
                        dve.wait_ge(pickw_ready, it * UN + q)
                    build_pick(it * UN + u, pick_ready)

                def weigh(it, u):
                    q = P0 + u
                    dve.wait_ge(pick_ready, it * UN + (q + 1))
                    if not (type(it) is int and it * UN + q < 1):
                        dve.wait_ge(st_done, it * UN + q)
                    dve.tensor_tensor(pickw, pick, wgt[:, it * UN + u].unsqueeze(3).to_broadcast([P, TT, 2, BLK]),
                                      ALU.mult).then_inc(pickw_ready, 1)

                pick_for(0, 0)

                def body(it):
                    for u in range(UN):
                        last = is_int(it, ITERS - 1) and u == UN - 1
                        weigh(it, u)
                        if not last:
                            pick_for(it, u + 1)
                        silu(it, u)
                        spread_out(it, u)

                over_pairs(dve, body)
                dve.wait_ge(c_done, P0 + PAIRS)
                for a in range(TT):
                    link(dve.tensor_tensor(xs[:, a, :], xs[:, a, :],
                                           ps[:, 2 * a:2 * a + 2, :].rearrange("p b n -> p (b n)"), ALU.add))
                over(layer)

            moe(0)

            norm_plain(POW_MIX1)
            transposed(2, [(hkvT, 1), (hqT, 2)])

            def head_norm(i0, dst, i):
                for j in range(4):
                    half, a = j // 2, j % 2
                    dve.wait_ge(sq_done, i0 + j + 1)
                    link(dve.tensor_reduce(ms[:, a * H + half * 4:a * H + half * 4 + 4],
                                           dst[:, a, half * 512:(half + 1) * 512]
                                           .rearrange("p (h n) -> p h n", n=P), AX.X, ALU.add))
                rms(i, TT * H, P)
                for a in range(TT):
                    dve.tensor_tensor(dst[:, a, :].rearrange("p (h n) -> p h n", n=P),
                                      ps[:, i0 + 2 * a:i0 + 2 * a + 2, :].rearrange("p b (h n) -> p (b h) n", n=P),
                                      rstd[:, a * H:(a + 1) * H].unsqueeze(2).to_broadcast([P, H, P]),
                                      ALU.mult).then_inc(kqn_ready, 1)

            head_norm(0, kn, POW_K)
            head_norm(4, qn, POW_Q)
            dve.wait_ge(biasload, 16)
            for h in range(H + 1):
                if h < H:
                    bank = (4 + h) % 8
                    dve.wait_ge(sc_done, h + 1)
                    dve.tensor_tensor(prob[:, h, 0:P], ps[:, bank, 0:P], bias[:, h, P:T], ALU.add)
                    link(dve.tensor_tensor(prob[:, h, P:NR], ps[:, bank, P:NR], bias[:, h, :], ALU.add))
                    dve.tensor_reduce(nmax[:, h, 0:1], prob[:, h, 0:P], AX.X, ALU.max, negate=True)
                    dve.tensor_reduce(nmax[:, h, 1:2], prob[:, h, P:NR], AX.X, ALU.max, negate=True)\
                       .then_inc(mx_ready, 1)
                if h >= 1:
                    dve.wait_ge(ex_done, h)
                    dve.reciprocal(einv[:, h - 1, :], esum[:, h - 1, :]).then_inc(ei_ready, 1)
            add_projection(4, 0)
            moe(1)
            for a in range(TT):
                dve.memset(mark[:, a:a + 1], 0.0).then_inc(x_ready, 1)

        @block.tensor
        def _(pe):
            def mm(o, l, r, start=True, stop=True):
                return pe.matmul(o, l, r, start=start, stop=stop)

            def tr(o, i):
                return pe.transpose(o, i, ident[:])

            def arrived(c, it=0):
                pe.wait_ge(loaded[c % RING], it * (16 * TURNS) + 16 * (c // RING + 1))

            def transposes(stage, src):
                for a in range(TT):
                    pe.wait_ge(xn_ready, TT * stage + a + 1)
                    for k in range(KD):
                        i = tr(ps[:, 4 + k // 2, (k % 2) * T + a * P:(k % 2) * T + (a + 1) * P],
                               src[:, a, k * P:(k + 1) * P])
                        if a == TT - 1 and k % 2:
                            i.then_inc(nt_done, 1)

            def project(c, lhs, bank, a, signal):
                arrived(c)
                for k in range(KD):
                    i = mm(ps[:, bank, :], lhs[:, k, a * P:(a + 1) * P], up_view(c)[:, k, :], k == 0, k == KD - 1)
                i.then_inc(signal, 1)

            pe.wait_ge(c_in, 16)
            transposes(0, xn)
            pe.wait_ge(hT_dve, 2)
            pe.wait_ge(hT_act, 2)
            for j, (signal, bank0) in enumerate(((f_done, 0), (q_done, 4))):
                for hp in range(4):
                    c = MIX0 + 2 * j + hp // 2
                    arrived(c)
                    if j == 1 and hp == 3:
                        pe.wait_ge(rb_ready, 1)
                    for h in (2 * hp, 2 * hp + 1):
                        for k in range(KD):
                            i = mm(ps[:, bank0 + hp, (h % 2) * T:(h % 2 + 1) * T],
                                   up_view(c)[:, k, (h % 4) * P:(h % 4 + 1) * P], hT[:, k, :], k == 0, k == KD - 1)
                    i.then_inc(signal, 1)
                if j == 0:
                    pe.wait_ge(w_in, SMALL)
                    mm(ps[0:H, 7, 0:NR], rbw, bucket).then_inc(rb_done, 1)

            q3 = qp_all.rearrange("p (h t) -> p h t", t=T)
            k3 = ks_all.rearrange("p (h t) -> p h t", t=T)
            pe.wait_ge(k_ready, 4)
            pe.wait_ge(q_ready, 4)
            for l in range(LEVELS + 1):
                if l:
                    pe.wait_ge(upd_ready, l)
                    pe.wait_ge(pred_done, l)
                for h in range(H):
                    for a in range(TT):
                        b = 2 * h + a
                        i = mm(ps[:, b // 4, (b % 4) * P:(b % 4 + 1) * P], k3[:, h, a * P:(a + 1) * P],
                               q3[:, h, a * P:(a + 1) * P])
                i.then_inc(lev_done, 1)
                if l >= 4:
                    pe.wait_ge(v_ready, l - 3)
                project(MIX0 + 4 + l // 2, hT, 4 + l % 4, l % 2, vg_done)
            pe.wait_ge(upd_ready, LEVELS + 1)
            pe.wait_ge(pred_done, LEVELS + 1)
            for h in range(H):
                i = mm(ps[:, h // 4, (h % 4) * P:(h % 4 + 1) * P], k3[:, h, 0:P], q3[:, h, P:T])
            i.then_inc(lev_done, 1)
            pe.wait_ge(gate_ready, 4)
            pe.wait_ge(v_ready, 4)
            for a in range(TT):
                if a:
                    pe.wait_ge(cross_ready, 1)
                for h in range(H):
                    o = ps[:, 4 + 2 * a + h // 4, (h % 4) * P:(h % 4 + 1) * P]
                    if a:
                        mm(o, scross[:, h, :], v_all[:, 0, h * P:(h + 1) * P], True, False)
                    i = mm(o, sdiag[:, 2 * h + a, :], v_all[:, a, h * P:(h + 1) * P], a == 0, True)
                i.then_inc(o_done, 1)
            for a in range(TT):
                pe.wait_ge(og_ready, a + 1)
                for k in range(KD):
                    i = tr(ps[:, k // 2, (k % 2) * T + a * P:(k % 2) * T + (a + 1) * P], og[:, a, k * P:(k + 1) * P])
                    if a == TT - 1 and k % 2:
                        i.then_inc(ot_done, 1)
            pe.wait_ge(oT_ready, 4)
            for i in range(4):
                project(MIX0 + 8 + i // 2, oT0, 4 + i, i % 2, pr_done)

            def gather(q, bank, half, signal):
                for k in range(4):
                    for a in range(TT):
                        i = mm(ps[:, bank, k * P:(k + 1) * P], hn[:, a, (4 * half + k) * P:(4 * half + k + 1) * P],
                               pick[:, a].rearrange("p e s -> p (e s)"), a == 0, a == TT - 1)
                if signal is not None:
                    i.then_inc(signal, 1)
                return i

            def up(c, bank, buf, signal):
                for k in range(KD):
                    for x2 in range(2):
                        rows = slice(x2 * BLK, (x2 + 1) * BLK)
                        i = mm(ps[rows, bank, :], xgT[:, buf, k, rows], up_view(c + x2)[:, k, :], k == 0, k == KD - 1)
                if signal is not None:
                    i.then_inc(signal, 1)

            def hidden_T(bank, signal):
                for k in range(KF):
                    i = tr(ps[:, bank, k * P:(k + 1) * P], hid[:, k * P:(k + 1) * P])
                i.then_inc(signal, 1)

            def down(c, half, signal):
                for k in range(KF):
                    for x2 in range(2):
                        rows = slice(x2 * BLK, (x2 + 1) * BLK)
                        i = mm(ps[rows, 6 + half, :], hidT[:, k, rows],
                               down_view(c + x2)[:, k, half * 512:(half + 1) * 512], k == 0, k == KF - 1)
                if signal is not None:
                    i.then_inc(signal, 1)

            def spread_T(bank, signal):
                for a in range(TT):
                    i = tr(ps[:, bank, a * P:(a + 1) * P], pickw[:, a].rearrange("p e s -> p (e s)"))
                if signal is not None:
                    i.then_inc(signal, 1)

            def over(layer):
                s = ov[layer]
                pe.wait_ge(nblk_ready, layer + 1)
                n = pe.value_load(nblk[0:1, layer:layer + 1], min_val=1, max_val=4)
                with pe.If(n > 1):
                    with pe.Fori(1, n) as b:
                        with pe.Fori(0, PAIRS) as q:
                            v = b * PAIRS + q - (PAIRS - 1)
                            pe.wait_ge(s["pick"], v)
                            gather(q, 4, 0, None)
                            gather(q, 5, 1, None)
                            spread_T(0, s["gat"])
                            pe.wait_ge(s["xg"], v)
                            pe.wait_ge(s["w"], v * (16 * 6))
                            up(0, 6, 0, None)
                            up(2, 7, 0, s["up"])
                            pe.wait_ge(s["hid"], v)
                            hidden_T(1, s["ht"])
                            pe.wait_ge(s["hidT"], v)
                            down(4, 0, None)
                            down(4, 1, s["y"])
                            pe.wait_ge(s["ye"], v)
                            for a in range(TT):
                                for half in range(2):
                                    i = mm(ps[:, 2 * a + half, :], spread[:, a * P:(a + 1) * P],
                                           y[:, half * 512:(half + 1) * 512])
                            i.then_inc(s["c"], 1)
                    pe.wait_ge(s["end"], 1)

            def moe(layer):
                transposes(1 + 2 * layer, hn)
                pe.wait_ge(hT_dve, (4, 10)[layer])
                pe.wait_ge(hT_act, (4, 10)[layer])
                for a in range(TT):
                    for k in range(KD):
                        i = mm(ps[:, 3, a * (NG + E):(a + 1) * (NG + E)], hrT[:, k, a * P:(a + 1) * P],
                               wr[:, layer, k, :], k == 0, k == KD - 1)
                i.then_inc(rt_done, 1)
                pe.wait_ge(asg_ready, layer + 1)
                mm(ps[:, 2, 0:E], before[:], asg[:, 0, :])
                mm(ps[:, 2, E:2 * E], ones[:], asg[:, 0, :], True, False)
                mm(ps[:, 2, E:2 * E], before[:], asg[:, 1, :], False, True)
                mm(ps[:, 2, 2 * E:3 * E], ones[:], asg[:, 0, :], True, False)
                mm(ps[:, 2, 2 * E:3 * E], ones[:], asg[:, 1, :], False, True).then_inc(pos_done, 1)
                P0 = layer * PAIRS

                def gather_next(it, u, half):
                    q = P0 + u
                    if half == 0:
                        pe.wait_ge(pick_ready, it * UN + (q + 1))
                    if not (type(it) is int and it * UN + q < 1 and half == 0):
                        pe.wait_ge(xg_ready, it * (2 * UN) + (2 * q + half))
                    gather(None, 4, half, gat_done)

                gather_next(0, 0, 0)
                gather_next(0, 0, 1)

                def body(it):
                    for u in range(UN):
                        last = is_int(it, ITERS - 1) and u == UN - 1
                        q = P0 + u
                        c0 = MOE[layer] + 6 * u
                        n0 = type(it) is int and it * UN + q < 1
                        pe.wait_ge(xg_ready, it * (2 * UN) + (2 * q + 2))
                        for half in range(2):
                            arrived(c0 + 2 * half, it)
                            arrived(c0 + 2 * half + 1, it)
                            if not n0:
                                pe.wait_ge(y_ready, it * (2 * UN) + (2 * q - 1 + half))
                            up(c0 + 2 * half, 6 + half, u % 2, up_done)
                        if not last:
                            gather_next(it, u + 1, 0)
                        pe.wait_ge(hid_ready, it * UN + (q + 1))
                        if not n0:
                            pe.wait_ge(s_ready, it * UN + q)
                        hidden_T(5, ht_done)
                        if not last:
                            gather_next(it, u + 1, 1)
                        pe.wait_ge(hidT_ready, it * UN + (q + 1))
                        arrived(c0 + 4, it)
                        arrived(c0 + 5, it)
                        down(c0 + 4, 0, down_done)
                        down(c0 + 4, 1, down_done)
                        pe.wait_ge(pickw_ready, it * UN + (q + 1))
                        spread_T(5, st_done)
                        pe.wait_ge(s_ready, it * UN + (q + 1))
                        for half in range(2):
                            pe.wait_ge(y_ready, it * (2 * UN) + (2 * q + 1 + half))
                            for a in range(TT):
                                i = mm(ps[:, 2 * a + half, :], spread[:, a * P:(a + 1) * P],
                                       y[:, half * 512:(half + 1) * 512], is_int(it, 0) and u == 0, last)
                        i.then_inc(c_done, 1)

                over_pairs(pe, body)
                over(layer)

            moe(0)

            transposes(2, xn)
            pe.wait_ge(hT_dve, 8)
            pe.wait_ge(hT_act, 8)
            for i in range(4):
                project(MIX1 + i // 2, hkvT, 2 * (i % 2) + i // 2, i % 2, kq_done)
            for i in range(4):
                project(MIX1 + 2 + i // 2, hqT, 4 + 2 * (i % 2) + i // 2, i % 2, kq_done)

            def heads_transposes(src, bank0, n0):
                for a in range(TT):
                    pe.wait_ge(kqn_ready, n0 + a + 1)
                    if a == 0:
                        pe.wait_ge(kqn_ready, n0 + 2)
                    for h in range(H):
                        i = tr(ps[:, bank0 + h // 2, (h % 2) * T + a * P:(h % 2) * T + (a + 1) * P],
                               src[:, a, h * P:(h + 1) * P])
                        if a and h % 2:
                            i.then_inc(tkq_done, 1)

            def att_v(i):
                pe.wait_ge(kqT_ready, i + 1)
                project(MIX1 + 4 + i // 2, hkvT, i, i % 2, av_done)

            heads_transposes(kn, 0, 0)
            att_v(0)
            att_v(1)
            heads_transposes(qn, 4, 2)
            att_v(2)
            att_v(3)
            pe.wait_ge(kqT_ready, 8)
            for h in range(H):
                if h == 4:
                    pe.wait_ge(av_ready, 4)
                bank = (4 + h) % 8
                mm(ps[:, bank, 0:P], qT[:, h, 0:P], kT[:, h, 0:P])
                mm(ps[:, bank, P:NR], qT[:, h, P:T], kT[:, h, :]).then_inc(sc_done, 1)
            for h in range(H):
                pe.wait_ge(pn_ready, h + 1)
                for j in range(3):
                    i = tr(ps[:, (4 + h) % 8, j * P:(j + 1) * P], prob[:, h, j * P:(j + 1) * P])
                i.then_inc(pt_done, 1)
            for b in range(4):
                pe.wait_ge(pT_ready, 2 * b + 2)
                for h in (2 * b, 2 * b + 1):
                    o = (h % 2) * T
                    mm(ps[:, 4 + b, o:o + T], v_all[:, 0, h * P:(h + 1) * P], probT[:, h, 0:T], True, False)
                    i = mm(ps[:, 4 + b, o + P:o + T], v_all[:, 1, h * P:(h + 1) * P], probT[:, h, T:NR], False, True)
                i.then_inc(pv_done, 1)
            pe.wait_ge(oT_ready, 8)
            pe.wait_ge(pT_ready, 8)
            for i in range(4):
                project(MIX1 + 6 + i // 2, oT1, i, i % 2, pr_done)
            moe(1)


SMALL = 16 * 22

_INS = ['x', 'mix_norm', 'ffn_norm', 'hg_w_in', 'hg_lb', 'hg_o_norm', 'hg_w_out', 'kv_norm', 'w_kv', 'k_norm',
        'att_w_q', 'q_norm', 'att_w_o', 'rel_bias', 'moe_w_group', 'moe_b_group', 'moe_w_expert', 'moe_b_expert',
        'moe_w_in', 'moe_w_out']


def constants():
    import math
    import numpy as np
    i = np.arange(P)
    masks = np.zeros((P, LEVELS + 1, P), np.float32)
    masks[i, 0, i] = 1
    for l in range(1, LEVELS + 1):
        m = 1 << (l - 1)
        masks[:, l, :] = ((i[:, None] // (2 * m) == i[None, :] // (2 * m)) & (i[:, None] // m % 2 == 0)
                          & (i[None, :] // m % 2 == 1))
    places = np.arange(BLK, dtype=np.float32)
    places[CAP:] = -1000.0
    dist = T - 1 - np.arange(NR)
    n = np.maximum(dist, 0)
    ratio = np.log(np.maximum(n, 16).astype(np.float32) / np.float32(16)) / np.float32(math.log(1024 / 16))
    buckets = np.where(n < 16, n, np.minimum(16 + (ratio * np.float32(16)).astype(np.int32), 31))
    return {
        "ident": np.eye(P, dtype=np.float32),
        "before": (i[:, None] < i[None, :]).astype(np.float32),
        "masks": masks,
        "slot": np.ascontiguousarray(np.broadcast_to(places, (P, BLK))),
        "prio": np.ascontiguousarray(np.broadcast_to(np.arange(EG, 0, -1, dtype=np.float32), (P, EG))),
        "bucket": (buckets[None, :] == np.arange(32)[:, None]).astype(np.float32),
        "future": np.ascontiguousarray(np.broadcast_to(np.where(dist < 0, -1e30, 0.0).astype(np.float32), (H, NR))),
    }


def kernel(**inputs):
    import numpy as _np
    import concourse.bacc as _bacc
    from concourse.bass_utils import run_bass_kernel_spmd as _run

    nc = _bacc.Bacc("TRN2", target_bir_lowering=False, num_devices=1)
    arrays, args = {}, []

    def give(name, a):
        arrays[name] = a
        args.append(nc.dram_tensor(name, a.shape, mybir.dt.from_np(a.dtype), kind="ExternalInput").ap())

    for name in _INS:
        give(f"in_{name}", _np.ascontiguousarray(inputs[name]))
    for name, a in constants().items():
        give(f"const_{name}", a)
    args.append(nc.dram_tensor("out_0", (1, T, D), FP32, kind="ExternalOutput").ap())
    build(nc, *args)
    r = _run(nc, [arrays], core_ids=[0])
    return r.results[0]["out_0"]
```

```python
import concourse.bass as bass
from concourse import mybir
from contextlib import ExitStack

FP32 = mybir.dt.float32
I32 = mybir.dt.int32
U8 = mybir.dt.uint8
ALU = mybir.AluOpType
ACT = mybir.ActivationFunctionType
AX = mybir.AxisListType

P = 128
T = 256
TT = T // P
D = 1024
KD = D // P
H = 8
LEVELS = 7
NG, EG = 4, 8
E = NG * EG
FF = 512
KF = FF // P
EPS = 1e-6
QSCALE = float(P) ** -0.5

BLK = 64
CAP = 64
PAIRS = E // 2
RING = 8
UN = 4
ITERS = PAIRS // UN
TURNS = 6 * UN // RING
MIX0, MOE0 = 0, 10
MIX1 = MOE0 + 6 * PAIRS - 2
MOE1 = MIX1 + 8
MOE = [MOE0, MOE1]
NR = 3 * P

XR = 16

(POW_MIX0, _, POW_O, _, _, _, POW_FFN0, _, POW_MIX1, _, POW_K, POW_Q, POW_FFN1, _) = range(1, 15)


def build(nc, x, mix_norm, ffn_norm, hg_w_in, hg_lb, hg_o_norm, hg_w_out, kv_norm, w_kv, k_norm,
          att_w_q, q_norm, att_w_o, rel_bias, moe_w_group, moe_b_group, moe_w_expert, moe_b_expert,
          moe_w_in, moe_w_out, c_ident, c_before, c_masks, c_slot, c_prio, c_bucket, c_future, out):
    with ExitStack() as ctx:
        def sb(name, shape, dt=FP32):
            return ctx.enter_context(nc.sbuf_tensor(name, shape, dt))

        def sem(name):
            return ctx.enter_context(nc.semaphore(name))

        ctx.enter_context(nc.allow_non_contiguous_dma(reason="small vectors spread over partitions"))
        ps = ctx.enter_context(nc.psum_tensor("ps", [P, 8, 512], FP32))
        bias_dram = nc.dram_tensor("bias_scratch", (H, P * (NR + 1)), FP32, kind="Internal").ap()

        ring = sb("ring", [P, RING, 4096])
        xs = sb("xs", [P, TT, D])
        ident = sb("ident", [P, P])
        before = sb("before", [P, P])
        ones = sb("ones", [P, P])
        masks = sb("masks", [P, LEVELS + 1, P], U8)
        slot = sb("slot", [P, BLK])
        prio = sb("prio", [P, EG])
        wcol = sb("wcol", [P, 5, KD])
        lbl = sb("lbl", [P, 2, H])
        lbw = sb("lbw", [P, 6, H])
        onorm = sb("onorm", [P, P])
        kqcol = sb("kqcol", [P, 3])
        wr = sb("wr", [P, 2, KD, NG + E])
        br = sb("br", [P, 2, NG + E])
        ms = sb("ms", [P, 18])
        rstd = sb("rstd", [P, 18])
        mhalf = sb("mhalf", [P, 18])
        nmax = sb("nmax", [P, H, 2])
        esum = sb("esum", [P, H, 2])
        einv = sb("einv", [P, H, 2])
        nblk = sb("nblk", [P, 2], I32)
        nblf = sb("nblf", [P, 4])
        mark = sb("mark", [P, 8])

        work = sb("work", [P, 8, 2048])

        def region(i, k=1):
            return work[:, i:i + k, :].rearrange("p r n -> p (r n)")

        hT = region(0).rearrange("p (k t) -> p k t", t=T)
        f_all = region(1)
        ks_all = region(2)
        qp_all = region(3)
        sdiag = region(4).rearrange("p (b t) -> p b t", t=P)
        scross = region(5)[:, 0:1024].rearrange("p (h t) -> p h t", t=P)
        t_odd = region(5)[:, 1024:2048]
        v_all = region(6).rearrange("p (a n) -> p a n", n=D)
        gate = region(7).rearrange("p (a n) -> p a n", n=D)
        xn = region(5).rearrange("p (a n) -> p a n", n=D)
        osq = region(0).rearrange("p (a n) -> p a n", n=D)
        og = region(1).rearrange("p (a n) -> p a n", n=D)
        oT = region(5).rearrange("p (k t) -> p k t", t=T)
        hkvT = hT
        hqT = region(1).rearrange("p (k t) -> p k t", t=T)
        kn = region(2).rearrange("p (a n) -> p a n", n=D)
        qn = region(3).rearrange("p (a n) -> p a n", n=D)
        kT = region(4).rearrange("p (h t) -> p h t", t=T)
        qT = region(5).rearrange("p (h t) -> p h t", t=T)
        bias = region(7).rearrange("p (h s) -> p h s", s=T)
        prob = region(2, 2)[:, 0:H * NR].rearrange("p (h s) -> p h s", s=NR)
        probT = region(0, 2)[:, 0:H * NR].rearrange("p (h s) -> p h s", s=NR)
        hn = region(0).rearrange("p (a n) -> p a n", n=D)
        hrT = region(1).rearrange("p (k t) -> p k t", t=T)
        xgT = region(2).rearrange("p (b k s) -> p b k s", b=2, s=P)
        y = region(1)[:, 0:1024]
        en = region(1)[:, 1024:1536]
        hid = region(1)[:, 1536:2048]
        hidT = region(5)[:, 1408:1920].rearrange("p (k s) -> p k s", s=P)
        pick = region(5)[:, 640:896].rearrange("p (a e s) -> p a e s", a=TT, s=BLK)
        pickw = region(5)[:, 896:1152].rearrange("p (a e s) -> p a e s", a=TT, s=BLK)
        spread = region(5)[:, 1152:1408]
        rt = region(5)
        lg = rt[:, 0:72].rearrange("p (a n) -> p a n", n=NG + E)
        gmx, gsm, m1, m2, dd, e2, ss, w1, w2 = (rt[:, 72 + 2 * i:74 + 2 * i] for i in range(9))
        goh, gpr, gex = (rt[:, 100 + 8 * i:108 + 8 * i].rearrange("p (a g) -> p a g", g=NG) for i in range(3))
        es, oh1, oh2, pr8, wt8, a8, es2 = (rt[:, 128 + 16 * i:144 + 16 * i].rearrange("p (a g) -> p a g", g=EG)
                                           for i in range(7))
        tmp32 = rt[:, 256:320].rearrange("p (a g e) -> p a g e", a=TT, g=NG)
        asg = rt[:, 320:384].rearrange("p (a e) -> p a e", a=TT)
        wgt = rt[:, 384:448].rearrange("p (q a e) -> p q a e", a=TT, e=2)
        pos = rt[:, 448:512].rearrange("p (q a e) -> p q a e", a=TT, e=2)
        tpos = rt[:, 512:576].rearrange("p (a e) -> p a e", a=TT)
        cmx = rt[:, 576:577]
        rbw = region(6)[0:32, 1024:1032]
        bucket = region(6)[0:32, 1040:1040 + NR]
        future = region(6)[0:H, 1430:1430 + NR]
        brow = region(7)[0:H, 0:NR]
        extra = [region(6, 2), region(3, 2)]
        masks_in = region(7)[:, 1024:2048].rearrange("p (l t) -> p l t", t=P)

        loaded = [sem(f"slot_loaded{i}") for i in range(RING)]
        x_in, c_in, w_in, late_in = sem("x_in"), sem("ident_in"), sem("first_small_in"), sem("small_in")
        part_in, rb_in, masks_ld = sem("first_heads_in"), sem("rel_bias_in"), sem("masks_in")
        extra_in = [sem(f"extra_slot_loaded{i}") for i in range(2)]
        biasload, biasout = sem("bias_in"), sem("bias_out")
        setup = sem("memsets_done")
        dv = sem("dve_step")
        ms_ready, rstd_ready = sem("ms_ready"), sem("rstd_ready")
        x_added = sem("residual_added")
        up_part_in, down_part_in = sem("last_up_first_half_in"), sem("last_down_first_half_in")
        count_done = sem("counts_done")
        xn_ready, nt_done = sem("normed_ready"), sem("normed_transposed")
        hT_dve, hT_act = sem("hT_by_dve"), sem("hT_by_act")
        lb_in, lb_exp = sem("lb_logits"), sem("lb_exp")
        f_done, f_exp, k_ready, q_done, q_ready = (sem(n) for n in ("f_done", "f_exp", "k_ready", "q_done", "q_ready"))
        lev_done, upd_ready, pred_done = sem("level_done"), sem("level_operands"), sem("level_scores")
        vg_done, v_ready, g_exp, gate_ready = (sem(n) for n in ("vg_done", "v_ready", "g_exp", "gate_ready"))
        cross_ready = sem("cross_ready")
        o_done, osq_done, og_ready = sem("o_done"), sem("osq_done"), sem("og_ready")
        ot_done, oT_ready, pr_done, x_ready = (sem(n) for n in ("ot_done", "oT_ready", "proj_done", "x_ready"))
        rb_done, rb_ready = sem("bias_row_done"), sem("bias_row_ready")
        rt_done, gl_ready, gl_exp, el_ready, el_exp = (sem(n) for n in ("router_done", "group_logits", "group_exp",
                                                                        "top2_gap", "top2_exp"))
        asg_ready, pos_done, nblk_ready = sem("assigned"), sem("positions_done"), sem("blocks_ready")
        pick_ready, pickw_ready, gat_done, xg_ready = (sem(n) for n in ("pick_ready", "pickw_ready", "gather_done",
                                                                        "gathered_ready"))
        up_done, exp_done, den_ready, sig_ready, silu_ready, hid_ready = (
            sem(n) for n in ("up_done", "silu_exp", "silu_denominator", "silu_sigmoid", "silu_ready", "hidden_ready"))
        ht_done, hidT_ready = sem("hidden_transposed"), sem("hiddenT_ready")
        st_done, s_ready = sem("spread_transposed"), sem("spread_ready")
        down_done, y_ready, c_done = sem("down_done"), sem("y_ready"), sem("combine_done")
        kq_done, sq_done, kqn_ready, tkq_done, kqT_ready = (sem(n) for n in ("kq_done", "kq_squares", "kq_normed",
                                                                             "kq_transposed", "kqT_ready"))
        av_done, av_ready = sem("att_v_done"), sem("att_v_ready")
        sc_done, mx_ready, ex_done, pn_ready = (sem(n) for n in ("scores_done", "max_ready", "probs_exp",
                                                                 "probs_ready"))
        pt_done, pT_ready, pv_done = sem("probs_transposed"), sem("probT_ready"), sem("pv_done")
        out_done = sem("out_done")
        ov = [{n: sem(f"over{l}_{n}") for n in ("w", "shift", "picked", "pick", "gat", "xg", "up", "exp", "den", "rec",
                                                "sil", "hid", "ht", "hidT", "y", "ye", "c", "x", "end")}
              for l in range(2)]

        def chunk(c):
            return ring[:, c % RING, :]

        def in_extra(r, it):
            return is_int(it, 0) and r in (RING, RING + 1)

        def last_pair(it, u):
            return is_int(it, ITERS - 1) and u == UN - 1

        def ring_chunk(layer, r, it):
            return MOE[layer] + r - (0 if is_int(it, 0) and r < RING else 2)

        def gate_or_up(layer, r, it):
            c = extra[r - RING] if in_extra(r, it) else chunk(ring_chunk(layer, r, it))
            return c.rearrange("p (k n) -> p k n", n=512)

        def up_view(c):
            return chunk(c).rearrange("p (k n) -> p k n", n=512)

        def down_view(c):
            return chunk(c).rearrange("p (k n) -> p k n", n=D)

        def over_pairs(eng, body):
            body(0)
            with eng.Fori(1, ITERS - 1) as it:
                body(it)
            body(ITERS - 1)

        def is_int(v, n):
            return type(v) is int and v == n

        block = ctx.enter_context(nc.Block())

        @block.sync
        def _(sp):
            for a in range(TT):
                sp.dma_start(xs[:, a, :], x[0, a * P:(a + 1) * P, :]).then_inc(x_in, 16)
            sp.dma_start(ident[:], c_ident).then_inc(c_in, 16)
            sp.dma_start(wcol[:, 0, :], mix_norm[0].rearrange("(k p) -> p k", p=P)).then_inc(w_in, 16)
            sp.dma_start(lbl[:], hg_lb.rearrange("a (k p) -> p a k", p=P)).then_inc(w_in, 16)

            def expert_read(layer, r, it=0):
                q = layer * PAIRS + r // 6
                if r % 6 < 4:
                    return up_done, it * (2 * UN) + (2 * q + 1 + r % 6 // 2)
                return down_done, it * (2 * UN) + (2 * q + 2)

            def read(c):
                if c >= MOE1:
                    return expert_read(1, c - MOE1 + 2)
                if c >= MIX1:
                    return ((kq_done, 2), (kq_done, 4), (kq_done, 6), (kq_done, 8), (av_done, 2), (av_done, 4),
                            (pr_done, 7), (pr_done, 8))[c - MIX1]
                if c >= MOE0:
                    return expert_read(0, c - MOE0 + 2)
                return ((f_done, 2), (f_done, 4), (q_done, 2), (q_done, 4), (vg_done, 2), (vg_done, 4), (vg_done, 6),
                        (vg_done, 8), (pr_done, 3), (pr_done, 4))[c]

            def load(c, dst, src):
                if c >= RING:
                    sp.wait_ge(*read(c - RING))
                sp.dma_start(dst, src).then_inc(loaded[c % RING], 16)

            def load_expert(layer, r, dst, src, it):
                c = ring_chunk(layer, r, it)
                if in_extra(r, it):
                    if layer == 0:
                        sp.wait_ge(o_done, 4)
                        if r == RING:
                            sp.wait_ge(og_ready, 2 * TT)
                    elif r == RING:
                        sp.wait_ge(pv_done, 4)
                        sp.wait_ge(mx_ready, H)
                    else:
                        sp.wait_ge(sc_done, H)
                        sp.wait_ge(pt_done, H)
                    sp.dma_start(dst, src).then_inc(extra_in[r - RING], 16)
                    return
                if is_int(it, 0) and r < RING:
                    sp.wait_ge(*read(c - RING))
                elif is_int(it, 0) and r < 2 * RING + 2:
                    sp.wait_ge(*expert_read(layer, r - RING - 2, it))
                else:
                    sp.wait_ge(*expert_read(layer, r - RING, it))
                sp.dma_start(dst, src).then_inc(loaded[c % RING], 16)

            def cols(w, j):
                return w[:, j * 512:(j + 1) * 512].rearrange("(k p) n -> p k n", p=P)

            f_cols = cols(hg_w_in[0], 2)
            sp.dma_start(up_view(MIX0)[:, :, 0:256], f_cols[:, :, 0:256]).then_inc(part_in, 16)
            sp.dma_start(up_view(MIX0)[:, :, 256:512], f_cols[:, :, 256:512]).then_inc(loaded[MIX0 % RING], 16)
            load(MIX0 + 1, up_view(1), cols(hg_w_in[0], 3))
            sp.dma_start(rbw, rel_bias).then_inc(rb_in, 16)
            sp.dma_start(bucket, c_bucket).then_inc(rb_in, 16)
            sp.dma_start(future, c_future).then_inc(rb_in, 16)
            sp.dma_start(masks_in, c_masks).then_inc(masks_ld, 16)
            for c, j in enumerate((0, 1, 6, 7, 4, 5)):
                load(MIX0 + 2 + c, up_view(MIX0 + 2 + c), cols(hg_w_in[0], j))
            sp.dma_start(onorm[:], hg_o_norm[0:1, :].to_broadcast([P, P])).then_inc(late_in, 16)
            sp.dma_start(wcol[:, 1, :], kv_norm.rearrange("(k p) -> p k", p=P)).then_inc(late_in, 16)
            sp.dma_start(wcol[:, 2, :], mix_norm[1].rearrange("(k p) -> p k", p=P)).then_inc(late_in, 16)
            for l in range(2):
                sp.dma_start(wcol[:, 3 + l, :], ffn_norm[l].rearrange("(k p) -> p k", p=P)).then_inc(late_in, 16)
            sp.dma_start(kqcol[:, 0:1], k_norm.rearrange("(p a) -> p a", a=1)).then_inc(late_in, 16)
            sp.dma_start(kqcol[:, 1:2], q_norm[0].rearrange("(p a) -> p a", a=1)).then_inc(late_in, 16)
            sp.dma_start(before[:], c_before).then_inc(late_in, 16)
            sp.dma_start(slot[:], c_slot).then_inc(late_in, 16)
            sp.dma_start(prio[:], c_prio).then_inc(late_in, 16)
            for l in range(2):
                sp.dma_start(wr[:, l, :, 0:NG], moe_w_group[l].rearrange("(k p) n -> p k n", p=P)).then_inc(late_in, 16)
                sp.dma_start(wr[:, l, :, NG:], moe_w_expert[l].rearrange("(k p) n -> p k n", p=P)).then_inc(late_in, 16)
                sp.dma_start(br[:, l, 0:NG], moe_b_group[l:l + 1, :].to_broadcast([P, NG])).then_inc(late_in, 16)
                sp.dma_start(br[:, l, NG:], moe_b_expert[l:l + 1, :].to_broadcast([P, E])).then_inc(late_in, 16)
            for j in range(2):
                load(MIX0 + 8 + j, up_view(MIX0 + 8 + j), cols(hg_w_out[0], j))

            def expert_chunk(layer, j, e, copy, c):
                if j < 4:
                    copy(up_view(c), cols(moe_w_in[layer, e], j // 2))
                else:
                    copy(down_view(c), moe_w_out[layer, e].rearrange("(k p) n -> p k n", p=P))

            def experts(layer):
                def load_next(r, it):
                    if in_extra(r, it):
                        load_expert(layer, r, gate_or_up(layer, r, it), cols(moe_w_in[layer, 2 + r % 2], 1), it)
                    else:
                        expert_chunk(layer, r % 6, it * (2 * UN) + (2 * (r // 6) + r % 2),
                                     lambda dst, src: load_expert(layer, r, dst, src, it), ring_chunk(layer, r, it))

                def body(it):
                    order = list(range(6 * UN))
                    if is_int(it, 0):
                        order = order[0:6] + [9, 8] + order[6:8] + order[10:]
                    if is_int(it, ITERS - 1):
                        order = order[:-4]
                    for r in order:
                        load_next(r, it)
                    if is_int(it, ITERS - 1):
                        load_last(it)

                def load_last(it):
                    for r in (6 * UN - 4, 6 * UN - 2):
                        c = ring_chunk(layer, r, it)
                        sp.wait_ge(*expert_read(layer, r - RING, it))
                        sp.wait_ge(*expert_read(layer, r + 1 - RING, it))
                        for part in range(2):
                            for x2 in range(2):
                                e = E - 2 + x2
                                if r == 6 * UN - 4:
                                    ks = slice(part * (KD // 2), (part + 1) * (KD // 2))
                                    dst, src = up_view(c + x2)[:, ks, :], cols(moe_w_in[layer, e], 1)[:, ks, :]
                                    part_in = up_part_in
                                else:
                                    ns = slice(part * 512, (part + 1) * 512)
                                    dst = down_view(c + x2)[:, :, ns]
                                    src = moe_w_out[layer, e].rearrange("(k p) n -> p k n", p=P)[:, :, ns]
                                    part_in = down_part_in
                                sp.dma_start(dst, src).then_inc(loaded[(c + x2) % RING] if part else part_in, 16)
                over_pairs(sp, body)
                over(layer)

            def over(layer):
                s = ov[layer]
                sp.wait_ge(nblk_ready, layer + 1)
                n = sp.value_load(nblk[0:1, layer:layer + 1], min_val=1, max_val=4)
                with sp.If(n > 1):
                    sp.wait_ge(down_done, 2 * (layer + 1) * PAIRS)
                    with sp.Fori(1, n) as b:
                        with sp.Fori(0, PAIRS) as q:
                            sp.wait_ge(s["x"], b * PAIRS + q - (PAIRS - 1))
                            for j in range(6):
                                expert_chunk(layer, j, q * 2 + j % 2,
                                             lambda dst, src: sp.dma_start(dst, src).then_inc(s["w"], 16), j)
                    sp.wait_ge(s["end"], 1)

            experts(0)
            c = MIX1
            for w, j in ((w_kv, 0), (w_kv, 1), (att_w_q[0], 0), (att_w_q[0], 1), (w_kv, 2), (w_kv, 3),
                         (att_w_o[0], 0), (att_w_o[0], 1)):
                load(c, up_view(c), cols(w, j))
                c += 1
            experts(1)
            for a in range(TT):
                sp.wait_ge(x_ready, a + 1)
                sp.dma_start(out[0, a * P:(a + 1) * P, :], xs[:, a, :]).then_inc(out_done, 16)
            sp.wait_ge(out_done, 16 * TT)
            sp.wait_ge(biasout, 16)

        @block.gpsimd
        def _(pool):
            pool.memset(ones[:], 1.0).then_inc(setup, 1)
            pool.memset(mhalf[:], -0.5).then_inc(setup, 1)
            pool.wait_ge(setup, 2)

            def root(i, c0, c1):
                pool.wait_ge(ms_ready, i)
                pool.tensor_tensor(rstd[:, c0:c1], ms[:, c0:c1], mhalf[:, c0:c1], ALU.pow).then_inc(rstd_ready, 1)

            def roots(i, n):
                for a in range(TT):
                    root(i + a, a * n, (a + 1) * n)

            pool.memset(region(4), 0.0).then_inc(setup, 1)
            roots(POW_MIX0, 1)
            pool.wait_ge(rb_ready, 1)
            pool.dma_start(bias_dram.rearrange("h (p n) -> h p n", p=P)[:, :, 0:NR],
                           brow.unsqueeze(1).to_broadcast([H, P, NR])).then_inc(biasout, 16)
            for g in range(4):
                root(POW_O + g, 4 * g, 4 * g + 4)
            roots(POW_FFN0, 1)
            pool.wait_ge(biasout, 16)
            pool.wait_ge(up_done, 4)
            pool.dma_start(bias, bass.AP(bias_dram.tensor, P - 1, [[NR, P], [P * (NR + 1), H], [1, T]])).then_inc(biasload, 16)
            for a in range(TT):
                root(POW_MIX1 + a, XR + a, XR + a + 1)
            root(POW_K, 0, TT * H)
            root(POW_Q, 0, TT * H)
            roots(POW_FFN1, 1)

        @block.scalar
        def _(act):
            def transposed(n, a, bank, dsts):
                act.wait_ge(nt_done, 2 * n + 2)
                ts = slice(a * P, (a + 1) * P)
                for dst, w in dsts:
                    src = ps[:, bank + 1, :].rearrange("p (k t) -> p k t", t=P)
                    for j in range(4):
                        i = act.activation(dst[:, 4 + j, ts], src[:, j, :], ACT.Copy, scale=wcol[:, w, 4 + j:5 + j])
                    i.then_inc(hT_act, 1)

            act.wait_ge(lb_in, 1)
            act.activation(lbw[:, 2:4, :], lbw[:, 0:2, :], ACT.Exp).then_inc(lb_exp, 1)
            act.wait_ge(w_in, SMALL)
            for a in range(TT):
                transposed(a, a, 4 + 2 * a, [(hT, 0)])
            for hp in range(4):
                act.wait_ge(f_done, hp + 1)
                act.activation(f_all[:, hp * 512:(hp + 1) * 512], ps[:, hp, :], ACT.Exp, scale=-1.0).then_inc(f_exp, 1)
            for hp in range(4):
                act.wait_ge(q_done, hp + 1)
                act.activation(qp_all[:, hp * 512:(hp + 1) * 512], ps[:, 4 + hp, :], ACT.Copy,
                               scale=QSCALE).then_inc(q_ready, 1)
            act.wait_ge(biasout, 16)
            for i in range(4):
                act.wait_ge(vg_done, i + 1)
                act.activation(gate[:, i % 2, (i // 2) * 512:(i // 2 + 1) * 512], ps[:, 4 + i, :], ACT.Exp,
                               scale=-1.0).then_inc(g_exp, 1)
            for i in range(4):
                act.wait_ge(vg_done, 5 + i)
                act.copy(v_all[:, i % 2, (i // 2) * 512:(i // 2 + 1) * 512], ps[:, 4 + i, :]).then_inc(v_ready, 1)
            for g in range(4):
                if g == 2:
                    act.wait_ge(lev_done, 9)
                    act.wait_ge(upd_ready, 8)
                    act.copy(scross, ps[:, 0:2, :].rearrange("p b (h t) -> p (b h) t", t=P)).then_inc(cross_ready, 1)
                act.wait_ge(o_done, g + 1)
                act.activation(osq[:, g // 2, (g % 2) * 512:(g % 2 + 1) * 512], ps[:, 4 + g, :],
                               ACT.Square).then_inc(osq_done, 1)

            def oT_tile(n, a, dst):
                for b in range(2):
                    act.wait_ge(ot_done, 2 * n + b + 1)
                    act.copy(dst[:, 4 * b:4 * b + 4, a * P:(a + 1) * P],
                             ps[:, 2 * a + b, :].rearrange("p (k t) -> p k t", t=P)).then_inc(oT_ready, 1)

            for a in range(TT):
                oT_tile(a, a, oT)

            def weighted_columns(layer, buf, half, bank):
                for k in range(4):
                    i = act.activation(xgT[:, buf, 4 * half + k, :], ps[:, bank, k * P:(k + 1) * P], ACT.Copy,
                                       scale=wcol[:, 3 + layer, 4 * half + k:4 * half + k + 1])
                return i

            def over(layer):
                s = ov[layer]
                act.wait_ge(nblk_ready, layer + 1)
                n = act.value_load(nblk[0:1, layer:layer + 1], min_val=1, max_val=4)
                with act.If(n > 1):
                    with act.Fori(1, n) as b:
                        with act.Fori(0, PAIRS) as q:
                            v = b * PAIRS + q - (PAIRS - 1)
                            act.wait_ge(s["gat"], v)
                            weighted_columns(layer, 0, 0, 4)
                            weighted_columns(layer, 0, 1, 5)
                            act.copy(spread, ps[:, 0, 0:T]).then_inc(s["xg"], 1)
                            act.wait_ge(s["up"], v)
                            act.activation(en, ps[:, 6, :], ACT.Exp, scale=-1.0).then_inc(s["exp"], 1)
                            act.wait_ge(s["y"], v)
                            act.copy(y, ps[:, 6:8, :].rearrange("p b n -> p (b n)")).then_inc(s["ye"], 1)
                    act.wait_ge(s["end"], 1)

            def moe(layer):
                for a in range(TT):
                    transposed((2, 6)[layer] + a, a, 2 * a, [(hrT, 3 + layer)])
                act.wait_ge(gl_ready, layer + 1)
                act.activation(gex, gpr, ACT.Exp).then_inc(gl_exp, 1)
                act.wait_ge(el_ready, layer + 1)
                act.activation(e2, dd, ACT.Exp).then_inc(el_exp, 1)
                P0 = layer * PAIRS

                def gathered(it, u, half):
                    q = P0 + u
                    act.wait_ge(gat_done, it * (2 * UN) + (2 * q + half + 1))
                    if not (type(it) is int and it * UN + q < 2):
                        act.wait_ge(up_done, it * (2 * UN) + 2 * (q - 1))
                    bank = 7 if is_int(it, 0) and u == 0 and half else 4
                    weighted_columns(layer, u % 2, half, bank).then_inc(xg_ready, 1)

                def body(it):
                    for u in range(UN):
                        q = P0 + u
                        last = last_pair(it, u)
                        act.wait_ge(up_done, it * (2 * UN) + (2 * q + 1))
                        if not (type(it) is int and it * UN + q < 1):
                            act.wait_ge(hid_ready, it * UN + q)
                        act.activation(en, ps[:, 6, :], ACT.Exp, scale=-1.0).then_inc(exp_done, 1)
                        if not last:
                            gathered(it, u + 1, 0)
                            gathered(it, u + 1, 1)
                        for half in range(2):
                            act.wait_ge(down_done, it * (2 * UN) + (2 * q + 1 + half))
                            if not (type(it) is int and it * UN + q < 1):
                                act.wait_ge(c_done, it * (2 * UN) + 2 * q)
                            act.copy(y[:, half * 512:(half + 1) * 512], ps[:, 6 + half, :]).then_inc(y_ready, 1)

                gathered(0, 0, 0)
                gathered(0, 0, 1)
                over_pairs(act, body)
                over(layer)

            moe(0)

            for a in range(TT):
                transposed(4 + a, a, 4 + 2 * a, [(hkvT, 1), (hqT, 2)])
            for i in range(8):
                dst = (kn, qn)[i // 4]
                half, a = (i % 4) // 2, i % 2
                act.wait_ge(kq_done, i + 1)
                if i < TT:
                    act.wait_ge(rstd_ready, POW_MIX1 + a)
                act.activation(dst[:, a, half * 512:(half + 1) * 512], ps[:, (i // 4) * 4 + 2 * a + half, :],
                               ACT.Square, scale=rstd[:, XR + a:XR + a + 1]).then_inc(sq_done, 1)

            def heads_T(i0, dst, w):
                for b in range(4):
                    act.wait_ge(tkq_done, i0 + b + 1)
                    act.activation(dst[:, 2 * b:2 * b + 2, :], ps[:, i0 + b, :].rearrange("p (k t) -> p k t", t=T),
                                   ACT.Copy, scale=kqcol[:, w:w + 1]).then_inc(kqT_ready, 1)

            def att_v(i):
                act.wait_ge(av_done, i + 1)
                act.activation(v_all[:, i % 2, (i // 2) * 512:(i // 2 + 1) * 512], ps[:, i, :], ACT.Copy,
                               scale=rstd[:, XR + i % 2:XR + i % 2 + 1]).then_inc(av_ready, 1)

            def head_exp(h):
                act.wait_ge(mx_ready, h + 1)
                act.activation(prob[:, h, 0:P], prob[:, h, 0:P], ACT.Exp, bias=nmax[:, h, 0:1],
                               accum_out=esum[:, h, 0:1])
                act.activation(prob[:, h, P:NR], prob[:, h, P:NR], ACT.Exp, bias=nmax[:, h, 1:2],
                               accum_out=esum[:, h, 1:2]).then_inc(ex_done, 1)

            def prob_T(h):
                act.wait_ge(pt_done, h + 1)
                act.copy(probT[:, h, :], ps[:, 4 + h % 4, 0:NR]).then_inc(pT_ready, 1)

            def heads_o(b):
                act.wait_ge(pv_done, b + 1)
                act.copy(oT[:, 2 * b:2 * b + 2, :], ps[:, b, :].rearrange("p (k t) -> p k t", t=T))\
                   .then_inc(oT_ready, 1)

            heads_T(0, kT, 0)
            att_v(0)
            heads_T(4, qT, 2)
            att_v(1)
            for h in range(4):
                head_exp(h)
            att_v(2)
            for h in range(4, H):
                head_exp(h)
            att_v(3)
            for h in range(6):
                prob_T(h)
            heads_o(0)
            prob_T(6)
            prob_T(7)
            for b in range(1, 4):
                heads_o(b)
            moe(1)

        @block.vector
        def _(dve):
            steps = [0]

            def link(ins):
                steps[0] += 1
                ins.then_inc(dv, 1)
                dve.wait_ge(dv, steps[0])

            def mean_ready(c0, c1, width):
                dve.tensor_scalar(ms[:, c0:c1], ms[:, c0:c1], 1.0 / width, EPS, ALU.mult, ALU.add)\
                   .then_inc(ms_ready, 1)

            def rms(i, c0, c1, width, meanwhile=lambda: None):
                mean_ready(c0, c1, width)
                meanwhile()
                dve.wait_ge(rstd_ready, i)

            def transposed(n, a, bank, dsts):
                dve.wait_ge(nt_done, 2 * n + 1)
                ts = slice(a * P, (a + 1) * P)
                for dst, w in dsts:
                    src = ps[:, bank, :].rearrange("p (k t) -> p k t", t=P)
                    dve.tensor_tensor(dst[:, 0:4, ts], src, wcol[:, w, 0:4].unsqueeze(2).to_broadcast([P, 4, P]),
                                      ALU.mult).then_inc(hT_dve, 1)

            def norm(i, dst, a, meanwhile=lambda: None):
                link(dve.tensor_tensor_reduce(out=dst[:, a, :], in0=xs[:, a, :], in1=xs[:, a, :], scale=1.0,
                                              scalar=0.0, op0=ALU.mult, op1=ALU.add, accum_out=ms[:, a:a + 1]))
                rms(i + a, a, a + 1, D, meanwhile)
                dve.tensor_scalar(dst[:, a, :], xs[:, a, :], rstd[:, a:a + 1], None, ALU.mult).then_inc(xn_ready, 1)

            def add_projection(n, a, half):
                dve.wait_ge(pr_done, 4 * n + 2 * a + half + 1)
                dst = xs[:, a, half * 512:(half + 1) * 512]
                dve.tensor_tensor(dst, dst, ps[:, 4 + 2 * a + half, :], ALU.add).then_inc(x_added, 1)
                dve.wait_ge(x_added, 4 * n + 2 * a + half + 1)

            def projected_and_normed(n, i):
                add_projection(n, 0, 0)
                add_projection(n, 0, 1)
                norm(i, hn, 0)
                transposed((2, 6)[n], 0, 0, [(hrT, 3 + n)])
                add_projection(n, 1, 0)
                add_projection(n, 1, 1)
                norm(i, hn, 1, lambda: transposed((2, 6)[n] + 1, 1, 2, [(hrT, 3 + n)]))

            for a in range(TT):
                dve.wait_ge(x_in, 16 * TT)
                norm(POW_MIX0, xn, a)
            dve.wait_ge(w_in, SMALL)
            link(dve.tensor_tensor(lbw[:, 4, :], lbl[:, 0, :], lbl[:, 1, :], ALU.max))
            dve.tensor_tensor(lbw[:, 0:2, :], lbl[:], lbw[:, 4:5, :].to_broadcast([P, 2, H]),
                              ALU.subtract).then_inc(lb_in, 1)
            dve.wait_ge(lb_exp, 1)
            link(dve.tensor_tensor(lbw[:, 4, :], lbw[:, 2, :], lbw[:, 3, :], ALU.add))
            link(dve.reciprocal(lbw[:, 4, :], lbw[:, 4, :]))
            link(dve.tensor_tensor(lbw[:, 0, :], lbw[:, 2, :], lbw[:, 4, :], ALU.mult))
            link(dve.tensor_scalar(lbw[:, 1, :], lbw[:, 0, :], -1.0, 1.0, ALU.mult, ALU.add))
            for a in range(TT):
                transposed(a, a, 4 + 2 * a, [(hT, 0)])
            for hp in range(4):
                sl = slice(hp * 512, (hp + 1) * 512)
                dve.wait_ge(f_exp, hp + 1)
                link(dve.tensor_scalar(f_all[:, sl], f_all[:, sl], 1.0, None, ALU.add))
                link(dve.reciprocal(f_all[:, sl], f_all[:, sl]))
                for h in (2 * hp, 2 * hp + 1):
                    hs = slice(h * T, (h + 1) * T)
                    i = dve.tensor_scalar(f_all[:, hs], f_all[:, hs], lbw[:, 1, h:h + 1], lbw[:, 0, h:h + 1],
                                          ALU.mult, ALU.add)
                link(i)
                dve.tensor_scalar(ks_all[:, sl], f_all[:, sl], -1.0, 1.0, ALU.mult, ALU.add).then_inc(k_ready, 1)

            dve.wait_ge(rb_in, 16 * 3)
            dve.wait_ge(rb_done, 1)
            dve.tensor_tensor(brow, ps[0:H, 7, 0:NR], future, ALU.add).then_inc(rb_ready, 1)

            def level(l):
                dve.wait_ge(lev_done, l + 1)
                m = 1 << l >> 1
                if l == 0:
                    dve.tensor_tensor(qp_all, qp_all, f_all, ALU.mult).then_inc(upd_ready, 1)
                else:
                    t_now, t_next = (f_all, t_odd) if l % 2 else (t_odd, f_all)
                    tv = t_now[:, 0:2048 // m].rearrange("p (b two) -> p b two", two=2)
                    qv = qp_all.rearrange("p (b two m) -> p b two m", two=2, m=m)
                    kv = ks_all.rearrange("p (b two m) -> p b two m", two=2, m=m)
                    nb = 2048 // (2 * m)
                    dve.tensor_tensor(qv[:, :, 1, :], qv[:, :, 1, :],
                                      tv[:, :, 0].unsqueeze(2).to_broadcast([P, nb, m]), ALU.mult)
                    dve.tensor_tensor(kv[:, :, 0, :], kv[:, :, 0, :],
                                      tv[:, :, 1].unsqueeze(2).to_broadcast([P, nb, m]), ALU.mult)\
                       .then_inc(upd_ready, 1)
                    if l < LEVELS:
                        link(dve.tensor_tensor(t_next[:, 0:nb], tv[:, :, 0], tv[:, :, 1], ALU.mult))
                dve.copy_predicated(sdiag, masks[:, l:l + 1, :].to_broadcast([P, 2 * H, P]),
                                    ps[:, 0:4, :].rearrange("p b (h t) -> p (b h) t", t=P)).then_inc(pred_done, 1)
                dve.wait_ge(upd_ready, l + 1)
                dve.wait_ge(pred_done, l + 1)

            def silu_gate(i):
                gv = gate[:, i % 2, (i // 2) * 512:(i // 2 + 1) * 512]
                dve.wait_ge(g_exp, i + 1)
                link(dve.tensor_scalar(gv, gv, 1.0, None, ALU.add))
                link(dve.reciprocal(gv, gv))
                link(dve.tensor_tensor(gv, ps[:, 4 + i, :], gv, ALU.mult))
                g3 = gv.rearrange("p (h n) -> p h n", n=P)
                dve.tensor_tensor(g3, g3, onorm[:, :].unsqueeze(1).to_broadcast([P, 4, P]), ALU.mult)\
                   .then_inc(gate_ready, 1)

            dve.wait_ge(masks_ld, 16)
            link(dve.tensor_copy(masks[:], masks_in))
            dve.wait_ge(late_in, LATE)
            link(dve.tensor_scalar(kqcol[:, 2:3], kqcol[:, 1:2], QSCALE, None, ALU.mult))
            dve.wait_ge(setup, 3)
            dve.wait_ge(q_ready, 4)
            dve.wait_ge(k_ready, 4)
            for l in range(LEVELS + 1):
                level(l)
                if l < 4:
                    silu_gate(l)
            dve.wait_ge(gate_ready, 4)
            def o_squares(g):
                dve.wait_ge(osq_done, g + 1)
                link(dve.tensor_reduce(ms[:, 4 * g:4 * g + 4], osq[:, g // 2, (g % 2) * 512:(g % 2 + 1) * 512]
                                       .rearrange("p (h n) -> p h n", n=P), AX.X, ALU.add))
                mean_ready(4 * g, 4 * g + 4, P)

            for a in range(TT):
                o_squares(2 * a)
                o_squares(2 * a + 1)
                for g in (2 * a, 2 * a + 1):
                    dve.wait_ge(rstd_ready, POW_O + g)
                    for j in range(4):
                        h = 4 * (g % 2) + j
                        i = dve.scalar_tensor_tensor(og[:, a, h * P:(h + 1) * P], ps[:, 4 + g, j * P:(j + 1) * P],
                                                     rstd[:, 4 * g + j:4 * g + j + 1], gate[:, a, h * P:(h + 1) * P],
                                                     ALU.mult, ALU.mult)
                    i.then_inc(og_ready, 1)
            projected_and_normed(0, POW_FFN0)

            def router(layer):
                dve.wait_ge(rt_done, layer + 1)
                for a in range(TT):
                    i = dve.scalar_tensor_tensor(lg[:, a, :], ps[:, 4, a * (NG + E):(a + 1) * (NG + E)],
                                                 rstd[:, a:a + 1], br[:, layer, :], ALU.mult, ALU.add)
                link(i)

                def b(v, n):
                    return v.unsqueeze(2).to_broadcast([P, TT, n])

                def one_hot(dst, tmp, v, mx, n):
                    link(dve.tensor_reduce(mx, v, AX.X, ALU.max))
                    link(dve.tensor_tensor(tmp, v, b(mx, n), ALU.is_equal))
                    link(dve.tensor_tensor(tmp, tmp, prio[:, 0:n].unsqueeze(1).to_broadcast([P, TT, n]), ALU.mult))
                    link(dve.tensor_reduce(ss, tmp, AX.X, ALU.max))
                    link(dve.tensor_tensor(dst, tmp, b(ss, n), ALU.is_equal))

                one_hot(goh, gpr, lg[:, :, 0:NG], gmx, NG)
                dve.tensor_tensor(gpr, lg[:, :, 0:NG], b(gmx, NG), ALU.subtract).then_inc(gl_ready, 1)
                link(dve.tensor_tensor(tmp32, lg[:, :, NG:].rearrange("p a (g e) -> p a g e", g=NG),
                                       goh.unsqueeze(3).to_broadcast([P, TT, NG, EG]), ALU.mult))
                link(dve.tensor_reduce(es, tmp32.rearrange("p a g e -> p a e g"), AX.X, ALU.add))
                one_hot(oh1, pr8, es, m1, EG)
                link(dve.scalar_tensor_tensor(es2, oh1, -3e38, es, ALU.mult, ALU.add))
                one_hot(oh2, pr8, es2, m2, EG)
                dve.tensor_tensor(dd, m2, m1, ALU.subtract).then_inc(el_ready, 1)
                link(dve.tensor_tensor(a8, oh1, oh2, ALU.add))
                dve.tensor_tensor(asg.rearrange("p a (g e) -> p a g e", g=NG), goh.unsqueeze(3)
                                  .to_broadcast([P, TT, NG, EG]), a8.unsqueeze(2).to_broadcast([P, TT, NG, EG]),
                                  ALU.mult).then_inc(asg_ready, 1)
                dve.wait_ge(gl_exp, layer + 1)
                link(dve.tensor_reduce(gsm, gex, AX.X, ALU.add))
                dve.wait_ge(el_exp, layer + 1)
                link(dve.tensor_scalar(w1, e2, 1.0, None, ALU.add))
                link(dve.tensor_tensor(w1, w1, gsm, ALU.mult))
                link(dve.reciprocal(w1, w1))
                link(dve.tensor_tensor(w2, w1, e2, ALU.mult))
                link(dve.tensor_tensor(oh1, oh1, b(w1, EG), ALU.mult))
                link(dve.tensor_tensor(oh2, oh2, b(w2, EG), ALU.mult))
                link(dve.tensor_tensor(wt8, oh1, oh2, ALU.add))
                link(dve.tensor_tensor(tmp32, goh.unsqueeze(3).to_broadcast([P, TT, NG, EG]),
                                       wt8.unsqueeze(2).to_broadcast([P, TT, NG, EG]), ALU.mult))
                t3 = tmp32.rearrange("p a g e -> p a (g e)")
                for a in range(TT):
                    i = dve.tensor_copy(wgt[:, :, a, :], t3[:, a, :].rearrange("p (q e) -> p q e", e=2))
                dve.wait_ge(pos_done, layer + 1)
                link(dve.scalar_tensor_tensor(tpos, ps[:, 5, 0:TT * E].rearrange("p (a e) -> p a e", e=E), 1.0, asg,
                                              ALU.add, ALU.mult))
                for a in range(TT):
                    i = dve.tensor_scalar(pos[:, :, a, :], tpos[:, a, :].rearrange("p (q e) -> p q e", e=2), -1.0,
                                          None, ALU.add)
                link(i)

            def passes(layer):
                dve.wait_ge(count_done, layer + 1)
                link(dve.tensor_reduce(cmx, ps[:, 6, 0:E], AX.X, ALU.max))
                for j in range(1, 4):
                    i = dve.tensor_scalar(nblf[:, j:j + 1], cmx, float(j * CAP), None, ALU.is_gt)
                link(i)
                link(dve.tensor_reduce(nblf[:, 0:1], nblf[:, 1:4], AX.X, ALU.add))
                dve.tensor_scalar(nblk[:, layer:layer + 1], nblf[:, 0:1], 1.0, None, ALU.add).then_inc(nblk_ready, 1)

            def over(layer, n):
                s = ov[layer]
                with dve.If(n > 1):
                    dve.memset(mark[:, 2:3], 0.0).then_inc(s["x"], 1)
                    with dve.Fori(1, n) as b:
                        dve.tensor_scalar(pos, pos, -float(CAP), None, ALU.add).then_inc(s["shift"], 1)
                        dve.wait_ge(s["shift"], b)
                        dve.memset(mark[:, 4:5], 0.0)
                        with dve.Fori(0, PAIRS) as q:
                            v = b * PAIRS + q - (PAIRS - 1)
                            dve.wait_ge(s["x"], v)
                            build_pick(q, s["picked"])
                            dve.wait_ge(s["picked"], v)
                            dve.tensor_tensor(pickw, pick, wgt[:, q].unsqueeze(3).to_broadcast([P, TT, 2, BLK]),
                                              ALU.mult).then_inc(s["pick"], 1)
                            dve.wait_ge(s["exp"], v)
                            dve.tensor_scalar(en, en, 1.0, None, ALU.add).then_inc(s["den"], 1)
                            dve.wait_ge(s["den"], v)
                            dve.reciprocal(en, en).then_inc(s["rec"], 1)
                            dve.wait_ge(s["rec"], v)
                            dve.tensor_tensor(en, en, ps[:, 6, :], ALU.mult).then_inc(s["sil"], 1)
                            dve.wait_ge(s["sil"], v)
                            dve.tensor_tensor(hid, en, ps[:, 7, :], ALU.mult).then_inc(s["hid"], 1)
                            dve.wait_ge(s["ht"], v)
                            dve.tensor_copy(hidT, ps[:, 1, :].rearrange("p (k s) -> p k s", s=P))\
                               .then_inc(s["hidT"], 1)
                            dve.wait_ge(s["c"], v)
                            for a in range(TT):
                                i = dve.tensor_tensor(xs[:, a, :], xs[:, a, :],
                                                      ps[:, 2 * a:2 * a + 2, :].rearrange("p b n -> p (b n)"),
                                                      ALU.add)
                            i.then_inc(s["x"], 1)
                    dve.memset(mark[:, 3:4], 0.0).then_inc(s["end"], 1)
                    dve.wait_ge(s["end"], 1)

            def build_pick(q, signal):
                ins = dve.tensor_tensor(pick, pos[:, q].unsqueeze(3).to_broadcast([P, TT, 2, BLK]),
                                        slot[:, :].unsqueeze(1).unsqueeze(1).to_broadcast([P, TT, 2, BLK]),
                                        ALU.is_equal)
                ins.then_inc(signal, 1)

            def moe(layer):
                router(layer)
                P0 = layer * PAIRS

                def silu(it, u):
                    q = P0 + u
                    dve.wait_ge(exp_done, it * UN + (q + 1))
                    dve.tensor_scalar(en, en, 1.0, None, ALU.add).then_inc(den_ready, 1)
                    dve.wait_ge(den_ready, it * UN + (q + 1))
                    dve.reciprocal(en, en).then_inc(sig_ready, 1)
                    dve.wait_ge(sig_ready, it * UN + (q + 1))
                    dve.tensor_tensor(en, en, ps[:, 6, :], ALU.mult).then_inc(silu_ready, 1)
                    dve.wait_ge(silu_ready, it * UN + (q + 1))
                    dve.wait_ge(up_done, it * (2 * UN) + (2 * q + 2))
                    if not (type(it) is int and it * UN + q < 1):
                        dve.wait_ge(ht_done, it * UN + q)
                    dve.tensor_tensor(hid, en, ps[:, 7, :], ALU.mult).then_inc(hid_ready, 1)
                    dve.wait_ge(ht_done, it * UN + (q + 1))
                    if not (type(it) is int and it * UN + q < 1):
                        dve.wait_ge(down_done, it * (2 * UN) + 2 * q)
                    dve.tensor_copy(hidT, ps[:, 5, :].rearrange("p (k s) -> p k s", s=P)).then_inc(hidT_ready, 1)

                def spread_out(it, u):
                    q = P0 + u
                    dve.wait_ge(st_done, it * UN + (q + 1))
                    if not (type(it) is int and it * UN + q < 1):
                        dve.wait_ge(c_done, it * (2 * UN) + 2 * q)
                    dve.tensor_copy(spread, ps[:, 5, 0:T]).then_inc(s_ready, 1)

                def pick_for(it, u):
                    q = P0 + u
                    if not (type(it) is int and it * UN + q < 1):
                        dve.wait_ge(gat_done, it * (2 * UN) + 2 * q)
                        dve.wait_ge(pickw_ready, it * UN + q)
                    build_pick(it * UN + u, pick_ready)

                def weigh(it, u):
                    q = P0 + u
                    dve.wait_ge(pick_ready, it * UN + (q + 1))
                    if not (type(it) is int and it * UN + q < 1):
                        dve.wait_ge(st_done, it * UN + q)
                    dve.tensor_tensor(pickw, pick, wgt[:, it * UN + u].unsqueeze(3).to_broadcast([P, TT, 2, BLK]),
                                      ALU.mult).then_inc(pickw_ready, 1)

                pick_for(0, 0)
                passes(layer)

                def body(it):
                    for u in range(UN):
                        last = last_pair(it, u)
                        weigh(it, u)
                        if not last:
                            pick_for(it, u + 1)
                        silu(it, u)
                        spread_out(it, u)

                over_pairs(dve, body)
                dve.wait_ge(nblk_ready, layer + 1)
                n = dve.value_load(nblk[0:1, layer:layer + 1], min_val=1, max_val=4)
                for a in range(TT):
                    dve.wait_ge(c_done, 2 * (P0 + PAIRS) - 1 + a)
                    link(dve.tensor_tensor(xs[:, a, :], xs[:, a, :],
                                           ps[:, 2 * a:2 * a + 2, :].rearrange("p b n -> p (b n)"), ALU.add))
                over(layer, n)

            moe(0)

            for a in range(TT):
                dve.memset(mark[:, a:a + 1], 0.0).then_inc(xn_ready, 1)
            for a in range(TT):
                link(dve.tensor_tensor_reduce(out=xn[:, a, :], in0=xs[:, a, :], in1=xs[:, a, :], scale=1.0,
                                              scalar=0.0, op0=ALU.mult, op1=ALU.add,
                                              accum_out=ms[:, XR + a:XR + a + 1]))
                rms(POW_MIX1 + a, XR + a, XR + a + 1, D,
                    lambda: transposed(4 + a, a, 4 + 2 * a, [(hkvT, 1), (hqT, 2)]))

            def head_norm(i0, dst, i):
                for j in range(4):
                    half, a = j // 2, j % 2
                    dve.wait_ge(sq_done, i0 + j + 1)
                    link(dve.tensor_reduce(ms[:, a * H + half * 4:a * H + half * 4 + 4],
                                           dst[:, a, half * 512:(half + 1) * 512]
                                           .rearrange("p (h n) -> p h n", n=P), AX.X, ALU.add))
                rms(i, 0, TT * H, P)
                for a in range(TT):
                    j = dve.tensor_scalar(rstd[:, a * H:(a + 1) * H], rstd[:, a * H:(a + 1) * H],
                                          rstd[:, XR + a:XR + a + 1], None, ALU.mult)
                link(j)
                for a in range(TT):
                    dve.tensor_tensor(dst[:, a, :].rearrange("p (h n) -> p h n", n=P),
                                      ps[:, i0 + 2 * a:i0 + 2 * a + 2, :].rearrange("p b (h n) -> p (b h) n", n=P),
                                      rstd[:, a * H:(a + 1) * H].unsqueeze(2).to_broadcast([P, H, P]),
                                      ALU.mult).then_inc(kqn_ready, 1)

            head_norm(0, kn, POW_K)
            head_norm(4, qn, POW_Q)
            dve.wait_ge(biasload, 16)
            for h in range(H + 1):
                if h < H:
                    bank = 4 + h % 4
                    dve.wait_ge(sc_done, h + 1)
                    dve.tensor_tensor(prob[:, h, 0:P], ps[:, bank, 0:P], bias[:, h, P:T], ALU.add)
                    link(dve.tensor_tensor(prob[:, h, P:NR], ps[:, bank, P:NR], bias[:, h, :], ALU.add))
                    dve.tensor_reduce(nmax[:, h, 0:1], prob[:, h, 0:P], AX.X, ALU.max, negate=True)
                    dve.tensor_reduce(nmax[:, h, 1:2], prob[:, h, P:NR], AX.X, ALU.max, negate=True)\
                       .then_inc(mx_ready, 1)
                if h >= 1:
                    dve.wait_ge(ex_done, h)
                    link(dve.reciprocal(einv[:, h - 1, :], esum[:, h - 1, :]))
                    dve.tensor_scalar(prob[:, h - 1, 0:P], prob[:, h - 1, 0:P], einv[:, h - 1, 0:1], None, ALU.mult)
                    dve.tensor_scalar(prob[:, h - 1, P:NR], prob[:, h - 1, P:NR], einv[:, h - 1, 1:2], None,
                                      ALU.mult).then_inc(pn_ready, 1)
            projected_and_normed(1, POW_FFN1)
            moe(1)
            for a in range(TT):
                dve.memset(mark[:, a:a + 1], 0.0).then_inc(x_ready, 1)

        @block.tensor
        def _(pe):
            def mm(o, l, r, start=True, stop=True):
                return pe.matmul(o, l, r, start=start, stop=stop)

            def tr(o, i):
                return pe.transpose(o, i, ident[:])

            def arrived(c, it=0):
                pe.wait_ge(loaded[c % RING], it * (16 * TURNS) + 16 * (c // RING + 1))

            def transposes(n, a, bank, src):
                for k in range(KD):
                    i = tr(ps[:, bank + k // 4, (k % 4) * P:(k % 4 + 1) * P], src[:, a, k * P:(k + 1) * P])
                    if k % 4 == 3:
                        i.then_inc(nt_done, 1)

            def hT_ready(n):
                pe.wait_ge(hT_dve, n)
                pe.wait_ge(hT_act, n)

            def project(c, lhs, bank, a, signal):
                arrived(c)
                for k in range(KD):
                    i = mm(ps[:, bank, :], lhs[:, k, a * P:(a + 1) * P], up_view(c)[:, k, :], k == 0, k == KD - 1)
                i.then_inc(signal, 1)

            pe.wait_ge(c_in, 16)
            for a in range(TT):
                pe.wait_ge(xn_ready, a + 1)
                transposes(a, a, 4 + 2 * a, xn)
            hT_ready(2)
            for j, (signal, bank0) in enumerate(((f_done, 0), (q_done, 4))):
                for hp in range(4):
                    c = MIX0 + 2 * j + hp // 2
                    if j == 0 and hp == 0:
                        pe.wait_ge(part_in, 16)
                    else:
                        arrived(c)
                    if j == 1 and hp == 3:
                        pe.wait_ge(rb_ready, 1)
                    for h in (2 * hp, 2 * hp + 1):
                        for k in range(KD):
                            i = mm(ps[:, bank0 + hp, (h % 2) * T:(h % 2 + 1) * T],
                                   up_view(c)[:, k, (h % 4) * P:(h % 4 + 1) * P], hT[:, k, :], k == 0, k == KD - 1)
                    i.then_inc(signal, 1)
                if j == 0:
                    pe.wait_ge(rb_in, 16 * 3)
                    mm(ps[0:H, 7, 0:NR], rbw, bucket).then_inc(rb_done, 1)

            q3 = qp_all.rearrange("p (h t) -> p h t", t=T)
            k3 = ks_all.rearrange("p (h t) -> p h t", t=T)
            pe.wait_ge(k_ready, 4)
            pe.wait_ge(q_ready, 4)
            for l in range(LEVELS + 1):
                if l:
                    pe.wait_ge(upd_ready, l)
                    pe.wait_ge(pred_done, l)
                for h in range(H):
                    for a in range(TT):
                        b = 2 * h + a
                        i = mm(ps[:, b // 4, (b % 4) * P:(b % 4 + 1) * P], k3[:, h, a * P:(a + 1) * P],
                               q3[:, h, a * P:(a + 1) * P])
                i.then_inc(lev_done, 1)
                if l >= 4:
                    pe.wait_ge(gate_ready, l - 3)
                project(MIX0 + 4 + l // 2, hT, 4 + l % 4, l % 2, vg_done)
            pe.wait_ge(upd_ready, LEVELS + 1)
            pe.wait_ge(pred_done, LEVELS + 1)
            pe.wait_ge(v_ready, 4)
            for a in range(TT):
                if a:
                    for h in range(H):
                        i = mm(ps[:, h // 4, (h % 4) * P:(h % 4 + 1) * P], k3[:, h, 0:P], q3[:, h, P:T])
                    i.then_inc(lev_done, 1)
                    pe.wait_ge(cross_ready, 1)
                for h in range(H):
                    o = ps[:, 4 + 2 * a + h // 4, (h % 4) * P:(h % 4 + 1) * P]
                    if a:
                        mm(o, scross[:, h, :], v_all[:, 0, h * P:(h + 1) * P], True, False)
                    i = mm(o, sdiag[:, 2 * h + a, :], v_all[:, a, h * P:(h + 1) * P], a == 0, True)
                    if h % 4 == 3:
                        i.then_inc(o_done, 1)
            def out_and_router(layer, n, c, lhs):
                for i in range(4):
                    a, half = i // 2, i % 2
                    if layer == 0 and half == 0:
                        if a:
                            pe.wait_ge(oT_ready, 2)
                        for k in range(KD):
                            if k % 4 == 0:
                                pe.wait_ge(og_ready, 2 * a + k // 4 + 1)
                            j = tr(ps[:, 2 * a + k // 4, (k % 4) * P:(k % 4 + 1) * P], og[:, a, k * P:(k + 1) * P])
                            if k % 4 == 3:
                                j.then_inc(ot_done, 1)
                        pe.wait_ge(oT_ready, 2 * a + 2)
                    project(c + half, lhs, 4 + i, a, pr_done)
                    if i == 2:
                        pe.wait_ge(x_added, 4 * layer + 2)
                        transposes(n, 0, 0, xs)
                router(layer, 0)
                pe.wait_ge(x_added, 4 * layer + 4)
                transposes(n + 1, 1, 2, xs)
                router(layer, 1)

            def router(layer, a):
                for k in range(KD):
                    if k == 0:
                        pe.wait_ge(hT_dve, (3, 9)[layer] + a)
                    if k == KD // 2:
                        pe.wait_ge(hT_act, (3, 9)[layer] + a)
                    i = mm(ps[:, 4, a * (NG + E):(a + 1) * (NG + E)], hrT[:, k, a * P:(a + 1) * P],
                           wr[:, layer, k, :], k == 0, k == KD - 1)
                if a == TT - 1:
                    i.then_inc(rt_done, 1)

            out_and_router(0, 2, MIX0 + 8, oT)

            def gather(q, bank, half, signal):
                for k in range(4):
                    for a in range(TT):
                        i = mm(ps[:, bank, k * P:(k + 1) * P], hn[:, a, (4 * half + k) * P:(4 * half + k + 1) * P],
                               pick[:, a].rearrange("p e s -> p (e s)"), a == 0, a == TT - 1)
                if signal is not None:
                    i.then_inc(signal, 1)
                return i

            def up(weights, bank, buf, signal, ks=range(KD)):
                for k in ks:
                    for x2 in range(2):
                        rows = slice(x2 * BLK, (x2 + 1) * BLK)
                        i = mm(ps[rows, bank, :], xgT[:, buf, k, rows], weights[x2][:, k, :], k == 0, k == KD - 1)
                if signal is not None:
                    i.then_inc(signal, 1)

            def hidden_T(bank, signal):
                for k in range(KF):
                    i = tr(ps[:, bank, k * P:(k + 1) * P], hid[:, k * P:(k + 1) * P])
                i.then_inc(signal, 1)

            def down(c, half, signal):
                for k in range(KF):
                    for x2 in range(2):
                        rows = slice(x2 * BLK, (x2 + 1) * BLK)
                        i = mm(ps[rows, 6 + half, :], hidT[:, k, rows],
                               down_view(c + x2)[:, k, half * 512:(half + 1) * 512], k == 0, k == KF - 1)
                if signal is not None:
                    i.then_inc(signal, 1)

            def spread_T(bank, signal):
                for a in range(TT):
                    i = tr(ps[:, bank, a * P:(a + 1) * P], pickw[:, a].rearrange("p e s -> p (e s)"))
                if signal is not None:
                    i.then_inc(signal, 1)

            def over(layer):
                s = ov[layer]
                pe.wait_ge(nblk_ready, layer + 1)
                n = pe.value_load(nblk[0:1, layer:layer + 1], min_val=1, max_val=4)
                with pe.If(n > 1):
                    with pe.Fori(1, n) as b:
                        with pe.Fori(0, PAIRS) as q:
                            v = b * PAIRS + q - (PAIRS - 1)
                            pe.wait_ge(s["pick"], v)
                            gather(q, 4, 0, None)
                            gather(q, 5, 1, None)
                            spread_T(0, s["gat"])
                            pe.wait_ge(s["xg"], v)
                            pe.wait_ge(s["w"], v * (16 * 6))
                            up((up_view(0), up_view(1)), 6, 0, None)
                            up((up_view(2), up_view(3)), 7, 0, s["up"])
                            pe.wait_ge(s["hid"], v)
                            hidden_T(1, s["ht"])
                            pe.wait_ge(s["hidT"], v)
                            down(4, 0, None)
                            down(4, 1, s["y"])
                            pe.wait_ge(s["ye"], v)
                            for a in range(TT):
                                for half in range(2):
                                    i = mm(ps[:, 2 * a + half, :], spread[:, a * P:(a + 1) * P],
                                           y[:, half * 512:(half + 1) * 512])
                            i.then_inc(s["c"], 1)
                    pe.wait_ge(s["end"], 1)

            def moe(layer):
                pe.wait_ge(asg_ready, layer + 1)
                mm(ps[:, 5, 0:E], before[:], asg[:, 0, :])
                mm(ps[:, 5, E:2 * E], ones[:], asg[:, 0, :], True, False)
                mm(ps[:, 5, E:2 * E], before[:], asg[:, 1, :], False, True).then_inc(pos_done, 1)
                mm(ps[:, 6, 0:E], ones[:], asg[:, 0, :], True, False)
                mm(ps[:, 6, 0:E], ones[:], asg[:, 1, :], False, True).then_inc(count_done, 1)
                P0 = layer * PAIRS

                def gather_next(it, u, half):
                    q = P0 + u
                    if half == 0:
                        pe.wait_ge(pick_ready, it * UN + (q + 1))
                    if not (type(it) is int and it * UN + q < 1 and half == 0):
                        pe.wait_ge(xg_ready, it * (2 * UN) + (2 * q + half))
                    gather(None, 4, half, gat_done)

                pe.wait_ge(xn_ready, (4, 8)[layer])
                gather_next(0, 0, 0)
                gather(None, 7, 1, gat_done)

                def body(it):
                    for u in range(UN):
                        last = last_pair(it, u)
                        q = P0 + u
                        n0 = type(it) is int and it * UN + q < 1
                        first = is_int(it, 0) and u == 0
                        pe.wait_ge(xg_ready, it * (2 * UN) + (2 * q + (1 if first else 2)))
                        for half in range(2):
                            r = 6 * u + 2 * half
                            for x2 in range(2):
                                if last and half:
                                    pe.wait_ge(up_part_in, 16 * 2 * (layer + 1))
                                elif in_extra(r, it):
                                    pe.wait_ge(extra_in[x2], 16 * (layer + 1))
                                else:
                                    arrived(ring_chunk(layer, r + x2, it), it)
                            if not n0:
                                pe.wait_ge(y_ready, it * (2 * UN) + (2 * q - 1 + half))
                            w = (gate_or_up(layer, r, it), gate_or_up(layer, r + 1, it))
                            if first and half == 0:
                                pe.wait_ge(nblk_ready, layer + 1)
                                up(w, 6, 0, None, range(KD // 2))
                                pe.wait_ge(xg_ready, 2 * q + 2)
                                up(w, 6, 0, up_done, range(KD // 2, KD))
                            elif last and half:
                                up(w, 7, u % 2, None, range(KD // 2))
                                arrived(ring_chunk(layer, r, it), it)
                                arrived(ring_chunk(layer, r + 1, it), it)
                                up(w, 7, u % 2, up_done, range(KD // 2, KD))
                            else:
                                up(w, 6 + half, u % 2, up_done)
                        if not last:
                            gather_next(it, u + 1, 0)
                        pe.wait_ge(hid_ready, it * UN + (q + 1))
                        if not n0:
                            pe.wait_ge(s_ready, it * UN + q)
                        hidden_T(5, ht_done)
                        if not last:
                            gather_next(it, u + 1, 1)
                        pe.wait_ge(hidT_ready, it * UN + (q + 1))
                        c = ring_chunk(layer, 6 * u + 4, it)
                        if last:
                            pe.wait_ge(pickw_ready, it * UN + (q + 1))
                            spread_T(5, st_done)
                            pe.wait_ge(down_part_in, 16 * 2 * (layer + 1))
                            down(c, 0, down_done)
                            arrived(c, it)
                            arrived(c + 1, it)
                            down(c, 1, down_done)
                        else:
                            arrived(c, it)
                            arrived(c + 1, it)
                            down(c, 0, down_done)
                            down(c, 1, down_done)
                            pe.wait_ge(pickw_ready, it * UN + (q + 1))
                            spread_T(5, st_done)
                        pe.wait_ge(s_ready, it * UN + (q + 1))
                        for a in range(TT):
                            for half in range(2):
                                if a == 0:
                                    pe.wait_ge(y_ready, it * (2 * UN) + (2 * q + 1 + half))
                                i = mm(ps[:, 2 * a + half, :], spread[:, a * P:(a + 1) * P],
                                       y[:, half * 512:(half + 1) * 512], is_int(it, 0) and u == 0, last)
                            i.then_inc(c_done, 1)

                over_pairs(pe, body)
                over(layer)

            moe(0)

            for a in range(TT):
                pe.wait_ge(xn_ready, 4 + a + 1)
                transposes(4 + a, a, 4 + 2 * a, xs)
            for i in range(4):
                if i < TT:
                    hT_ready(5 + 2 * i)
                project(MIX1 + i // 2, hkvT, 2 * (i % 2) + i // 2, i % 2, kq_done)
            hT_ready(8)
            for i in range(4):
                project(MIX1 + 2 + i // 2, hqT, 4 + 2 * (i % 2) + i // 2, i % 2, kq_done)

            def heads_transposes(src, bank0, n0):
                for a in range(TT):
                    pe.wait_ge(kqn_ready, n0 + a + 1)
                    if a == 0:
                        pe.wait_ge(kqn_ready, n0 + 2)
                    for h in range(H):
                        i = tr(ps[:, bank0 + h // 2, (h % 2) * T + a * P:(h % 2) * T + (a + 1) * P],
                               src[:, a, h * P:(h + 1) * P])
                        if a and h % 2:
                            i.then_inc(tkq_done, 1)

            def att_v(i):
                pe.wait_ge(kqT_ready, i + 1)
                project(MIX1 + 4 + i // 2, hkvT, i, i % 2, av_done)

            def scores(h):
                if h >= 4:
                    pe.wait_ge(mx_ready, h - 3)
                bank = 4 + h % 4
                mm(ps[:, bank, 0:P], qT[:, h, 0:P], kT[:, h, 0:P])
                mm(ps[:, bank, P:NR], qT[:, h, P:T], kT[:, h, :]).then_inc(sc_done, 1)

            def probs_T(h):
                pe.wait_ge(pn_ready, h + 1)
                if h < 4:
                    pe.wait_ge(mx_ready, h + 5)
                else:
                    pe.wait_ge(pT_ready, h - 3)
                for j in range(3):
                    i = tr(ps[:, 4 + h % 4, j * P:(j + 1) * P], prob[:, h, j * P:(j + 1) * P])
                i.then_inc(pt_done, 1)

            def probs_v(b):
                pe.wait_ge(pT_ready, 2 * b + 2)
                for h in (2 * b, 2 * b + 1):
                    o = (h % 2) * T
                    mm(ps[:, b, o:o + T], v_all[:, 0, h * P:(h + 1) * P], probT[:, h, 0:T], True, False)
                    i = mm(ps[:, b, o + P:o + T], v_all[:, 1, h * P:(h + 1) * P], probT[:, h, T:NR], False, True)
                i.then_inc(pv_done, 1)

            heads_transposes(kn, 0, 0)
            att_v(0)
            heads_transposes(qn, 4, 2)
            att_v(1)
            pe.wait_ge(kqT_ready, 8)
            for h in range(4):
                scores(h)
            att_v(2)
            for h in range(4, H):
                scores(h)
            att_v(3)
            for h in range(4):
                probs_T(h)
            pe.wait_ge(av_ready, 4)
            for b in range(4):
                probs_v(b)
                if b < 2:
                    probs_T(4 + 2 * b)
                    probs_T(5 + 2 * b)
            pe.wait_ge(oT_ready, 8)
            out_and_router(1, 6, MIX1 + 6, oT)
            moe(1)


SMALL = 16 * 2
LATE = 16 * 18

_INS = ['x', 'mix_norm', 'ffn_norm', 'hg_w_in', 'hg_lb', 'hg_o_norm', 'hg_w_out', 'kv_norm', 'w_kv', 'k_norm',
        'att_w_q', 'q_norm', 'att_w_o', 'rel_bias', 'moe_w_group', 'moe_b_group', 'moe_w_expert', 'moe_b_expert',
        'moe_w_in', 'moe_w_out']


def constants():
    import math
    import numpy as np
    i = np.arange(P)
    masks = np.zeros((P, LEVELS + 1, P), np.float32)
    masks[i, 0, i] = 1
    for l in range(1, LEVELS + 1):
        m = 1 << (l - 1)
        masks[:, l, :] = ((i[:, None] // (2 * m) == i[None, :] // (2 * m)) & (i[:, None] // m % 2 == 0)
                          & (i[None, :] // m % 2 == 1))
    places = np.arange(BLK, dtype=np.float32)
    places[CAP:] = -1000.0
    dist = T - 1 - np.arange(NR)
    n = np.maximum(dist, 0)
    ratio = np.log(np.maximum(n, 16).astype(np.float32) / np.float32(16)) / np.float32(math.log(1024 / 16))
    buckets = np.where(n < 16, n, np.minimum(16 + (ratio * np.float32(16)).astype(np.int32), 31))
    return {
        "ident": np.eye(P, dtype=np.float32),
        "before": (i[:, None] < i[None, :]).astype(np.float32),
        "masks": masks,
        "slot": np.ascontiguousarray(np.broadcast_to(places, (P, BLK))),
        "prio": np.ascontiguousarray(np.broadcast_to(np.arange(EG, 0, -1, dtype=np.float32), (P, EG))),
        "bucket": (buckets[None, :] == np.arange(32)[:, None]).astype(np.float32),
        "future": np.ascontiguousarray(np.broadcast_to(np.where(dist < 0, -1e30, 0.0).astype(np.float32), (H, NR))),
    }


def kernel(**inputs):
    import numpy as _np
    import concourse.bacc as _bacc
    from concourse.bass_utils import run_bass_kernel_spmd as _run

    nc = _bacc.Bacc("TRN2", target_bir_lowering=False, num_devices=1)
    arrays, args = {}, []

    def give(name, a):
        arrays[name] = a
        args.append(nc.dram_tensor(name, a.shape, mybir.dt.from_np(a.dtype), kind="ExternalInput").ap())

    for name in _INS:
        give(f"in_{name}", _np.ascontiguousarray(inputs[name]))
    for name, a in constants().items():
        give(f"const_{name}", a)
    args.append(nc.dram_tensor("out_0", (1, T, D), FP32, kind="ExternalOutput").ap())
    build(nc, *args)
    r = _run(nc, [arrays], core_ids=[0])
    return r.results[0]["out_0"]
```
